# Optimizing a Trainium2 kernel written in Bass

```python
import math
import jax
import jax.numpy as jnp
from jax import lax
import numpy as np

D_MODEL = 2048
BATCH = 1
SEQ = 512
DEPTH = 2
DEC_BATCH = 8
DEC_SEQ = 1
PAST_LEN = 512
PAGE_SIZE = 128

N_A = DEPTH // 2
N_B = DEPTH - N_A
D_POOL = D_MODEL
POOL_WINDOWS = (2, 4, 8, 16)
N_POOL_GROUPS = len(POOL_WINDOWS)
POOL_GROUP = D_POOL // N_POOL_GROUPS
POOL_BUF = max(POOL_WINDOWS) - 1
HEAD_DIM = 128
N_HEADS = D_MODEL // HEAD_DIM
N_KV = 4
GROUP_REP = N_HEADS // N_KV
D_ATT = N_HEADS * HEAD_DIM
D_KV = N_KV * HEAD_DIM
N_BRANCH = 3
CMP_LEN = 32
CMP_STRIDE = 16
SLC_BLOCK = 64
N_SEL = 8
WINDOW = 512
N_BUCKETS = 32
MAX_DISTANCE = 128
Q_BLOCK = 32
RMS_EPS = 1e-6
SCALE = HEAD_DIM ** -0.5
NEG_INF = -1e30
FORCE_SCORE = 1e9

kernel_name = 'yoco_pool_nsa_decode_step'

def rms_norm(x, g):
    xf = x.astype(jnp.float32)
    y = xf * lax.rsqrt(jnp.mean(xf * xf, axis=-1, keepdims=True) + RMS_EPS)
    return (y * g.astype(jnp.float32)).astype(x.dtype)

def ada_modulate(c, w_ada, b_ada):
    mod = jax.nn.silu(c) @ w_ada + b_ada
    shift, scale, gate = jnp.split(mod, 3, axis=-1)
    return shift[:, None], scale[:, None], gate[:, None]

def rel_bucket(dist):
    max_exact = N_BUCKETS // 2
    d = jnp.maximum(dist, 0)
    df = jnp.maximum(d, max_exact).astype(jnp.float32)
    large = max_exact + (jnp.log(df / max_exact) / math.log(MAX_DISTANCE / max_exact) * (N_BUCKETS - max_exact)).astype(jnp.int32)
    return jnp.where(d < max_exact, d, jnp.minimum(large, N_BUCKETS - 1))

def pool_mixer(h, prefix, qpos, w_in, w_grp, pool_scale, w_out):
    B, T = h.shape[:2]
    u, z = jnp.split(h @ w_in, 2, axis=-1)
    u_ext = jnp.concatenate([prefix.astype(u.dtype), u], axis=1)
    uf = u_ext.astype(jnp.float32)
    csum = jnp.concatenate([jnp.zeros_like(uf[:, :1]), jnp.cumsum(uf, axis=1)], axis=1)
    hi = csum[:, POOL_BUF + 1:]
    u32 = uf[:, POOL_BUF:]
    outs = []
    for gi, w in enumerate(POOL_WINDOWS):
        sl = slice(gi * POOL_GROUP, (gi + 1) * POOL_GROUP)
        lo = csum[:, POOL_BUF + 1 - w:POOL_BUF + 1 - w + T, sl]
        cnt = jnp.minimum(qpos + 1, w).astype(jnp.float32)[None, :, None]
        outs.append((hi[..., sl] - lo) / cnt - u32[..., sl])
    pooled = jnp.stack(outs, axis=2).astype(h.dtype)
    mixed = jnp.einsum('btgc,gcd->btgd', pooled, w_grp).reshape(B, T, D_POOL)
    y = mixed * pool_scale * jax.nn.silu(z)
    return y @ w_out, u_ext[:, -POOL_BUF:]

def shared_kv(x, g_kv, w_kv):
    B, T = x.shape[:2]
    kv = (rms_norm(x, g_kv) @ w_kv).reshape(B, T, 2 * N_BRANCH, N_KV, HEAD_DIM)
    return [kv[:, :, i] for i in range(2 * N_BRANCH)]

def gather_pages(cache, page_table):
    rows = cache[page_table]
    return rows.reshape(page_table.shape[0], page_table.shape[1] * PAGE_SIZE, N_KV, HEAD_DIM)

def compress(rows, pe, w1, w2):
    B, T = rows.shape[:2]
    n_sub = -(-T // CMP_STRIDE)
    rows = jnp.pad(rows, ((0, 0), (0, n_sub * CMP_STRIDE - T), (0, 0), (0, 0)))
    sub = rows.reshape(B, n_sub, CMP_STRIDE, N_KV, HEAD_DIM)
    blocks = jnp.concatenate([sub[:, :-1], sub[:, 1:]], axis=2) + pe[None, None, :, None, :]
    flat = blocks.transpose(0, 1, 3, 2, 4).reshape(B, n_sub - 1, N_KV, CMP_LEN * HEAD_DIM)
    return jax.nn.silu(flat @ w1) @ w2

def to_blocks(rows):
    B, T = rows.shape[:2]
    n = -(-T // SLC_BLOCK)
    rows = jnp.pad(rows, ((0, 0), (0, n * SLC_BLOCK - T), (0, 0), (0, 0)))
    return rows.reshape(B, n, SLC_BLOCK, N_KV, HEAD_DIM).transpose(0, 3, 1, 2, 4)

def compressed_branch(qg, qpos, kc, vc, rel_bias):
    Tq, n_cmp = qg.shape[1], kc.shape[1]
    end = jnp.arange(n_cmp, dtype=jnp.int32) * CMP_STRIDE + CMP_LEN - 1
    dist = qpos[:, None] - end[None, :]
    vis = dist >= 0
    bias = rel_bias[rel_bucket(dist)].transpose(2, 0, 1).reshape(N_KV, GROUP_REP, Tq, n_cmp)
    s = jnp.einsum('bqgrd,bngd->bgrqn', qg, kc).astype(jnp.float32) * SCALE + bias
    p = jax.nn.softmax(jnp.where(vis, s, NEG_INF), axis=-1)
    p = jnp.where(jnp.any(vis, axis=-1)[:, None], p, 0.0)
    o = jnp.einsum('bgrqn,bngd->bqgrd', p.astype(vc.dtype), vc)
    return o, p

def selection_indices(p_cmp, qpos, n_slc):
    n_cmp = p_cmp.shape[-1]
    cs = jnp.arange(n_cmp, dtype=jnp.int32) * CMP_STRIDE
    bs = jnp.arange(n_slc, dtype=jnp.int32) * SLC_BLOCK
    overlap = jnp.clip(jnp.minimum(cs[:, None] + CMP_LEN, bs[None, :] + SLC_BLOCK) - jnp.maximum(cs[:, None], bs[None, :]), 0, None).astype(jnp.float32) / CMP_LEN
    imp = jnp.einsum('bgrqn,nj->bgqj', p_cmp, overlap)
    j = jnp.arange(n_slc, dtype=jnp.int32)
    cur = qpos // SLC_BLOCK
    forced = (j[None, :] == cur[:, None]) | (j[None, :] == 0)
    valid = j[None, :] <= cur[:, None]
    imp = jnp.where(forced, FORCE_SCORE, jnp.where(valid, imp, -FORCE_SCORE))
    _, idx = lax.top_k(imp, min(N_SEL, n_slc))
    return idx

def selected_branch(qg, qpos, idx, kb, vb, rel_bias):
    B, Tq = qg.shape[:2]
    gather = jax.vmap(jax.vmap(lambda blk, ix: blk[ix]))
    ks = gather(kb, idx)
    vs = gather(vb, idx)
    n_sel = idx.shape[-1]
    kpos = idx[..., None] * SLC_BLOCK + jnp.arange(SLC_BLOCK, dtype=jnp.int32)
    dist = qpos[None, None, :, None, None] - kpos
    tbl = rel_bias.T.reshape(N_KV, GROUP_REP, N_BUCKETS)
    g_ix = jnp.arange(N_KV)[None, :, None, None, None, None]
    r_ix = jnp.arange(GROUP_REP)[None, None, :, None, None, None]
    bias = tbl[g_ix, r_ix, rel_bucket(dist)[:, :, None]]
    s = jnp.einsum('bqgrd,bgqnsd->bgrqns', qg, ks).astype(jnp.float32) * SCALE + bias
    s = jnp.where((dist >= 0)[:, :, None], s, NEG_INF).reshape(B, N_KV, GROUP_REP, Tq, n_sel * SLC_BLOCK)
    p = jax.nn.softmax(s, axis=-1).reshape(B, N_KV, GROUP_REP, Tq, n_sel, SLC_BLOCK)
    return jnp.einsum('bgrqns,bgqnsd->bqgrd', p.astype(vs.dtype), vs)

def window_branch(qg, qpos, kw, vw, kpos, rel_bias):
    Tq, Tk = qg.shape[1], kw.shape[1]
    dist = qpos[:, None] - kpos[None, :]
    vis = (dist >= 0) & (dist < WINDOW) & (kpos[None, :] >= 0)
    bias = rel_bias[rel_bucket(dist)].transpose(2, 0, 1).reshape(N_KV, GROUP_REP, Tq, Tk)
    s = jnp.einsum('bqgrd,bkgd->bgrqk', qg, kw).astype(jnp.float32) * SCALE + bias
    p = jax.nn.softmax(jnp.where(vis, s, NEG_INF), axis=-1)
    return jnp.einsum('bgrqk,bkgd->bqgrd', p.astype(vw.dtype), vw)

def prompt_sparse_branches(qg, idx, kb, vb, kw, vw, rel_bias):
    B, T = qg.shape[:2]
    kw_pad = jnp.pad(kw, ((0, 0), (WINDOW, 0), (0, 0), (0, 0)))
    vw_pad = jnp.pad(vw, ((0, 0), (WINDOW, 0), (0, 0), (0, 0)))

    def one_block(jb):
        start = jb * Q_BLOCK
        qpos = start + jnp.arange(Q_BLOCK, dtype=jnp.int32)
        q_j = lax.dynamic_slice_in_dim(qg, start, Q_BLOCK, axis=1)
        idx_j = lax.dynamic_slice_in_dim(idx, start, Q_BLOCK, axis=2)
        o_slc = selected_branch(q_j, qpos, idx_j, kb, vb, rel_bias)
        kw_j = lax.dynamic_slice_in_dim(kw_pad, start, WINDOW + Q_BLOCK, axis=1)
        vw_j = lax.dynamic_slice_in_dim(vw_pad, start, WINDOW + Q_BLOCK, axis=1)
        kpos = start - WINDOW + jnp.arange(WINDOW + Q_BLOCK, dtype=jnp.int32)
        o_win = window_branch(q_j, qpos, kw_j, vw_j, kpos, rel_bias)
        return o_slc, o_win

    o_slc, o_win = lax.map(one_block, jnp.arange(T // Q_BLOCK, dtype=jnp.int32))
    o_slc = jnp.moveaxis(o_slc, 0, 1).reshape(B, T, N_KV, GROUP_REP, HEAD_DIM)
    o_win = jnp.moveaxis(o_win, 0, 1).reshape(B, T, N_KV, GROUP_REP, HEAD_DIM)
    return o_slc, o_win

def nsa_mixer(h, qpos, ctx, w_in, w_out, rel_bias, prompt_mode):
    B, T = h.shape[:2]
    proj = h @ w_in
    q = proj[..., :D_ATT].reshape(B, T, N_KV, GROUP_REP, HEAD_DIM)
    z = proj[..., D_ATT:(1 + N_BRANCH) * D_ATT].reshape(B, T, N_BRANCH, N_HEADS, HEAD_DIM)
    gates = jax.nn.sigmoid(proj[..., (1 + N_BRANCH) * D_ATT:].reshape(B, T, N_BRANCH, N_HEADS))
    o_cmp, p_cmp = compressed_branch(q, qpos, ctx['kc'], ctx['vc'], rel_bias)
    idx = selection_indices(p_cmp, qpos, ctx['kb'].shape[2])
    if prompt_mode:
        o_slc, o_win = prompt_sparse_branches(q, idx, ctx['kb'], ctx['vb'], ctx['kw'], ctx['vw'], rel_bias)
    else:
        o_slc = selected_branch(q, qpos, idx, ctx['kb'], ctx['vb'], rel_bias)
        o_win = window_branch(q, qpos, ctx['kw'], ctx['vw'], ctx['kw_pos'], rel_bias)
    o = jnp.stack([o_cmp, o_slc, o_win], axis=2).reshape(B, T, N_BRANCH, N_HEADS, HEAD_DIM)
    y = jnp.sum(gates[..., None] * o * jax.nn.silu(z), axis=2).reshape(B, T, D_ATT)
    return y @ w_out

def run_trunk(x, c, qpos, pool_prefix, build_ctx, prompt_mode, g_norm, w_ada, b_ada, w_in_a, w_grp, pool_scale, w_out_a, w_in_b, w_out_b, rel_bias, g_final):
    new_pool = []
    for l in range(DEPTH):
        shift, scale, gate = ada_modulate(c, w_ada[l], b_ada[l])
        if l == N_A:
            ctx, kv_state = build_ctx(x)
        h = rms_norm(x, g_norm[l]) * (1 + scale) + shift
        if l < N_A:
            y, pref = pool_mixer(h, pool_prefix[l], qpos, w_in_a[l], w_grp[l], pool_scale[l], w_out_a[l])
            new_pool.append(pref)
        else:
            y = nsa_mixer(h, qpos, ctx, w_in_b[l - N_A], w_out_b[l - N_A], rel_bias, prompt_mode)
        x = x + gate * y
    return rms_norm(x, g_final), jnp.stack(new_pool), kv_state

def setup_inputs(seed: int = 0) -> dict:
    key = jax.random.key(seed)
    ks = jax.random.split(key, 32)
    n_pages = PAST_LEN // PAGE_SIZE
    n_phys = (DEC_BATCH * n_pages * 5) // 4
    win_buf = min(WINDOW, PAST_LEN)

    def nrm(k, shape, scale=1.0):
        return jax.random.normal(k, shape, jnp.float32) * scale

    perm = jax.random.permutation(ks[0], n_phys)
    page_table = perm[:DEC_BATCH * n_pages].reshape(DEC_BATCH, n_pages).astype(jnp.int32)
    cache_shape = (n_phys, PAGE_SIZE, N_KV, HEAD_DIM)
    win_shape = (DEC_BATCH, win_buf, N_KV, HEAD_DIM)
    return {
        'x_prompt': nrm(ks[1], (BATCH, SEQ, D_MODEL)),
        'x_sample': nrm(ks[2], (DEC_BATCH, DEC_SEQ, D_MODEL)),
        'state_pool': nrm(ks[3], (N_A, DEC_BATCH, POOL_BUF, D_POOL)),
        'cache_k_cmp': nrm(ks[4], cache_shape),
        'cache_v_cmp': nrm(ks[5], cache_shape),
        'cache_k_slc': nrm(ks[6], cache_shape),
        'cache_v_slc': nrm(ks[7], cache_shape),
        'state_k_win': nrm(ks[8], win_shape),
        'state_v_win': nrm(ks[9], win_shape),
        'page_table': page_table,
        'c_prompt': nrm(ks[10], (BATCH, D_MODEL)),
        'c_sample': nrm(ks[11], (DEC_BATCH, D_MODEL)),
        'g_norm': 1.0 + nrm(ks[12], (DEPTH, D_MODEL), 0.02),
        'w_ada': nrm(ks[13], (DEPTH, D_MODEL, 3 * D_MODEL), 0.5 * D_MODEL ** -0.5),
        'b_ada': nrm(ks[14], (DEPTH, 3 * D_MODEL), 0.01),
        'w_in_a': nrm(ks[15], (N_A, D_MODEL, 2 * D_POOL), D_MODEL ** -0.5),
        'w_grp': nrm(ks[16], (N_A, N_POOL_GROUPS, POOL_GROUP, POOL_GROUP), POOL_GROUP ** -0.5),
        'pool_scale': 1.0 + nrm(ks[17], (N_A, D_POOL), 0.02),
        'w_out_a': nrm(ks[18], (N_A, D_POOL, D_MODEL), D_POOL ** -0.5),
        'g_kv': 1.0 + nrm(ks[19], (D_MODEL,), 0.02),
        'w_kv': nrm(ks[20], (D_MODEL, 2 * N_BRANCH * D_KV), D_MODEL ** -0.5),
        'pe_k': nrm(ks[21], (CMP_LEN, HEAD_DIM), 0.1),
        'w_ck1': nrm(ks[22], (CMP_LEN * HEAD_DIM, HEAD_DIM), (CMP_LEN * HEAD_DIM) ** -0.5),
        'w_ck2': nrm(ks[23], (HEAD_DIM, HEAD_DIM), 1.5 * HEAD_DIM ** -0.5),
        'pe_v': nrm(ks[24], (CMP_LEN, HEAD_DIM), 0.1),
        'w_cv1': nrm(ks[25], (CMP_LEN * HEAD_DIM, HEAD_DIM), (CMP_LEN * HEAD_DIM) ** -0.5),
        'w_cv2': nrm(ks[26], (HEAD_DIM, HEAD_DIM), 1.5 * HEAD_DIM ** -0.5),
        'rel_bias': nrm(ks[27], (N_BUCKETS, N_HEADS), 0.5),
        'w_in_b': nrm(ks[28], (N_B, D_MODEL, (1 + N_BRANCH) * D_ATT + N_BRANCH * N_HEADS), D_MODEL ** -0.5),
        'w_out_b': nrm(ks[29], (N_B, D_ATT, D_MODEL), D_ATT ** -0.5),
        'g_final': 1.0 + nrm(ks[30], (D_MODEL,), 0.02),
    }

def reference(x_prompt, x_sample, state_pool, cache_k_cmp, cache_v_cmp, cache_k_slc, cache_v_slc, state_k_win, state_v_win, page_table, c_prompt, c_sample, g_norm, w_ada, b_ada, w_in_a, w_grp, pool_scale, w_out_a, g_kv, w_kv, pe_k, w_ck1, w_ck2, pe_v, w_cv1, w_cv2, rel_bias, w_in_b, w_out_b, g_final):
    def prompt_ctx(xs):
        k_cmp, v_cmp, k_slc, v_slc, k_win, v_win = shared_kv(xs, g_kv, w_kv)
        ctx = {'kc': compress(k_cmp, pe_k, w_ck1, w_ck2), 'vc': compress(v_cmp, pe_v, w_cv1, w_cv2),
               'kb': to_blocks(k_slc), 'vb': to_blocks(v_slc), 'kw': k_win, 'vw': v_win}
        wb = min(WINDOW, xs.shape[1])
        return ctx, (k_cmp, v_cmp, k_slc, v_slc, k_win[:, -wb:], v_win[:, -wb:])

    def sample_ctx(xs):
        k_cmp, v_cmp, k_slc, v_slc, k_win, v_win = shared_kv(xs, g_kv, w_kv)
        k_cmp_all = jnp.concatenate([gather_pages(cache_k_cmp, page_table), k_cmp], axis=1)
        v_cmp_all = jnp.concatenate([gather_pages(cache_v_cmp, page_table), v_cmp], axis=1)
        k_slc_all = jnp.concatenate([gather_pages(cache_k_slc, page_table), k_slc], axis=1)
        v_slc_all = jnp.concatenate([gather_pages(cache_v_slc, page_table), v_slc], axis=1)
        kw = jnp.concatenate([state_k_win, k_win], axis=1)
        vw = jnp.concatenate([state_v_win, v_win], axis=1)
        wb = state_k_win.shape[1]
        kw_pos = PAST_LEN - wb + jnp.arange(wb + xs.shape[1], dtype=jnp.int32)
        ctx = {'kc': compress(k_cmp_all, pe_k, w_ck1, w_ck2), 'vc': compress(v_cmp_all, pe_v, w_cv1, w_cv2),
               'kb': to_blocks(k_slc_all), 'vb': to_blocks(v_slc_all), 'kw': kw, 'vw': vw, 'kw_pos': kw_pos}
        return ctx, (k_cmp, v_cmp, k_slc, v_slc, kw[:, -wb:], vw[:, -wb:])

    qpos_p = jnp.arange(x_prompt.shape[1], dtype=jnp.int32)
    pool_zero = jnp.zeros((N_A, x_prompt.shape[0], POOL_BUF, D_POOL), x_prompt.dtype)
    y_prompt, pool_p, kv_p = run_trunk(x_prompt, c_prompt, qpos_p, pool_zero, prompt_ctx, True, g_norm, w_ada, b_ada, w_in_a, w_grp, pool_scale, w_out_a, w_in_b, w_out_b, rel_bias, g_final)
    k_cmp_p, v_cmp_p, k_slc_p, v_slc_p, k_win_p, v_win_p = kv_p

    qpos_s = PAST_LEN + jnp.arange(x_sample.shape[1], dtype=jnp.int32)
    y_sample, pool_s, kv_s = run_trunk(x_sample, c_sample, qpos_s, state_pool, sample_ctx, False, g_norm, w_ada, b_ada, w_in_a, w_grp, pool_scale, w_out_a, w_in_b, w_out_b, rel_bias, g_final)
    k_cmp_s, v_cmp_s, k_slc_s, v_slc_s, k_win_s, v_win_s = kv_s

    return (y_prompt, y_sample, pool_p, k_cmp_p, v_cmp_p, k_slc_p, v_slc_p, k_win_p, v_win_p, pool_s, k_cmp_s, v_cmp_s, k_slc_s, v_slc_s, k_win_s, v_win_s)


_drawn_inputs = setup_inputs


def setup_inputs(seed=0):
    import zlib

    import numpy as np

    out = dict(_drawn_inputs(seed))
    spreads = {}
    factors = {'cache_k_cmp': 3.142,
     'cache_k_slc': 7.247,
     'cache_v_slc': 6.216,
     'g_norm': 3.032,
     'b_ada': 4.344,
     'pool_scale': 8.0,
     'g_kv': 8.217,
     'pe_k': 8.0,
     'pe_v': 20.099,
     'rel_bias': 3.707,
     'g_final': 7.602}
    for name, (base, spread) in spreads.items():
        noise = np.random.default_rng([zlib.crc32(name.encode()), seed]).standard_normal(out[name].shape)
        drawn = base * np.exp(spread * noise) if base else spread * noise
        out[name] = jnp.asarray(drawn.astype(out[name].dtype))
    for name, factor in factors.items():
        out[name] = (out[name] * factor).astype(out[name].dtype)
    return out
```

```python
from contextlib import ExitStack

import numpy as np
import concourse.bass as bass
from concourse import mybir

F32 = mybir.dt.float32
F32R = mybir.dt.float32r
I32 = mybir.dt.int32
ALU = mybir.AluOpType
ACT = mybir.ActivationFunctionType
AX = mybir.AxisListType

P = 128
DM = 2048
KT = DM // P
TP, TS = 512, 8
T = TP + TS
HT = T // 2
NT = TP // P
ML = 48
NC = 9
NH, NKV, REP, HD = 16, 4, 4, 128
NBR = 3
PB = 15
WINDOWS = (2, 4, 8, 16)
NCMP = 31
CL, CS_ = 32, 16
NPG = 4
GLEN = 1025
SCALE = float(HD) ** -0.5
EPS = 1e-6
NEG = -1e30

C_ID, C_ONE, C_RSUM, C_CNT, C_SELP, C_SEL19, C_OVL, C_IOTA, C_VIS, C_EPS, C_MSK = 0, 128, 256, 384, 448, 480, 489, 498, 505, 506, 507
NCONST = 507 + 64


def shape_constants():
    c = np.zeros((P, NCONST), np.float32)
    c[:, C_ID:C_ID + P] = np.eye(P)
    c[:, C_ONE:C_ONE + P] = 1.0
    row = np.arange(P)
    same = (row[:, None] // 4) == (row[None, :] // 4)
    c[:, C_RSUM:C_RSUM + P] = same
    for g, w in enumerate(WINDOWS):
        c[:, C_CNT + 16 * g:C_CNT + 16 * g + 16] = 1.0 / np.minimum(np.arange(16) + 1, w)
        for b in range(TS):
            for t in range(PB):
                c[b * PB + t, C_SELP + 8 * g + b] = float(t >= PB + 1 - w)
    for j in range(NC):
        c[j, C_SEL19 + j] = c[NC + j, C_SEL19 + j] = 1.0
    c[2 * NC, C_SEL19:C_SEL19 + NC] = 1.0
    for g in range(NKV):
        for n in range(NCMP):
            for j in range(9):
                o = min(16 * n + 32, 64 * j + 64) - max(16 * n, 64 * j)
                c[g * NCMP + n, C_OVL + j] = max(o, 0) / CL
    c[:, C_IOTA:C_IOTA + 7] = np.arange(1, 8)
    c[:, C_VIS] = row >= CL - 1
    c[:, C_EPS] = EPS
    c[:, C_MSK:C_MSK + 64] = np.eye(8).reshape(1, 64)
    return c


def bucket_onehots():
    d = np.arange(512, -513, -1)
    df = np.maximum(d, 16).astype(np.float32)
    large = 16 + (np.log(df / np.float32(16)) / np.float32(np.log(128 / 16)) * np.float32(16)).astype(np.int32)
    bucket = np.where(d < 16, np.maximum(d, 0), np.minimum(large, 31))
    bucket = np.where(d < 0, 32, bucket)
    fall = (np.arange(33)[:, None] == bucket[None, :]).astype(np.float32)
    return np.concatenate([fall, fall[:, ::-1]], axis=1)


def wait(eng, sem, value):
    if not (isinstance(value, int) and value <= 0):
        eng.wait_ge(sem, value)


class Own:

    def __init__(self, eng, sem):
        self.eng, self.sem, self.base, self.n = eng, sem, 0, 0

    def __call__(self, ins):
        self.n += 1
        ins.then_inc(self.sem, 1)
        self.eng.wait_ge(self.sem, self.base + self.n)

    def turn(self, i, body):
        if isinstance(i, int):
            self.start = self.base + self.n
            self.base, self.n = self.start, 0
            body(i)
            self.per = self.n
            self.base, self.n = self.start + self.per, 0
        else:
            self.base, self.n = self.start + i * self.per, 0
            body(i)
            assert self.n == self.per

    def ended(self, turns):
        self.base, self.n = self.start + turns * self.per, 0


def looped(eng, own, turns, body):
    own.turn(0, body)
    if turns > 1:
        with eng.Fori(1, turns) as i:
            own.turn(i, body)
    own.ended(turns)


Q_ADA, Q_U, Q_MIX, Q_Z, Q_OA, Q_KV, Q_G, Q_H, Q_OB = 0, 48, 56, 58, 66, 74, 86, 87, 119
D_U, D_MIX, D_OA, D_KV, D_G, D_H, D_OB = 0, 8, 16, 24, 36, 37, 69


def build(nc, ins, outs):
    A = ins
    (y_prompt, y_sample, pool_p, k_cmp_p, v_cmp_p, k_slc_p, v_slc_p, k_win_p, v_win_p,
     pool_s, k_cmp_s, v_cmp_s, k_slc_s, v_slc_s, k_win_s, v_win_s) = outs

    with ExitStack() as ctx:
        def sem(name):
            return ctx.enter_context(nc.semaphore(name))

        def dram(name, shape):
            return nc.dram_tensor(name, shape, F32, kind="Internal").ap()

        BASE = 16512
        cursor = [BASE]

        def place(name, shape, dt=F32):
            n = int(np.prod(shape[1:])) * 4
            t = nc.alloc_sbuf_tensor_at(name, list(shape), dt, offset=cursor[0])
            cursor[0] += (n + 31) // 32 * 32
            return t

        RAW = [place(f"raw{i}", [P, 4, 256]) for i in range(4)]
        HI = [place(f"w_hi{i}", [P, 4, 256], F32R) for i in range(2)]
        LO = [place(f"w_lo{i}", [P, 4, 256], F32R) for i in range(2)]
        CON = place("consts", [P, NCONST])
        MODT = place("modT", [P, 2 * ML, NC])
        AMOD = place("a_mod", [P, 2, KT, NC])
        VECT = place("vecT", [P, 80])
        PTAB = place("page_tab", [1, 32], I32)
        h_at = cursor[0]
        HH = place("h_hi", [P, KT, T], F32R)
        HL = place("h_lo", [P, KT, T], F32R)
        h_end = y_at = cursor[0]
        Y = place("y", [P, KT, T])
        x_at = cursor[0]
        X = place("x", [P, KT, T])
        c_at = cursor[0]
        END = 229368

        cursor[0] = h_at
        CROW = place("c_rows", [NC, DM])
        CSIL = place("c_silu", [NC, DM])
        XN = [place(f"x_nat{i}", [P, DM]) for i in range(2)]
        VEC = place("vec_rows", [80, P])
        RELA = place("rel_rows", [33, NH])
        ONEH = place("onehots", [33, 2 * GLEN])
        GROW = place("bias_rows", [NH, 2 * GLEN])
        assert cursor[0] <= h_end
        cursor[0] = y_at
        CST = place("c_split", [P, KT, P], F32R)
        CTF = place("c_cols", [P, KT, NC])
        MROW = place("mod_rows", [19, 2, 256])
        assert cursor[0] <= x_at
        cursor[0] = c_at
        SQ = [place(f"squares{i}", [P, T]) for i in range(2)]
        TN = [place(f"normed{i}", [P, T]) for i in range(2)]
        HF = [place(f"h_full{i}", [P, T]) for i in range(2)]
        RMS = place("rms", [P, T])
        c_norm_end = cursor[0]
        RSTD = nc.alloc_sbuf_tensor_at("rstd", [P, T], F32, offset=(END - 2112) // 32 * 32)
        c_top = (END - 2112) // 32 * 32
        assert cursor[0] <= c_top
        cursor[0] = c_at
        PHI = place("pooled_hi", [P, 4, T], F32R)
        PLO = place("pooled_lo", [P, 4, T], F32R)
        SPN = place("state_rows", [TS * PB, DM])
        PAD = [place(f"window_sum{i}", [P, 16 + TP]) for i in range(2)]
        STMP = place("sample_tmp", [P, 4, TS])
        assert cursor[0] <= END, cursor[0]
        UT = nc.alloc_sbuf_tensor_at("u_rows", [23, DM], F32, offset=c_at)
        cursor[0] = c_at
        ZT = [place(f"z_tile{i}", [P, T]) for i in range(2)]
        RT = [place(f"resid_tmp{i}", [P, TS]) for i in range(2)]
        cursor[0] = c_norm_end
        KS = place("k_slc_T", [P, NKV, T])
        KW = place("k_win_T", [P, NKV, T])
        KCP = place("kc_prompt_T", [P, NKV * NCMP])
        KCS = place("kc_sample_T", [P, TS, NKV * NCMP])
        assert cursor[0] <= c_top, (cursor[0], c_top)
        keep_end = cursor[0]
        VCS = nc.alloc_sbuf_tensor_at("vc_sample", [NKV * NCMP, TS, P], F32, offset=c_at)
        cursor[0] = y_at
        KCF = place("k_cmp_T", [P, NKV, T])
        VCF = place("v_cmp_T", [P, NKV, T])
        VF = place("v_T", [P, NKV, T])
        TM = [place(f"token_rows{i}", [P, 512]) for i in range(4)]
        assert cursor[0] <= x_at
        cursor[0] = h_at
        W1 = [place(f"w_c1_{i}", [P, CL, P]) for i in range(2)]
        PG = [place(f"pages{i}", [P, NPG, 512]) for i in range(2)]
        RT_T = [place(f"rows_T{i}", [P, NKV, TP]) for i in range(2)]
        CSIL2 = [place(f"c_hidden{i}", [P, NKV * NCMP]) for i in range(2)]
        assert cursor[0] <= h_end, (cursor[0], h_end)
        cursor[0] = y_at + 2 * NKV * T * 4
        W2 = [place(f"w_c2_{i}", [P, P]) for i in range(2)]
        PE_ = [place(f"pe{i}", [CL, P]) for i in range(2)]
        PET = [place(f"pe_T{i}", [P, CL]) for i in range(2)]
        PEC = place("pe_term", [P, 2])
        VCP = place("vc_prompt", [NCMP, NKV, P])
        assert cursor[0] <= y_at + 3 * NKV * T * 4 + 0
        cursor[0] = x_at
        PR = place("probs", [P, 1280])
        PT = place("probs_T", [P, 1280])
        VG = place("v_group", [P, 2, NT, P])
        BH = place("bias_heads", [P, 2, 512])
        ZB = place("z_silu", [P, NBR, 2, T])
        TMP = place("o_times_z", [P, TP])
        assert cursor[0] <= c_at
        cursor[0] = c_at + TS * P * 4
        QS = place("q_heads", [P, 2, TP])
        BC = place("bias_cmp", [NCMP, 2, TP])
        VCG = place("vc_group", [NCMP, P])
        GT = place("gate_rows", [P, NT, 48])
        assert cursor[0] <= c_norm_end, (cursor[0], c_norm_end)
        cursor[0] = keep_end
        SZD = place("z_silu_sample", [P, NBR, NH, TS])
        QD = place("q_sample", [P, NH, TS])
        STAT = place("row_stats", [P, 16])
        GF = nc.alloc_sbuf_tensor_at("gates_T", [48, T], F32, offset=y_at)
        assert cursor[0] <= END, cursor[0]
        cursor[0] = h_at
        cursor[0] = h_at
        QPAD = [place(f"q_one_sample{i}", [P, NKV, 32]) for i in range(2)]
        KN = [place(f"k_new{i}", [P, NKV]) for i in range(2)]
        KCB = [place(f"kc_one_sample{i}", [P, NKV * NCMP]) for i in range(2)]
        PTD = [place(f"probs_T_sample{i}", [P, NPG, P]) for i in range(2)]
        PTN = place("probs_T_new", [1, 2, P])
        PTC = place("probs_T_cmp", [NKV * NCMP, P])
        PTG = place("probs_T_cmp_gated", [NKV * NCMP, P])
        SD = [place(f"scores_sample{i}", [P, 513]) for i in range(2)]
        SC = place("scores_cmp", [P, NCMP])
        PX = place("probs_cmp_spread", [P, NKV * NCMP])
        BD = place("bias_sample", [P, 513])
        BCD = place("bias_cmp_sample", [P, NCMP])
        IMP = place("importance", [P, 9])
        DRP = place("dropped", [P, 3, 7])
        GD = place("gates_sample", [P, NBR])
        SST = place("sample_stats", [P, 16])
        VN = [place(f"v_new{i}", [1, 512]) for i in range(2)]
        OD = [place(f"o_sample{i}", [P, TS, NH]) for i in range(NBR)]
        OM = place("o_sample_tmp", [P, NH, TS])
        ZERO = place("zeros", [P, P])
        assert cursor[0] <= h_at + 2 * CL * P * 4, cursor[0] - h_at
        cursor[0] = y_at
        YN = [place(f"y_rows{i}", [P, DM]) for i in range(2)]

        def bank(name):
            return ctx.enter_context(nc.psum_tensor(name, [P, 512], F32))

        D = [bank(f"acc{i}") for i in range(4)]
        S = [bank(f"work{i}") for i in range(3)]
        O = bank("out_acc")

        g_scr = dram("g_scr", (NH, 2 * GLEN))
        b_scr = dram("b_scr", (NH, P, 512))
        c_scr = dram("c_scr", (NH, NCMP, TP))
        x_scr = dram("x_scr", (P, KT * T))
        vc_scr = dram("vc_scr", (NCMP, NKV * P))
        gd_scr = dram("gd_scr", (NBR, P))

        ident = CON[:, C_ID:C_ID + P]
        ones = CON[:, C_ONE:C_ONE + P]

        raw_full = [sem(f"raw_full{i}") for i in range(4)]
        hi_ready = sem("hi_ready")
        lo_ready = sem("lo_ready")
        w_used = sem("w_used")
        first_done = sem("first_tile_done")
        acc_free = sem("acc_free")
        own = {e: sem(f"own_{e}") for e in ("act", "dve", "pool", "pe")}
        s_con = sem("consts_in")
        s_rows = sem("setup_rows_in")
        s_x = [sem(f"x_rows_in{i}") for i in range(2)]
        s_rel = sem("rel_in")
        s_negrow = sem("neg_row")
        s_t = sem("setup_transposed")
        s_te = sem("setup_copied")
        s_csil = sem("c_silu_done")
        s_cz = sem("c_split_zero")
        s_cs = sem("c_split_done")
        s_gscr = sem("bias_rows_out")
        s_bscr = sem("bias_tables_out")
        z_first = sem("z_first_tile_done")
        mr_ready = sem("mod_rows_ready")
        s_brow = [sem(f"b_row_in{i}") for i in range(2)]
        tr_done = sem("mod_turned")
        mt_ready = sem("mod_ready")
        amod = sem("a_mod_ready")
        sq_ready = sem("square_ready")
        sq_used = sem("square_used")
        rms_ready = sem("rms_ready")
        rstd_ready = sem("rstd_ready")
        tn_ready = sem("normed_ready")
        hf_ready = sem("h_full_ready")
        hhi_ready = sem("h_hi_ready")
        h_ready = sem("h_ready")
        s_sp = sem("state_rows_in")
        s_ut = sem("u_turned")
        s_ute = sem("u_rows_ready")
        s_uo = sem("u_rows_out")
        s_ps = sem("prefix_sums")
        s_pooled = sem("pooled_ready")
        s_ph = sem("pooled_hi_ready")
        s_pl = sem("pooled_split")
        zt_ready = sem("z_tile_ready")
        zt_used = sem("z_tile_used")
        kv_copied = sem("kv_tiles_copied")
        kv_tr = sem("kv_turned")
        tm_ready = sem("token_rows_ready")
        tm_out = [sem(f"token_rows_out{i}") for i in range(4)]
        s_copy = sem("states_copied")
        s_cw = sem("compress_weights_in")
        s_pt = sem("page_table_in")
        s_pe = sem("pe_turned")
        s_pee = sem("pe_copied")
        s_pg = [sem(f"pages_in{i}") for i in range(2)]
        ctr = sem("pages_turned")
        ctre = sem("pages_turned_copied")
        cw1 = sem("hidden_done")
        csr = sem("hidden_silu_done")
        cw2 = sem("compressed_done")
        cout = sem("compressed_copied")
        s_vcp = sem("vc_prompt_out")
        s_xs = sem("x_spilled")
        g_tr = sem("gates_turned")
        gt_ready = sem("gate_rows_ready")
        s_gd = sem("gates_sample_out")
        hd_in = sem("head_data_in")
        q_ready = sem("q_ready")
        z_ready = sem("z_ready")
        a_done = sem("scores_done")
        negm = sem("max_ready")
        e_done = sem("exp_done")
        r_ready = sem("row_factor_ready")
        p_ready = sem("probs_ready")
        b_done = sem("probs_turned")
        pt_ready = sem("probs_T_ready")
        c_done = sem("values_done")
        o_used = sem("values_used")
        s_dm = sem("sample_consts_ready")
        s_bd = sem("sample_bias_in")
        qp_ready = sem("q_one_sample_ready")
        kst = sem("sample_keys_staged")
        dsc = sem("sample_scores_done")
        sd_step = sem("sample_softmax_step")
        sd_exp = sem("sample_exp")
        sd_pe = sem("sample_pe_step")
        sd_ev = sem("sample_copied")
        s_vn = [sem(f"v_new_in{i}") for i in range(2)]
        pv = sem("sample_values_done")
        pve = sem("sample_values_copied")
        ydec = sem("y_sample_ready")
        ys_hi = sem("y_hi_ready")
        ys = sem("y_split")
        s_xb = sem("x_back")
        yn_tr = sem("y_turned")
        yn_ready = sem("y_rows_ready")
        yn_out = [sem(f"y_rows_out{i}") for i in range(2)]

        def vec(v, k):
            return VECT[:, v * KT + k:v * KT + k + 1]

        def halves(ap):
            return [ap[:, 0:HT], ap[:, HT:T]]

        def dyn(t, i, n=1):
            return t[:, bass.ds(i, n)] if not isinstance(i, int) else t[:, i:i + n]

        def flat(ap):
            return ap.rearrange("p a n -> p (a n)")

        def cols(w, j, at, n=256):
            w = w.rearrange("(k p) n -> p k n", p=P)[:, 4 * j:4 * j + 4]
            return w[:, :, bass.ds(at, n)] if not isinstance(at, int) else w[:, :, at:at + n]

        w_a, w_oa, w_kv, w_b, w_ob = A["w_in_a"][0], A["w_out_a"][0], A["w_kv"], A["w_in_b"][0], A["w_out_b"][0]
        kv_out_p = [x[0].rearrange("t g d -> t (g d)") for x in (k_cmp_p, v_cmp_p, k_slc_p, v_slc_p, k_win_p, v_win_p)]
        kv_out_s = [x[:, x.shape[1] - 1].rearrange("b g d -> b (g d)") for x in (k_cmp_s, v_cmp_s, k_slc_s, v_slc_s, k_win_s, v_win_s)]

        block = ctx.enter_context(nc.Block())

        @block.sync
        def _(sp):
            o = Own(sp, own["pe"])

            def load(q, j, src, n=256):
                wait(sp, lo_ready, 4 * q + j - 3)
                sp.dma_start(RAW[j][:, :, 0:n], src).then_inc(raw_full[j], 16)

            def quads(q0, w, n, at=lambda i: i * 256):
                def body(i):
                    for j in range(4):
                        load(q0 + i, j, cols(w, j, at(i)))
                looped(sp, o, n, body)

            for l in range(2):
                quads(Q_ADA + 24 * l, A["w_ada"][l], 24)
            quads(Q_U, w_a, 8)
            for g in range(4):
                for c in range(2):
                    load(Q_MIX + g // 2, 2 * (g % 2) + c, cols(A["w_grp"][0][g], 0, 256 * c))
            quads(Q_Z, w_a, 8, lambda i: DM + i * 256)
            quads(Q_OA, w_oa, 8)
            quads(Q_KV, w_kv, 12)
            for j in range(4):
                load(Q_G, j, cols(w_b, j, 4 * DM, 48), 48)

            def heads(i):
                for blk in range(4):
                    for j in range(4):
                        load(Q_H + 4 * i + blk, j, cols(w_b, j, blk * DM + i * 256))
            looped(sp, o, 8, heads)
            quads(Q_OB, w_ob, 8)

        @block.gpsimd
        def _(pool):
            o = Own(pool, own["pool"])
            pool.dma_start(CON[:, :], A["consts"]).then_inc(s_con, 16)
            pool.dma_start(CROW[0:1, :], A["c_prompt"]).then_inc(s_rows, 16)
            pool.dma_start(CROW[1:NC, :], A["c_sample"]).then_inc(s_rows, 16)
            for v, src in enumerate((A["g_norm"][0:1], A["g_norm"][1:2], A["g_kv"].rearrange("(o n) -> o n", o=1),
                                     A["g_final"].rearrange("(o n) -> o n", o=1), A["pool_scale"])):
                pool.dma_start(VEC[KT * v:KT * v + KT, :], src.rearrange("o (k p) -> (o k) p", p=P)).then_inc(s_rows, 16)
            pool.dma_start(RELA[0:32, :], A["rel_bias"]).then_inc(s_rel, 16)
            pool.dma_start(ONEH[:, :], A["onehots"]).then_inc(s_rel, 16)
            pool.dma_start(PTAB[:, :], A["page_table"].rearrange("b n -> (b n)").rearrange("(o n) -> o n", o=1)).then_inc(s_pt, 16)
            nc.gpsimd.memset(CST[:, :, :].bitcast(F32), 0.0).then_inc(s_cz, 1)
            for t in range(5):
                if t >= 2:
                    pool.wait_ge(s_t, 2 + 4 * (t - 1))
                src = A["x_prompt"][0][t * P:(t + 1) * P] if t < NT else A["x_sample"].rearrange("b s d -> (b s) d")
                pool.dma_start(XN[t % 2][0:src.shape[0], :], src).then_inc(s_x[t % 2], 16)
            pool.wait_ge(s_te, 2 + 20 + 6)
            pool.dma_start(g_scr, GROW[:, :]).then_inc(s_gscr, 16)
            pool.wait_ge(s_gscr, 16)
            pool.dma_start(b_scr, bass.AP(tensor=g_scr.tensor, offset=P, ap=[[2 * GLEN, NH], [-1, P], [1, 512]])).then_inc(s_bscr, 16)
            pool.dma_start(c_scr, bass.AP(tensor=g_scr.tensor, offset=GLEN + 481, ap=[[2 * GLEN, NH], [-16, NCMP], [1, TP]])).then_inc(s_bscr, 16)

            def b_rows(l):
                def body(i):
                    for s in range(2):
                        p = 2 * i + s + 24 * l
                        wait(pool, tr_done, p - 1)
                        b = A["b_ada"][l:l + 1]
                        at = (2 * i + s) * 256
                        b = b[:, bass.ds(at, 256)] if not isinstance(at, int) else b[:, at:at + 256]
                        pool.dma_start(MROW[18:19, s, :], b).then_inc(s_brow[s], 16)
                return body
            for l in range(2):
                looped(pool, o, 12, b_rows(l))
            pool.dma_start(pool_s[0][:, 0:PB - 1, :], A["state_pool"][0][:, 1:PB, :]).then_inc(s_copy, 16)
            pool.dma_start(k_win_s[:, 0:TP - 1], A["state_k_win"][:, 1:TP]).then_inc(s_copy, 16)
            pool.dma_start(v_win_s[:, 0:TP - 1], A["state_v_win"][:, 1:TP]).then_inc(s_copy, 16)

            def apply(a):
                pool.wait_ge(rstd_ready, (1, 2, 2, 3)[a])
                for k in range(KT):
                    wait(pool, hf_ready, KT * a + k - 1)
                    nc.gpsimd.tensor_tensor(TN[k % 2][:, :], X[:, k, :], RSTD[:, :], ALU.mult).then_inc(tn_ready, 1)

            apply(0)
            pool.wait_ge(h_ready, KT)
            pool.dma_start(SPN[:, :], A["state_pool"][0].rearrange("b t d -> (b t) d")).then_inc(s_sp, 16)
            pool.wait_ge(s_ute, 4)
            pool.dma_start(pool_p[0, 0], UT[0:PB, :]).then_inc(s_uo, 16)
            pool.dma_start(pool_s[0][:, PB - 1, :], UT[PB:PB + TS, :]).then_inc(s_uo, 16)
            apply(1)

            def kv_rows(i):
                for t in range(5):
                    n = 5 * i + t
                    pool.wait_ge(tm_ready, n + 1)
                    rows = P if t < NT else TS
                    dst = kv_out_p[i][t * P:(t + 1) * P] if t < NT else kv_out_s[i]
                    pool.dma_start(dst, TM[n % 4][0:rows, :]).then_inc(tm_out[n % 4], 16)
            for i in range(5):
                kv_rows(i)
            pool.wait_ge(w_used, 4 * (Q_KV + 12))
            for i, n in enumerate("kv"):
                pool.dma_start(W1[i][:, :, :], A[f"w_c{n}1"].rearrange("(l p) n -> p l n", p=P)).then_inc(s_cw, 16)
            kv_rows(5)
            pool.wait_ge(kv_tr, 30)
            for i, n in enumerate("kv"):
                pool.dma_start(W2[i][:, :], A[f"w_c{n}2"]).then_inc(s_cw, 16)
                pool.dma_start(PE_[i][:, :], A[f"pe_{n}"]).then_inc(s_cw, 16)
            pool.wait_ge(s_pt, 16)

            def page_loads(i, b, free, value, cache):
                page = [pool.value_load(PTAB[0:1, bass.ds(b * NPG + t, 1)], min_val=0, max_val=cache.shape[0] - 1) for t in range(NPG)]
                wait(pool, free, value)
                for t in range(NPG):
                    pool.dma_start(PG[i][:, t, :], cache[bass.ds(page[t], 1)].rearrange("o t g d -> (o t) (g d)")).then_inc(s_pg[i], 16)

            def pages(b):
                for kv, cache in enumerate((A["cache_k_cmp"], A["cache_v_cmp"])):
                    page_loads(kv, b, ctr, 4 * (2 * b + kv) - 4, cache)
            looped(pool, o, TS, pages)
            pool.wait_ge(cout, 18)
            pool.dma_start(vc_scr, VCP[:, :, :].rearrange("p g d -> p (g d)")).then_inc(s_vcp, 16)
            apply(2)
            pool.wait_ge(tn_ready, 3 * KT)
            pool.dma_start(x_scr, flat(X[:, :, :])).then_inc(s_xs, 16)
            pool.wait_ge(acc_free, 2 * (D_G + 1))
            for br in range(NBR):
                for g in range(NKV):
                    pool.dma_start(bass.AP(tensor=gd_scr.tensor, offset=br * P + g * 32, ap=[[1, REP], [4, TS]]),
                                   GF[br * NH + g * REP:br * NH + g * REP + REP, TP:T],
                                   allow_slow_non_contiguous=True).then_inc(s_gd, 16)
            pool.wait_ge(s_gd, 16 * 12)
            pool.wait_ge(s_xs, 16)
            pool.wait_ge(s_vcp, 16)
            pool.wait_ge(s_bscr, 32)
            for s in range(4):
                pool.wait_ge(tm_out[s], 16 * len([n for n in range(30) if n % 4 == s]))

            def head_loads(i):
                wait(pool, c_done, 6 * i)
                g = i // 2
                gd = lambda w: w.rearrange("(t p) (g d) -> g p t d", p=P, d=P)
                for br, v in enumerate((kv_out_p[3], kv_out_p[5])):
                    src = gd(v)
                    src = src[bass.ds(g, 1)] if not isinstance(g, int) else src[g:g + 1]
                    pool.dma_start(VG[:, br, :, :], src.rearrange("o p t d -> (o p) t d")).then_inc(hd_in, 16)
                vs = vc_scr.rearrange("n (g d) -> g n d", d=P)
                vs = vs[bass.ds(g, 1)] if not isinstance(g, int) else vs[g:g + 1]
                pool.dma_start(VCG[:, :], vs.rearrange("o n d -> (o n) d")).then_inc(hd_in, 16)
                h2 = lambda w: (w[bass.ds(i * 2, 2)] if not isinstance(i, int) else w[2 * i:2 * i + 2]).rearrange("h p n -> p h n")
                pool.dma_start(BH[:, :, :], h2(b_scr)).then_inc(hd_in, 16)
                pool.dma_start(BC[:, :, :], h2(c_scr)).then_inc(hd_in, 16)
                for u in range(6):
                    n = 6 * i + u
                    pool.wait_ge(r_ready, n + 1)
                    if u < 2:
                        last = nc.gpsimd.tensor_tensor(
                            PR[:, 0:NT * NCMP].rearrange("p (t n) -> p t n", n=NCMP), PR[:, 0:NT * NCMP].rearrange("p (t n) -> p t n", n=NCMP),
                            STAT[:, 8:12].unsqueeze(2).broadcast_to([P, NT, NCMP]), ALU.mult)
                    else:
                        at = 0
                        for t in range(NT):
                            w = P * (t + 1)
                            last = nc.gpsimd.tensor_tensor(PR[:, at:at + w], PR[:, at:at + w],
                                                           STAT[:, 8 + t:9 + t].broadcast_to([P, w]), ALU.mult)
                            at += w
                    last.then_inc(p_ready, 1)
            looped(pool, o, 8, head_loads)

            pool.wait_ge(w_used, 4 * Q_OB)
            nc.gpsimd.memset(PX[:, :], 0.0)
            nc.gpsimd.memset(ZERO[:, :], 0.0).then_inc(s_dm, 1)
            pool.dma_start(GD[:, :], bass.AP(tensor=gd_scr.tensor, offset=0, ap=[[1, P], [P, NBR]]),
                           allow_slow_non_contiguous=True).then_inc(s_bd, 16)
            for g in range(NKV):
                for b in range(TS):
                    r = 32 * g + 4 * b
                    pool.dma_start(BD[r:r + 4, :], g_scr[4 * g:4 * g + 4, 0:513]).then_inc(s_bd, 16)
                    pool.dma_start(BCD[r:r + 4, :], g_scr[4 * g:4 * g + 4, 31:31 + 16 * NCMP:16],
                                   allow_slow_non_contiguous=True).then_inc(s_bd, 16)

            def state_load(i, b, state):
                src = state.rearrange("b (t p) g d -> b p t (g d)", p=P)
                src = src[bass.ds(b, 1)] if not isinstance(b, int) else src[b:b + 1]
                pool.dma_start(PG[i][:, :, :], src.rearrange("o p t n -> (o p) t n")).then_inc(s_pg[i], 16)

            def key_loads(br):
                def body(i):
                    for s in range(2):
                        b = 2 * i + s
                        m = 8 * br + b
                        if br == 0:
                            page_loads(s, b, ctr, 64 + 4 * m - 4, A["cache_k_slc"])
                        else:
                            pool.wait_ge(ctr, 64 + 4 * m - 4)
                            state_load(s, b, A["state_k_win"])
                        pool.wait_ge(dsc, m + 1)
                        q = QD[:, :, :].rearrange("p (g r) b -> p g b r", g=NKV)
                        mk = CON[:, bass.ds(b * 8 + C_MSK, 8)] if not isinstance(b, int) else CON[:, C_MSK + 8 * b:C_MSK + 8 * b + 8]
                        mk = mk.unsqueeze(1).unsqueeze(3).broadcast_to([P, NKV, TS, REP])
                        nc.gpsimd.tensor_tensor(QPAD[s][:, :, :].rearrange("p g (b r) -> p g b r", b=TS), q, mk, ALU.mult).then_inc(qp_ready, 1)
                return body
            for br in range(2):
                looped(pool, o, 4, key_loads(br))

            def value_loads(br):
                def body(i):
                    for s in range(2):
                        b = 2 * i + s
                        m = 8 * br + b
                        pool.wait_ge(ctr, 64 + 64)
                        if br == 0:
                            page_loads(s, b, pv, m - 1, A["cache_v_slc"])
                        else:
                            pool.wait_ge(pv, m - 1)
                            state_load(s, b, A["state_v_win"])
                        src = kv_out_s[3 if br == 0 else 5]
                        src = src[bass.ds(b, 1)] if not isinstance(b, int) else src[b:b + 1]
                        pool.dma_start(VN[s][:, :], src).then_inc(s_vn[s], 16)
                return body
            for br in range(2):
                looped(pool, o, 4, value_loads(br))
            pool.wait_ge(ydec, 1)
            pool.dma_start(flat(X[:, :, :]), x_scr).then_inc(s_xb, 16)
            apply(3)
            for t in range(5):
                pool.wait_ge(yn_ready, 4 * (t + 1))
                rows = P if t < NT else TS
                dst = y_prompt[0, t * P:(t + 1) * P] if t < NT else y_sample[:, 0]
                pool.dma_start(dst, YN[t % 2][0:rows, :]).then_inc(yn_out[t % 2], 16)
            pool.wait_ge(yn_out[0], 48)
            pool.wait_ge(yn_out[1], 32)
            pool.wait_ge(s_copy, 48)
            pool.wait_ge(s_uo, 32)

        @block.scalar
        def _(act):
            o = Own(act, own["act"])

            def hi(q, j, n=256):
                act.wait_ge(raw_full[j], 16 * (q + 1))
                wait(act, w_used, 4 * q + j - 1)
                nc.scalar.activation(HI[j % 2][:, :, 0:n], RAW[j][:, :, 0:n], ACT.Copy).then_inc(hi_ready, 1)

            act.wait_ge(s_rows, 16 * 7)
            nc.scalar.activation(CSIL[:, :], CROW[:, :], ACT.Silu).then_inc(s_csil, 1)
            act.wait_ge(s_te, 2)
            act.wait_ge(s_cz, 1)
            nc.scalar.activation(CST[:, :, 0:NC], CTF[:, :, :], ACT.Copy).then_inc(s_cs, 1)

            def ada(l):
                def body(i):
                    for s in range(2):
                        p = 2 * i + s + 24 * l
                        for j in range(4):
                            hi(Q_ADA + p, j)
                        act.wait_ge(w_used, 4 * (Q_ADA + p) + 4)
                        wait(act, tr_done, p - 1)
                        nc.scalar.activation(MROW[0:18, s, :], D[s][0:18, 0:256], ACT.Copy).then_inc(mr_ready, 1)
                return body
            for l in range(2):
                looped(act, o, 12, ada(l))

            def stats(r):
                for k in range(KT):
                    if r:
                        act.wait_ge(acc_free, 2 * (0, D_OA, D_OB)[r] + k + 1)
                    wait(act, sq_used, KT * r + k - 1)
                    nc.scalar.activation(SQ[k % 2][:, :], X[:, k, :], ACT.Square).then_inc(sq_ready, 1)
                act.wait_ge(sq_used, KT * (r + 1))
                for half in range(2):
                    last = nc.scalar.activation(RMS[:, half * HT:(half + 1) * HT], S[half][:, 0:HT], ACT.Sqrt,
                                                scale=1.0 / DM, bias=CON[:, C_EPS:C_EPS + 1])
                last.then_inc(rms_ready, 1)

            def apply_hi(a):
                for k in range(KT):
                    act.wait_ge(hf_ready, KT * a + k + 1)
                    nc.scalar.activation(HH[:, k, :], HF[k % 2][:, :], ACT.Copy).then_inc(hhi_ready, 1)

            stats(0)
            apply_hi(0)

            def dense_tile(q, d, mm):
                if mm == 0:
                    act.wait_ge(first_done, d + 1)
                else:
                    act.wait_ge(w_used, 4 * q + 4)

            def evac(dst, mm):
                for half, h in enumerate(halves(dst)):
                    last = nc.scalar.activation(h, D[2 * mm + half][:, 0:HT], ACT.Copy)
                last.then_inc(acc_free, 1)

            def u_pairs(i):
                for j in range(4):
                    hi(Q_U + i, j)
                for mm in range(2):
                    dense_tile(Q_U + i, D_U + i, mm)
                    dst = dyn(Y, 2 * i + mm).rearrange("p o t -> p (o t)")
                    evac(dst, mm)
            looped(act, o, 8, u_pairs)
            act.wait_ge(s_uo, 32)
            for g in range(4):
                act.wait_ge(s_pooled, g + 1)
                wait(act, w_used, 4 * Q_MIX + 2 * g)
                nc.scalar.activation(PHI[:, :, :], Y[:, 4 * g:4 * g + 4, :], ACT.Copy).then_inc(s_ph, 1)
                for c in range(2):
                    hi(Q_MIX + g // 2, 2 * (g % 2) + c)
                for c in range(2):
                    for mm in range(2):
                        n = 2 * g + c
                        if mm == 0:
                            act.wait_ge(first_done, D_MIX + n + 1)
                        else:
                            act.wait_ge(w_used, 4 * Q_MIX + n + 1)
                        m = 4 * g + 2 * c + mm
                        for half, h in enumerate(halves(Y[:, m, :])):
                            last = nc.scalar.activation(h, D[2 * mm + half][:, 0:HT], ACT.Copy, scale=vec(4, m))
                        last.then_inc(acc_free, 1)

            def z_pairs(i):
                for j in range(4):
                    hi(Q_Z + i, j)
                for mm in range(2):
                    if mm == 0:
                        act.wait_ge(z_first, i + 1)
                    else:
                        act.wait_ge(w_used, 4 * (Q_Z + i) + 4)
                    wait(act, zt_used, 2 * i + mm - 1)
                    for half, h in enumerate(halves(ZT[mm])):
                        last = nc.scalar.activation(h, D[2 * mm + half][:, 0:HT], ACT.Silu)
                    last.then_inc(zt_ready, 1)
            looped(act, o, 8, z_pairs)

            def y_hi(n):
                for k in range(KT):
                    if n == 0:
                        act.wait_ge(zt_used, k + 1)
                    if k == 0:
                        act.wait_ge(w_used, 4 * (Q_OA if n == 0 else Q_OB))
                        if n == 1:
                            act.wait_ge(ydec, 1)
                    nc.scalar.activation(HH[:, k, :], Y[:, k, :], ACT.Copy).then_inc(ys_hi, 1)

            def his(q0, n):
                def body(i):
                    for j in range(4):
                        hi(q0 + i, j)
                looped(act, o, n, body)
            y_hi(0)
            his(Q_OA, 8)
            stats(1)
            act.wait_ge(w_used, 4 * Q_KV)
            apply_hi(1)
            for i, dst in enumerate((KCF, VCF, KS, VF, KW, VF)):
                if i == 5:
                    act.wait_ge(kv_tr, 20)

                def kv_pair(pp, i=i, dst=dst):
                    q, d = Q_KV + 2 * i + pp, D_KV + 2 * i + pp
                    for j in range(4):
                        hi(q, j)
                    for mm in range(2):
                        dense_tile(q, d, mm)
                        for half in range(2):
                            to = dyn(dst, 2 * pp + mm)[:, :, half * HT:(half + 1) * HT].rearrange("p o t -> p (o t)")
                            last = nc.scalar.activation(to, D[2 * mm + half][:, 0:HT], ACT.Copy)
                        last.then_inc(acc_free, 1)
                looped(act, o, 2, kv_pair)

            def hidden(n, kv, base):
                act.wait_ge(cw1, n + 1)
                if base:
                    act.wait_ge(cw2, n - 1)
                nc.scalar.activation(CSIL2[kv][:, :], S[2][:, 0:NKV * NCMP], ACT.Silu, bias=PEC[:, kv:kv + 1]).then_inc(csr, 1)

            act.wait_ge(s_pee, 3)

            def hiddens(b):
                for kv in range(2):
                    hidden(2 * b + kv, kv, not isinstance(b, int))
            looped(act, o, TS, hiddens)
            for kv in range(2):
                hidden(16 + kv, kv, True)
            act.wait_ge(cw2, 18)
            apply_hi(2)
            for j in range(4):
                hi(Q_G, j, 48)
            act.wait_ge(w_used, 4 * (Q_G + 1))
            for half in range(2):
                last = nc.scalar.activation(GF[:, half * HT:(half + 1) * HT], D[half][0:48, 0:HT], ACT.Sigmoid)
            last.then_inc(acc_free, 2)

            def exps(n, u):
                act.wait_ge(negm, n + 1)
                if u < 2:
                    nc.scalar.activation(PR[:, 0:NT * NCMP], PR[:, 0:NT * NCMP], ACT.Exp).then_inc(e_done, 1)
                else:
                    at = 0
                    for t in range(NT):
                        w = P * (t + 1)
                        last = nc.scalar.activation(PR[:, at:at + w], PR[:, at:at + w], ACT.Exp,
                                                    bias=STAT[:, t:t + 1], accum_out=STAT[:, 4 + t:5 + t])
                        at += w
                    last.then_inc(e_done, 1)

            def turned(n, u):
                act.wait_ge(b_done, n + 1)
                wait(act, c_done, n)
                if u < 2:
                    nc.scalar.activation(PT[0:NCMP, 0:512], S[0][0:NCMP, :], ACT.Copy).then_inc(pt_ready, 1)
                else:
                    nc.scalar.activation(PT[:, 0:512], S[0][:, :], ACT.Copy)
                    nc.scalar.activation(PT[:, 512:1024], S[1][:, :], ACT.Copy)
                    nc.scalar.activation(PT[:, 1024:1280], S[2][:, 0:256], ACT.Copy).then_inc(pt_ready, 1)

            act.wait_ge(s_xs, 16)

            def heads(i):
                for s in range(17):
                    if s < 16:
                        hi(Q_H + 4 * i + s // 4, s % 4)
                    if s >= 4 and s % 4 == 0:
                        blk = s // 4 - 1
                        for mm in range(2):
                            dense_tile(Q_H + 4 * i + blk, D_H + 4 * i + blk, mm)
                            if blk == 0:
                                wait(act, a_done, 6 * i)
                                nc.scalar.activation(QS[:, mm, 0:HT], D[2 * mm][:, 0:HT], ACT.Copy, scale=SCALE)
                                nc.scalar.activation(QS[:, mm, HT:TP], D[2 * mm + 1][:, 0:TP - HT], ACT.Copy, scale=SCALE)
                                to = dyn(QD, 2 * i + mm).rearrange("p o b -> p (o b)")
                                nc.scalar.activation(to, D[2 * mm + 1][:, TP - HT:HT], ACT.Copy, scale=SCALE).then_inc(acc_free, 1)
                            else:
                                wait(act, o_used, 6 * i)
                                for half in range(2):
                                    nc.scalar.activation(ZB[:, blk - 1, mm, half * HT:(half + 1) * HT], D[2 * mm + half][:, 0:HT], ACT.Silu)
                                to = SZD[:, blk - 1]
                                to = dyn(to, 2 * i + mm).rearrange("p o b -> p (o b)")
                                nc.scalar.activation(to, D[2 * mm + 1][:, TP - HT:HT], ACT.Silu).then_inc(acc_free, 1)
                    u = (s - 4) // 2
                    if s >= 4 and s % 2 == 0 and u < 6:
                        exps(6 * i + u, u)
                    if s >= 5 and s % 2 == 1:
                        turned(6 * i + (s - 5) // 2, (s - 5) // 2)
            looped(act, o, 8, heads)

            for br in range(2):
                def stage(i, br=br):
                    for s in range(2):
                        b = 2 * i + s
                        m = 8 * br + b
                        act.wait_ge(dsc, m + 1)
                        if br == 0:
                            nc.scalar.activation(KCB[s][:, :], dyn(KCS, b).rearrange("p o n -> p (o n)"), ACT.Copy)
                        kt_ = (KS if br == 0 else KW)
                        kn = kt_[:, :, bass.ds(b + TP, 1)] if not isinstance(b, int) else kt_[:, :, b + TP:b + TP + 1]
                        nc.scalar.activation(KN[s][:, :], kn.rearrange("p g o -> p (g o)"), ACT.Copy).then_inc(kst, 1)
                looped(act, o, 4, stage)
            for n in range(3):
                act.wait_ge(sd_step, n + 1)
                src = (SC[:, :], SD[0][:, :], SD[1][:, :])[n]
                nc.scalar.activation(src, src, ACT.Exp, bias=SST[:, n:n + 1], accum_out=SST[:, 4 + n:5 + n]).then_inc(sd_exp, 1)
            y_hi(1)
            his(Q_OB, 8)
            stats(2)

        @block.vector
        def _(dve):
            o = Own(dve, own["dve"])
            V = nc.vector

            def lo(q, j, n=256):
                dve.wait_ge(hi_ready, 4 * q + j + 1)
                V.tensor_tensor(LO[j % 2][:, :, 0:n], RAW[j][:, :, 0:n], HI[j % 2][:, :, 0:n].bitcast(F32), ALU.subtract).then_inc(lo_ready, 1)

            V.memset(RELA[32:33, :], NEG).then_inc(s_negrow, 1)
            dve.wait_ge(s_t, 1)
            V.tensor_copy(VECT[:, :], S[0][:, 0:80]).then_inc(s_te, 1)
            dve.wait_ge(s_t, 2)
            V.tensor_copy(flat(CTF[:, :, :]), S[1][:, 0:KT * NC]).then_inc(s_te, 1)
            dve.wait_ge(s_cs, 1)
            V.tensor_tensor(CST[:, :, NC:2 * NC], CTF[:, :, :], CST[:, :, 0:NC].bitcast(F32), ALU.subtract).then_inc(s_cs, 1)
            for t in range(5):
                n = P if t < NT else TS
                for k4 in range(4):
                    dve.wait_ge(s_t, 2 + 4 * t + k4 + 1)
                    V.tensor_copy(X[:, 4 * k4:4 * k4 + 4, t * P:t * P + n],
                                  S[k4 % 2][:, :].rearrange("p (k t) -> p k t", k=4)[:, :, 0:n]).then_inc(s_te, 1)
            for n in range(6):
                dve.wait_ge(s_t, 22 + n + 1)
                at = (n // 3) * GLEN + (n % 3) * 512
                w = min(512, GLEN - (n % 3) * 512)
                V.tensor_copy(GROW[:, at:at + w], S[n % 2][0:NH, 0:w]).then_inc(s_te, 1)

            def ada(l):
                def body(i):
                    for s in range(2):
                        p = 2 * i + s + 24 * l
                        for j in range(4):
                            lo(Q_ADA + p, j)
                        dve.wait_ge(tr_done, p + 1)
                        V.tensor_copy(dyn(MODT, 2 * p, 2), S[s][:, 0:2 * NC].rearrange("p (a n) -> p a n", a=2)).then_inc(mt_ready, 1)
                return body
            for l in range(2):
                looped(dve, o, 12, ada(l))
            dve.wait_ge(mt_ready, 48)
            for l in range(2):
                o(V.tensor_scalar(AMOD[:, l, :, :], MODT[:, ML * l + KT:ML * l + 2 * KT, :], 1.0, None, ALU.add))
                o(V.tensor_tensor(AMOD[:, l, :, :], AMOD[:, l, :, :],
                                  VECT[:, KT * l:KT * l + KT].unsqueeze(2).broadcast_to([P, KT, NC]), ALU.mult))

            def rstd(r):
                dve.wait_ge(rms_ready, r + 1)
                V.reciprocal(RSTD[:, :], RMS[:, :]).then_inc(rstd_ready, 1)

            def apply_lo(a, k):
                dve.wait_ge(hhi_ready, KT * a + k + 1)
                V.tensor_tensor(HL[:, k, :], HF[k % 2][:, :], HH[:, k, :].bitcast(F32), ALU.subtract).then_inc(h_ready, 1)

            def apply(a):
                l = {0: 0, 1: None, 2: 1}[a]
                for k in range(KT):
                    dve.wait_ge(tn_ready, KT * a + k + 1)
                    tn, hf = TN[k % 2], HF[k % 2]
                    if a or k >= 2:
                        dve.wait_ge(h_ready, KT * a + k - 1)
                    if l is None:
                        V.tensor_scalar(hf[:, :], tn[:, :], vec(2, k), None, ALU.mult).then_inc(hf_ready, 1)
                    else:
                        sh = ML * l + k
                        o(V.tensor_tensor(hf[:, TP:T], tn[:, TP:T], AMOD[:, l, k, 1:NC], ALU.mult))
                        V.tensor_tensor(hf[:, TP:T], hf[:, TP:T], MODT[:, sh, 1:NC], ALU.add)
                        V.tensor_scalar(hf[:, 0:TP], tn[:, 0:TP], AMOD[:, l, k, 0:1], MODT[:, sh, 0:1], ALU.mult, ALU.add).then_inc(hf_ready, 1)
                    if k:
                        apply_lo(a, k - 1)
                apply_lo(a, KT - 1)

            rstd(0)
            apply(0)

            def los(q0, n):
                def body(i):
                    for j in range(4):
                        lo(q0 + i, j)
                looped(dve, o, n, body)
            los(Q_U, 8)
            for k4 in range(4):
                dve.wait_ge(s_ut, k4 + 1)
                V.tensor_copy(UT[:, 512 * k4:512 * k4 + 512], S[k4 % 2][0:23, :]).then_inc(s_ute, 1)
            dve.wait_ge(s_ps, 1)
            for i in range(2):
                o(V.memset(PAD[i][:, 0:16], 0.0))
            for g, w in enumerate(WINDOWS):
                us = Y[:, 4 * g:4 * g + 4, TP:T]
                ps = O[:, 32 * g:32 * g + 32].rearrange("p (k b) -> p k b", k=4)
                o(V.tensor_tensor(STMP[:, :, :], ps, us, ALU.add))
                o(V.scalar_tensor_tensor(out=us, in0=STMP[:, :, :], scalar=1.0 / w, in1=us, op0=ALU.mult, op1=ALU.subtract))
                for k in range(4 * g, 4 * g + 4):
                    u = Y[:, k, 0:TP]
                    o(V.tensor_copy(PAD[0][:, 16:16 + TP], u))
                    src, step = 0, 1
                    while step < w:
                        o(V.tensor_tensor(PAD[1 - src][:, 16:16 + TP], PAD[src][:, 16:16 + TP], PAD[src][:, 16 - step:16 + TP - step], ALU.add))
                        src, step = 1 - src, 2 * step
                    s = PAD[src]
                    o(V.tensor_tensor(s[:, 16:32], s[:, 16:32], CON[:, C_CNT + 16 * g:C_CNT + 16 * g + 16], ALU.mult))
                    o(V.tensor_tensor(u[:, 0:16], s[:, 16:32], u[:, 0:16], ALU.subtract))
                    last = V.scalar_tensor_tensor(out=u[:, 16:TP], in0=s[:, 32:16 + TP], scalar=1.0 / w, in1=u[:, 16:TP],
                                                  op0=ALU.mult, op1=ALU.subtract)
                    if k == 4 * g + 3:
                        last.then_inc(s_pooled, 1)
                    else:
                        o(last)
                dve.wait_ge(s_ph, g + 1)
                V.tensor_tensor(PLO[:, :, :], Y[:, 4 * g:4 * g + 4, :], PHI[:, :, :].bitcast(F32), ALU.subtract).then_inc(s_pl, 1)
                for c in range(2):
                    lo(Q_MIX + g // 2, 2 * (g % 2) + c)

            def z_pairs(i):
                for j in range(4):
                    lo(Q_Z + i, j)
                for mm in range(2):
                    dve.wait_ge(zt_ready, 2 * i + mm + 1)
                    y = dyn(Y, 2 * i + mm).rearrange("p o t -> p (o t)")
                    V.tensor_tensor(y, y, ZT[mm][:, :], ALU.mult).then_inc(zt_used, 1)
            looped(dve, o, 8, z_pairs)

            def y_lo(n):
                for k in range(KT):
                    dve.wait_ge(ys_hi, KT * n + k + 1)
                    V.tensor_tensor(HL[:, k, :], Y[:, k, :], HH[:, k, :].bitcast(F32), ALU.subtract).then_inc(ys, 1)
            y_lo(0)

            def resid(l, q0, d0):
                def body(i):
                    for j in range(4):
                        lo(q0 + i, j)
                    for mm in range(2):
                        m = 2 * i + mm
                        if mm == 0:
                            dve.wait_ge(first_done, d0 + i + 1)
                        else:
                            dve.wait_ge(w_used, 4 * (q0 + i) + 4)
                        x = dyn(X, m).rearrange("p o t -> p (o t)")
                        gate = dyn(MODT, m + ML * l + 2 * KT).rearrange("p o n -> p (o n)")
                        a, b = D[2 * mm], D[2 * mm + 1]
                        V.scalar_tensor_tensor(out=x[:, 0:HT], in0=a[:, 0:HT], scalar=gate[:, 0:1], in1=x[:, 0:HT], op0=ALU.mult, op1=ALU.add)
                        V.scalar_tensor_tensor(out=x[:, HT:TP], in0=b[:, 0:TP - HT], scalar=gate[:, 0:1], in1=x[:, HT:TP], op0=ALU.mult, op1=ALU.add)
                        dve.wait_ge(acc_free, 2 * (d0 + i) + mm - 1)
                        o(V.tensor_tensor(RT[mm][:, :], b[:, TP - HT:HT], gate[:, 1:NC], ALU.mult))
                        V.tensor_tensor(x[:, TP:T], x[:, TP:T], RT[mm][:, :], ALU.add).then_inc(acc_free, 1)
                return body
            looped(dve, o, 8, resid(0, Q_OA, D_OA))
            rstd(1)
            apply(1)

            for i, src in enumerate((KCF, VCF, KS, VF, KW, VF)):
                los(Q_KV + 2 * i, 2)
                for t in range(5):
                    n = 5 * i + t
                    rows = P if t < NT else TS
                    dve.wait_ge(kv_tr, n + 1)
                    if n >= 4:
                        dve.wait_ge(tm_out[n % 4], 16 * (n // 4))
                    V.tensor_copy(TM[n % 4][0:rows, :], S[n % 2][0:rows, :]).then_inc(tm_ready, 1)

            for kv in range(2):
                dve.wait_ge(s_pe, kv + 1)
                V.tensor_copy(PET[kv][:, :], S[kv][:, 0:CL]).then_inc(s_pee, 1)
            dve.wait_ge(s_pe, 3)
            V.tensor_copy(PEC[:, :], O[:, 0:2]).then_inc(s_pee, 1)

            def compress_out(n, kv, b):
                dve.wait_ge(cw2, n + 1)
                if kv == 0:
                    dst = dyn(KCS, b).rearrange("p o n -> p (o n)")
                    V.tensor_copy(dst, O[:, 0:NKV * NCMP]).then_inc(cout, 1)
                else:
                    dst = VCS[:, bass.ds(b, 1), :] if not isinstance(b, int) else VCS[:, b:b + 1, :]
                    V.tensor_copy(dst.rearrange("p o n -> p (o n)"), O[0:NKV * NCMP, 0:P]).then_inc(cout, 1)

            def pages_out(n, slot, base=0):
                for g in range(NKV):
                    dve.wait_ge(ctr, 4 * n + g + 1 + base)
                    V.tensor_copy(RT_T[slot][:, g, :], S[g % 2][:, :]).then_inc(ctre, 1)

            def compress(b):
                for kv in range(2):
                    pages_out(2 * b + kv, kv)
                    compress_out(2 * b + kv, kv, b)
            looped(dve, o, TS, compress)
            dve.wait_ge(cw2, 17)
            V.tensor_copy(KCP[:, :], O[:, 0:NKV * NCMP]).then_inc(cout, 1)
            dve.wait_ge(cw2, 18)
            V.tensor_copy(flat(VCP[:, :, :]), O[0:NCMP, :]).then_inc(cout, 1)

            apply(2)
            for j in range(4):
                lo(Q_G, j, 48)
            dve.wait_ge(g_tr, 1)
            V.tensor_copy(flat(GT[:, :, :]), S[0][:, 0:NT * 48]).then_inc(gt_ready, 1)
            dve.wait_ge(gt_ready, 1)
            dve.wait_ge(s_xs, 16)

            W_AT = [0, 1, 3, 6]

            def softmax(i, u):
                n, br, hh = 6 * i + u, u // 2, u % 2
                dve.wait_ge(a_done, n + 1)
                if u == 0:
                    dve.wait_ge(hd_in, 80 * (i + 1))
                wait(dve, b_done, n)
                if u < 2:
                    sc = S[0][:, 0:NT * NCMP].rearrange("p (t n) -> p t n", n=NCMP)
                    pr = PR[:, 0:NT * NCMP].rearrange("p (t n) -> p t n", n=NCMP)
                    o(V.tensor_reduce(STAT[:, 0:4], sc, AX.X, ALU.max))
                    V.tensor_tensor(pr, sc, STAT[:, 0:4].unsqueeze(2).broadcast_to([P, NT, NCMP]), ALU.subtract).then_inc(negm, 1)
                else:
                    where = (S[1][:, 384:512], S[2][:, 0:256], S[1][:, 0:384], S[0][:, :])
                    V.memset(STAT[:, 12:13], 0.0)
                    for t in range(NT):
                        w = P * (t + 1)
                        at = W_AT[t] * P
                        last = V.tensor_tensor_reduce(PR[:, at:at + w], where[t], BH[:, hh, (3 - t) * P:512], 1.0, -3e38,
                                                      ALU.add, ALU.max, STAT[:, t:t + 1])
                    o(last)
                    V.tensor_scalar(STAT[:, 0:4], STAT[:, 0:4], -1.0, None, ALU.mult).then_inc(negm, 1)

            def factor(i, u):
                n, br, hh = 6 * i + u, u // 2, u % 2
                dve.wait_ge(e_done, n + 1)
                if u < 2:
                    o(V.tensor_reduce(STAT[:, 4:8], PR[:, 0:NT * NCMP].rearrange("p (t n) -> p t n", n=NCMP), AX.X, ALU.add))
                o(V.reciprocal(STAT[:, 8:12], STAT[:, 4:8]))
                at = 2 * i + (br * NH + hh)
                gate = GT[:, :, bass.ds(at, 1)] if not isinstance(at, int) else GT[:, :, at:at + 1]
                mul = V.tensor_tensor(STAT[:, 8:12], STAT[:, 8:12], gate.rearrange("p t o -> p (t o)"), ALU.mult)
                if u < 2:
                    o(mul)
                    mul = V.tensor_tensor(STAT[:, 8:9], STAT[:, 8:9], CON[:, C_VIS:C_VIS + 1], ALU.mult)
                mul.then_inc(r_ready, 1)

            def values(i, u):
                n, br, hh = 6 * i + u, u // 2, u % 2
                dve.wait_ge(c_done, n + 1)
                dve.wait_ge(acc_free, 2 * (D_H + 4 * i + br + 1) + hh + 1)
                y = dyn(Y, 2 * i + hh)[:, :, 0:TP].rearrange("p o t -> p (o t)")
                if br == 0:
                    V.tensor_tensor(y, O[:, :], ZB[:, br, hh, 0:TP], ALU.mult).then_inc(o_used, 1)
                else:
                    V.tensor_tensor(TMP[:, :], O[:, :], ZB[:, br, hh, 0:TP], ALU.mult).then_inc(o_used, 1)
                    dve.wait_ge(o_used, n + 1)
                    o(V.tensor_tensor(y, y, TMP[:, :], ALU.add))

            def heads(i):
                for s in range(17):
                    if s < 16:
                        lo(Q_H + 4 * i + s // 4, s % 4)
                    if s >= 4 and s % 2 == 0 and s < 16:
                        softmax(i, (s - 4) // 2)
                        factor(i, (s - 4) // 2)
                    if s >= 8 and s % 2 == 0:
                        values(i, (s - 8) // 2)
                values(i, 5)
            looped(dve, o, 8, heads)

            dve.wait_ge(s_bd, 16 * 65)
            dve.wait_ge(s_dm, 1)
            for br in range(2):
                def keys(i, br=br):
                    for s in range(2):
                        pages_out(8 * br + 2 * i + s, s, 64)
                looped(dve, o, 4, keys)
            dve.wait_ge(sd_pe, 1)
            o(V.tensor_tensor(SC[:, :], D[3][:, 0:NCMP], BCD[:, :], ALU.add))
            o(V.tensor_reduce(SST[:, 0:1], SC[:, :], AX.X, ALU.max))
            V.tensor_scalar(SST[:, 0:1], SST[:, 0:1], -1.0, None, ALU.mult).then_inc(sd_step, 1)
            dve.wait_ge(sd_exp, 1)
            o(V.reciprocal(SST[:, 8:9], SST[:, 4:5]))
            o(V.tensor_scalar(SC[:, :], SC[:, :], SST[:, 8:9], None, ALU.mult))
            for g in range(NKV):
                last = V.tensor_copy(PX[32 * g:32 * g + 32, NCMP * g:NCMP * g + NCMP], SC[32 * g:32 * g + 32, :])
            last.then_inc(sd_ev, 1)
            dve.wait_ge(sd_pe, 2)
            V.tensor_copy(PTC[:, :], S[0][0:NKV * NCMP, 0:P]).then_inc(sd_ev, 1)
            V.tensor_scalar(PX[:, :], PX[:, :], GD[:, 0:1], None, ALU.mult).then_inc(sd_ev, 1)
            dve.wait_ge(sd_pe, 3)
            V.tensor_copy(IMP[:, :], S[1][:, 0:9]).then_inc(sd_ev, 1)
            dve.wait_ge(sd_pe, 4)
            V.tensor_copy(PTG[:, :], S[0][0:NKV * NCMP, P:2 * P]).then_inc(sd_ev, 1)
            dve.wait_ge(sd_pe, 5)
            o(V.tensor_copy(DRP[:, 0, :], S[2][:, 1:8]))
            o(V.tensor_reduce(SST[:, 12:13], DRP[:, 0, :], AX.X, ALU.min))
            o(V.tensor_scalar(DRP[:, 1, :], DRP[:, 0, :], SST[:, 12:13], None, ALU.is_equal))
            o(V.tensor_tensor(DRP[:, 1, :], DRP[:, 1, :], CON[:, C_IOTA:C_IOTA + 7], ALU.mult))
            o(V.tensor_reduce(SST[:, 13:14], DRP[:, 1, :], AX.X, ALU.max))
            o(V.tensor_scalar(DRP[:, 2, :], DRP[:, 1, :], SST[:, 13:14], NEG, ALU.is_equal, ALU.mult))
            for br in range(2):
                o(V.tensor_tensor(SD[br][:, 0:512], D[br][:, :], BD[:, 0:512], ALU.add))
                o(V.tensor_tensor(SD[br][:, 512:513], D[2][:, br:br + 1], BD[:, 512:513], ALU.add))
                if br == 0:
                    blocks = SD[0][:, 64:512].rearrange("p (j n) -> p j n", j=7)
                    o(V.tensor_tensor(blocks, blocks, DRP[:, 2, :].unsqueeze(2).broadcast_to([P, 7, 64]), ALU.add))
                else:
                    o(V.tensor_scalar(SD[1][:, 0:1], SD[1][:, 0:1], NEG, None, ALU.add))
                o(V.tensor_reduce(SST[:, 1 + br:2 + br], SD[br][:, :], AX.X, ALU.max))
                V.tensor_scalar(SST[:, 1 + br:2 + br], SST[:, 1 + br:2 + br], -1.0, None, ALU.mult).then_inc(sd_step, 1)
            for br in range(2):
                dve.wait_ge(sd_exp, 2 + br)
                o(V.reciprocal(SST[:, 9 + br:10 + br], SST[:, 5 + br:6 + br]))
                o(V.tensor_tensor(SST[:, 9 + br:10 + br], SST[:, 9 + br:10 + br], GD[:, 1 + br:2 + br], ALU.mult))
                V.tensor_scalar(SD[br][:, :], SD[br][:, :], SST[:, 9 + br:10 + br], None, ALU.mult).then_inc(sd_ev, 1)
            for br in range(2):
                dve.wait_ge(sd_pe, 7)
                V.tensor_copy(flat(PTD[br][:, :, :]), S[br][:, :])
                V.tensor_copy(PTN[:, br, :], S[2][0:1, P * br:P * br + P]).then_inc(sd_ev, 1)
            dve.wait_ge(sd_pe, 8)
            V.tensor_copy(OD[0][:, :, :].rearrange("p b h -> p (b h)"), O[:, 0:P]).then_inc(sd_ev, 1)
            for br in range(2):
                def vals(i, br=br):
                    for s in range(2):
                        b = 2 * i + s
                        m = 8 * br + b
                        dve.wait_ge(pv, m + 1)
                        V.tensor_copy(dyn(OD[1 + br], b).rearrange("p o h -> p (o h)"), S[s][:, 0:NH]).then_inc(pve, 1)
                looped(dve, o, 4, vals)
            dve.wait_ge(pve, 16)
            dve.wait_ge(sd_ev, 10)
            yd = Y[:, :, TP:T]
            for br in range(NBR):
                dst = yd if br == 0 else OM[:, :, :]
                o(V.tensor_tensor(dst, OD[br][:, :, :].rearrange("p b h -> p h b"), SZD[:, br, :, :], ALU.mult))
                if br:
                    last = V.tensor_tensor(yd, yd, OM[:, :, :], ALU.add)
                    if br == 1:
                        o(last)
            last.then_inc(ydec, 1)
            y_lo(1)
            dve.wait_ge(s_xb, 16)
            looped(dve, o, 8, resid(1, Q_OB, D_OB))
            rstd(2)
            for k in range(KT):
                dve.wait_ge(tn_ready, 3 * KT + k + 1)
                V.tensor_scalar(X[:, k, :], TN[k % 2][:, :], vec(3, k), None, ALU.mult).then_inc(hf_ready, 1)
            for t in range(5):
                rows = P if t < NT else TS
                for k4 in range(4):
                    n = 4 * t + k4
                    dve.wait_ge(yn_tr, n + 1)
                    if t >= 2 and k4 == 0:
                        dve.wait_ge(yn_out[t % 2], 16 * (t // 2))
                    V.tensor_copy(YN[t % 2][0:rows, 512 * k4:512 * k4 + 512], S[n % 2][0:rows, :]).then_inc(yn_ready, 1)

        @block.tensor
        def _(pe):
            o = Own(pe, own["pe"])
            mm_, tr = nc.tensor.matmul, nc.tensor.transpose

            pe.wait_ge(s_con, 16)
            pe.wait_ge(s_rows, 16 * 7)
            tr(S[0][:, 0:80], VEC[:, :], ident[0:80, 0:80]).then_inc(s_t, 1)
            pe.wait_ge(s_csil, 1)
            for k in range(KT):
                last = tr(S[1][:, NC * k:NC * k + NC], CSIL[:, P * k:P * k + P], ident[0:NC, 0:NC])
            last.then_inc(s_t, 1)
            for t in range(5):
                rows = P if t < NT else TS
                pe.wait_ge(s_x[t % 2], 16 * (t // 2 + 1))
                for k4 in range(4):
                    pe.wait_ge(s_te, 4 * t + k4 + 1)
                    for k in range(4):
                        at = (4 * k4 + k) * P
                        last = tr(S[k4 % 2][:, P * k:P * k + rows], XN[t % 2][0:rows, at:at + P], ident[0:rows, 0:rows])
                    last.then_inc(s_t, 1)
            pe.wait_ge(s_rel, 32)
            pe.wait_ge(s_negrow, 1)
            for n in range(6):
                pe.wait_ge(s_te, 21 + n)
                at = (n // 3) * GLEN + (n % 3) * 512
                w = min(512, GLEN - (n % 3) * 512)
                mm_(S[n % 2][0:NH, 0:w], RELA[:, :], ONEH[:, at:at + w], start=True, stop=True).then_inc(s_t, 1)
            pe.wait_ge(s_te, 28)

            pe.wait_ge(s_cs, 2)

            def ada(l):
                def body(i):
                    for s in range(2):
                        p = 2 * i + s + 24 * l
                        wait(pe, mr_ready, p - 1)
                        for j in range(4):
                            pe.wait_ge(lo_ready, 4 * (Q_ADA + p) + j + 1)
                            for kk in range(4):
                                k = 4 * j + kk
                                mm_(D[s][:, 0:256], CST[:, k, :], HI[j % 2][:, kk, :], start=(k == 0), stop=False)
                                last = mm_(D[s][:, 0:256], CST[:, k, :], LO[j % 2][:, kk, :], start=False, stop=(k == KT - 1))
                            last.then_inc(w_used, 1)
                        pe.wait_ge(mr_ready, p + 1)
                        pe.wait_ge(s_brow[s], 16 * (i + 1 + 12 * l))
                        wait(pe, mt_ready, p - 1)
                        for h in range(2):
                            last = mm_(S[s][:, NC * h:NC * h + NC], MROW[0:19, s, P * h:P * h + P],
                                       CON[0:19, C_SEL19:C_SEL19 + NC], start=True, stop=True)
                        last.then_inc(tr_done, 1)
                return body
            for l in range(2):
                looped(pe, o, 12, ada(l))
            pe.wait_ge(mt_ready, 48)

            def stats(r):
                for k in range(KT):
                    pe.wait_ge(sq_ready, KT * r + k + 1)
                    for half in range(2):
                        last = mm_(S[half][:, 0:HT], ones, SQ[k % 2][:, half * HT:(half + 1) * HT], start=(k == 0), stop=(k == KT - 1))
                    last.then_inc(sq_used, 1)

            def products(out, slot, kk, mm, hi_src, lo_src, k, first, end, n=P):
                cols_ = slice(mm * P, mm * P + n)
                for part, src in ((HI, hi_src), (HI, lo_src), (LO, hi_src)):
                    for half in range(2):
                        last = mm_(out[half][0:n, 0:HT], part[slot][:, kk, cols_], src[:, k, half * HT:(half + 1) * HT],
                                   start=(first and part is HI and src is hi_src), stop=(end and part is LO))
                return last

            def quad(q, d, j, ready=None):
                pe.wait_ge(lo_ready, 4 * q + j + 1)
                if ready is not None:
                    pe.wait_ge(ready[0], ready[1] + 4 * (j + 1))
                for mm in range(2):
                    if j == 0:
                        wait(pe, acc_free, 2 * d + mm - 1)
                    for kk in range(4):
                        last = products(D[2 * mm:2 * mm + 2], j % 2, kk, mm, HH, HL, 4 * j + kk, j == 0 and kk == 0, j == 3 and kk == 3)
                    if mm == 0 and j == 3:
                        last.then_inc(first_done, 1)
                last.then_inc(w_used, 1)

            def pairs(q0, d0, n, ready):
                def body(i):
                    for j in range(4):
                        quad(q0 + i, d0 + i, j, ready if isinstance(i, int) else None)
                looped(pe, o, n, body)

            stats(0)
            pe.wait_ge(mr_ready, 48)
            pairs(Q_U, D_U, 8, (h_ready, 0))
            pe.wait_ge(acc_free, 16)
            pe.wait_ge(rms_ready, 1)
            for k4 in range(4):
                if k4 >= 2:
                    pe.wait_ge(s_ute, k4 - 1)
                for k in range(4):
                    last = tr(S[k4 % 2][0:23, P * k:P * k + P], Y[:, 4 * k4 + k, TP - PB:T], ident)
                last.then_inc(s_ut, 1)
            pe.wait_ge(s_sp, 16)
            for k in range(KT):
                last = mm_(O[:, 8 * k:8 * k + 8], SPN[:, P * k:P * k + P], CON[0:TS * PB, C_SELP + 8 * (k // 4):C_SELP + 8 * (k // 4) + 8],
                           start=True, stop=True)
            last.then_inc(s_ps, 1)
            for g in range(4):
                pe.wait_ge(s_pl, g + 1)
                for c in range(2):
                    n = 2 * g + c
                    slot = n % 2
                    pe.wait_ge(lo_ready, 4 * Q_MIX + n + 1)
                    for mm in range(2):
                        pe.wait_ge(acc_free, 2 * (D_MIX + n) + mm - 1)
                        for kk in range(4):
                            last = products(D[2 * mm:2 * mm + 2], slot, kk, mm, PHI, PLO, kk, kk == 0, kk == 3)
                        if mm == 0:
                            last.then_inc(first_done, 1)
                    last.then_inc(w_used, 1)

            def z_pairs(i):
                for j in range(4):
                    q = Q_Z + i
                    pe.wait_ge(lo_ready, 4 * q + j + 1)
                    for mm in range(2):
                        if j == 0:
                            if isinstance(i, int):
                                pe.wait_ge(acc_free, 2 * D_OA + mm - 1)
                            else:
                                pe.wait_ge(zt_ready, 2 * i + mm - 1)
                        for kk in range(4):
                            last = products(D[2 * mm:2 * mm + 2], j % 2, kk, mm, HH, HL, 4 * j + kk, j == 0 and kk == 0, j == 3 and kk == 3)
                        if mm == 0 and j == 3:
                            last.then_inc(z_first, 1)
                    last.then_inc(w_used, 1)
            looped(pe, o, 8, z_pairs)
            pe.wait_ge(zt_ready, 16)

            pairs(Q_OA, D_OA, 8, (ys, 0))
            stats(1)
            for i, src in enumerate((KCF, VCF, KS, VF, KW, VF)):
                pairs(Q_KV + 2 * i, D_KV + 2 * i, 2, (h_ready, KT) if i == 0 else None)
                pe.wait_ge(acc_free, 2 * (D_KV + 2 * i + 2))
                if i == 0:
                    pe.wait_ge(rms_ready, 2)
                for t in range(5):
                    rows = P if t < NT else TS
                    n = 5 * i + t
                    if n >= 2:
                        pe.wait_ge(tm_ready, n - 1)
                    for g in range(NKV):
                        last = tr(S[n % 2][0:rows, P * g:P * g + P], src[:, g, t * P:t * P + rows], ident)
                    last.then_inc(kv_tr, 1)

            pe.wait_ge(s_cw, 16 * 6)
            pe.wait_ge(tm_ready, 30)
            for kv in range(2):
                tr(S[kv][:, 0:CL], PE_[kv][:, :], ident[0:CL, 0:CL]).then_inc(s_pe, 1)
            for kv in range(2):
                pe.wait_ge(s_pee, kv + 1)
                for l in range(CL):
                    last = mm_(O[:, kv:kv + 1], W1[kv][:, l, :], PET[kv][:, l:l + 1], start=(l == 0), stop=(l == CL - 1))
            last.then_inc(s_pe, 1)
            pe.wait_ge(s_pee, 3)

            def turn_pages(n, slot, base=0):
                for g in range(NKV):
                    wait(pe, ctre, 4 * n + g - 1 + base)
                    for t in range(NPG):
                        last = tr(S[g % 2][:, P * t:P * t + P], PG[slot][:, t, P * g:P * g + P], ident)
                    last.then_inc(ctr, 1)

            def hidden(n, kv, src, peeled=False):
                wait(pe, csr, n)
                for l in range(CL):
                    at = [src[:, :, l:l + 16 * (NCMP - 1) + 1:16]]
                    last = mm_(S[2][:, 0:NKV * NCMP], W1[kv][:, l, :], at[0], start=(l == 0), stop=(l == CL - 1))
                last.then_inc(cw1, 1)

            def second(n, kv, prompt=False):
                pe.wait_ge(csr, n + 1)
                wait(pe, cout, n)
                if kv == 0:
                    last = mm_(O[:, 0:NKV * NCMP], W2[0][:, :], CSIL2[0][:, :], start=True, stop=True)
                elif not prompt:
                    last = mm_(O[0:NKV * NCMP, 0:P], CSIL2[1][:, :], W2[1][:, :], start=True, stop=True)
                else:
                    for g in range(NKV):
                        last = mm_(O[0:NCMP, P * g:P * g + P], CSIL2[1][:, NCMP * g:NCMP * g + NCMP], W2[1][:, :], start=True, stop=True)
                last.then_inc(cw2, 1)

            def compress(b):
                for kv in range(2):
                    n = 2 * b + kv
                    pe.wait_ge(s_pg[kv], 64 * (b + 1))
                    turn_pages(n, kv)
                    pe.wait_ge(ctre, 4 * n + 4)
                    hidden(n, kv, RT_T[kv])
                    second(n, kv)
            looped(pe, o, TS, compress)
            for kv in range(2):
                hidden(16 + kv, kv, KCF if kv == 0 else VCF)
                second(16 + kv, kv, True)

            for j in range(4):
                pe.wait_ge(lo_ready, 4 * Q_G + j + 1)
                pe.wait_ge(h_ready, 2 * KT + 4 * (j + 1))
                for kk in range(4):
                    last = products(D[0:2], j % 2, kk, 0, HH, HL, 4 * j + kk, j == 0 and kk == 0, j == 3 and kk == 3)
                    if j == 3 and kk == 2:
                        last.then_inc(first_done, 1)
                last.then_inc(w_used, 1)
            pe.wait_ge(acc_free, 2 * (D_G + 1))
            pe.wait_ge(cout, 18)
            for t in range(NT):
                last = tr(S[0][:, 48 * t:48 * t + 48], GF[:, P * t:P * t + P], ident[0:48, 0:48])
            last.then_inc(g_tr, 1)
            pe.wait_ge(gt_ready, 1)

            def scores(i, u):
                n, br, hh = 6 * i + u, u // 2, u % 2
                g = i // 2
                if u == 0:
                    pe.wait_ge(acc_free, 2 * (D_H + 4 * i + 1))
                    pe.wait_ge(hd_in, 80 * (i + 1))
                wait(pe, pt_ready, n)
                qs = lambda t: QS[:, hh, P * t:P * t + P]
                if br == 0:
                    at = g * NCMP
                    kc = KCP[:, bass.ds(at, NCMP)] if not isinstance(at, int) else KCP[:, at:at + NCMP]
                    for t in range(NT):
                        out = S[0][:, NCMP * t:NCMP * t + NCMP]
                        mm_(out, BC[:, hh, P * t:P * t + P], ident[0:NCMP, 0:NCMP], start=True, stop=False)
                        last = mm_(out, qs(t), kc, start=False, stop=True)
                else:
                    kt_ = KS if br == 1 else KW
                    kt_ = dyn(kt_, g)
                    where = (S[1][:, 384:512], S[2][:, 0:256], S[1][:, 0:384], S[0][:, :])
                    for t in (3, 2, 1, 0):
                        last = mm_(where[t], qs(t), kt_[:, :, 0:P * (t + 1)].rearrange("p o t -> p (o t)"), start=True, stop=True)
                last.then_inc(a_done, 1)

            W_AT = [0, 1, 3, 6]

            def turn(i, u):
                n = 6 * i + u
                pe.wait_ge(p_ready, n + 1)
                if u < 2:
                    for t in range(NT):
                        last = tr(S[0][0:NCMP, P * t:P * t + P], PR[:, NCMP * t:NCMP * t + NCMP], ident)
                else:
                    for b, at, j in ((0, 0, 0), (1, 0, 1), (1, 3, 3), (2, 0, 2)):
                        for t in range(j, NT):
                            c = (at + t - j) * P
                            src = (W_AT[t] + j) * P
                            last = tr(S[b][:, c:c + P], PR[:, src:src + P], ident)
                last.then_inc(b_done, 1)

            def values(i, u):
                n, br = 6 * i + u, u // 2
                pe.wait_ge(pt_ready, n + 1)
                wait(pe, o_used, n)
                if br == 0:
                    last = mm_(O[:, :], VCG[:, :], PT[0:NCMP, 0:512], start=True, stop=True)
                else:
                    for j, at in ((0, 0), (1, 512), (2, 1024), (3, 512 + 384)):
                        last = mm_(O[:, P * j:512], VG[:, br - 1, j, :], PT[:, at:at + 512 - P * j], start=(j == 0), stop=(j == 3),
                                   skip_group_check=True)
                last.then_inc(c_done, 1)

            def heads(i):
                for s in range(16):
                    quad(Q_H + 4 * i + s // 4, D_H + 4 * i + s // 4, s % 4)
                    if s >= 6 and s % 2 == 0:
                        values(i, (s - 6) // 2)
                    if s >= 4 and s % 2 == 0:
                        u = (s - 4) // 2
                        if u < 6:
                            turn(i, u)
                    if s >= 3 and s % 2 == 1:
                        u = (s - 3) // 2
                        if u < 6:
                            scores(i, u)
                values(i, 5)
            looped(pe, o, 8, heads)

            pe.wait_ge(s_dm, 1)
            pe.wait_ge(acc_free, 2 * D_OB)
            for b in range(4):
                last = mm_(D[b][:, :], ZERO[:, :], Y[:, 0, 0:512], start=True, stop=(b < 0), skip_group_check=True)
            last.then_inc(dsc, 2)
            for br in range(2):
                def keys(i, br=br):
                    for s in range(2):
                        b = 2 * i + s
                        m = 8 * br + b
                        pe.wait_ge(s_pg[s], (512 + 64 * (i + 1)) if br == 0 else (768 + 16 * (i + 1)))
                        turn_pages(m, s, 64)
                        pe.wait_ge(qp_ready, m + 1)
                        pe.wait_ge(ctre, 64 + 4 * m + 4)
                        pe.wait_ge(kst, m + 1)
                        for g in range(NKV):
                            r = slice(32 * g, 32 * g + 32)
                            q = QPAD[s][:, g, :]
                            mm_(D[br][r, :], q, RT_T[s][:, g, :], start=False, stop=False, skip_group_check=True)
                            last = mm_(D[2][r, br:br + 1], q, KN[s][:, g:g + 1], start=False, stop=False, skip_group_check=True)
                            if br == 0:
                                last = mm_(D[3][r, 0:NCMP], q, KCB[s][:, NCMP * g:NCMP * g + NCMP], start=False, stop=False, skip_group_check=True)
                        last.then_inc(dsc, 1)
                looped(pe, o, 4, keys)
            for b in range(4):
                last = mm_(D[b][:, :], ZERO[:, :], Y[:, 0, 0:512], start=False, stop=True, skip_group_check=True)
            last.then_inc(sd_pe, 1)
            pe.wait_ge(sd_ev, 1)
            tr(S[0][0:NKV * NCMP, 0:P], PX[:, :], ident).then_inc(sd_pe, 1)
            pe.wait_ge(sd_ev, 2)
            mm_(S[1][:, 0:9], PTC[:, :], CON[0:NKV * NCMP, C_OVL:C_OVL + 9], start=True, stop=True).then_inc(sd_pe, 1)
            pe.wait_ge(sd_ev, 3)
            tr(S[0][0:NKV * NCMP, P:2 * P], PX[:, :], ident).then_inc(sd_pe, 1)
            pe.wait_ge(sd_ev, 4)
            mm_(S[2][:, 0:9], CON[:, C_RSUM:C_RSUM + P], IMP[:, :], start=True, stop=True).then_inc(sd_pe, 1)
            for br in range(2):
                pe.wait_ge(sd_ev, 6 + br)
                for t in range(NPG):
                    tr(S[br][:, P * t:P * t + P], SD[br][:, P * t:P * t + P], ident)
                tr(S[2][0:1, P * br:P * br + P], SD[br][:, 512:513], ident).then_inc(sd_pe, 1)
            for b in range(TS):
                last = mm_(O[:, NH * b:NH * b + NH], VCS[:, b, :], PTG[:, :].rearrange("p (g n) -> p g n", g=NKV)[:, :, 4 * b:4 * b + 4],
                           start=True, stop=True)
            last.then_inc(sd_pe, 1)
            pe.wait_ge(sd_ev, 9)
            for br in range(2):
                def vals(i, br=br):
                    for s in range(2):
                        b = 2 * i + s
                        m = 8 * br + b
                        pe.wait_ge(s_pg[s], (832 + 64 * (i + 1)) if br == 0 else (1088 + 16 * (i + 1)))
                        pe.wait_ge(s_vn[s], 16 * (4 * br + i + 1))
                        wait(pe, pve, m - 1)
                        for g in range(NKV):
                            out = S[s][:, 4 * g:4 * g + 4]
                            at = b * 4 + 32 * g
                            for t in range(NPG):
                                rhs = PTD[br][:, t, bass.ds(at, 4)] if not isinstance(at, int) else PTD[br][:, t, at:at + 4]
                                mm_(out, PG[s][:, t, P * g:P * g + P], rhs, start=(t == 0), stop=False)
                            rhs = PTN[:, br, bass.ds(at, 4)] if not isinstance(at, int) else PTN[:, br, at:at + 4]
                            last = mm_(out, VN[s][:, P * g:P * g + P], rhs, start=False, stop=True)
                        last.then_inc(pv, 1)
                looped(pe, o, 4, vals)

            pairs(Q_OB, D_OB, 8, (ys, KT))
            stats(2)
            pe.wait_ge(rms_ready, 3)
            pe.wait_ge(hf_ready, 4 * KT)
            for t in range(5):
                rows = P if t < NT else TS
                for k4 in range(4):
                    n = 4 * t + k4
                    if n >= 2:
                        pe.wait_ge(yn_ready, n - 1)
                    for k in range(4):
                        last = tr(S[n % 2][0:rows, P * k:P * k + P], X[:, 4 * k4 + k, t * P:t * P + rows], ident)
                    last.then_inc(yn_tr, 1)


_OUTS = [(1, 512, 2048), (8, 1, 2048), (1, 1, 15, 2048)] + [(1, 512, 4, 128)] * 6 + \
    [(1, 8, 15, 2048)] + [(8, 1, 4, 128)] * 4 + [(8, 512, 4, 128)] * 2


def kernel(**inputs):
    import concourse.bacc as bacc
    from concourse.bass_utils import run_bass_kernel_spmd

    nc = bacc.Bacc("TRN2", target_bir_lowering=False, num_devices=1)
    arrays = {n: np.ascontiguousarray(a) for n, a in inputs.items()}
    arrays["consts"] = shape_constants()
    arrays["onehots"] = bucket_onehots()
    ins = {n: nc.dram_tensor(f"in_{n}", a.shape, mybir.dt.from_np(a.dtype), kind="ExternalInput").ap() for n, a in arrays.items()}
    outs = [nc.dram_tensor(f"out_{i}", s, F32, kind="ExternalOutput").ap() for i, s in enumerate(_OUTS)]
    build(nc, ins, outs)
    r = run_bass_kernel_spmd(nc, [{f"in_{n}": a for n, a in arrays.items()}], core_ids=[0])
    return tuple(r.results[0][f"out_{i}"] for i in range(len(_OUTS)))
```

```python
from contextlib import ExitStack

import numpy as np
import concourse.bass as bass
from concourse import mybir

F32 = mybir.dt.float32
F32R = mybir.dt.float32r
I32 = mybir.dt.int32
ALU = mybir.AluOpType
ACT = mybir.ActivationFunctionType
AX = mybir.AxisListType

P = 128
DM = 2048
KT = DM // P
TP, TS = 512, 8
T = TP + TS
HT = T // 2
NT = TP // P
ML = 48
NC = 9
NH, NKV, REP, HD = 16, 4, 4, 128
NBR = 3
PB = 15
WINDOWS = (2, 4, 8, 16)
NCMP = 31
CL, CS_ = 32, 16
NPG = 4
GLEN = 1025
SCALE = float(HD) ** -0.5
EPS = 1e-6
NEG = -1e30

C_ID, C_ONE, C_RSUM, C_CNT, C_SELP, C_SEL19, C_OVL, C_IOTA, C_VIS, C_EPS, C_MSK = 0, 128, 256, 384, 448, 480, 489, 498, 505, 506, 507
NCONST = 507 + 64


def shape_constants():
    c = np.zeros((P, NCONST), np.float32)
    c[:, C_ID:C_ID + P] = np.eye(P)
    c[:, C_ONE:C_ONE + P] = 1.0
    row = np.arange(P)
    same = (row[:, None] // 4) == (row[None, :] // 4)
    c[:, C_RSUM:C_RSUM + P] = same
    for g, w in enumerate(WINDOWS):
        c[:, C_CNT + 16 * g:C_CNT + 16 * g + 16] = 1.0 / np.minimum(np.arange(16) + 1, w)
        for b in range(TS):
            for t in range(PB):
                c[b * PB + t, C_SELP + 8 * g + b] = float(t >= PB + 1 - w)
    for j in range(NC):
        c[j, C_SEL19 + j] = c[NC + j, C_SEL19 + j] = 1.0
    c[2 * NC, C_SEL19:C_SEL19 + NC] = 1.0
    for g in range(NKV):
        for n in range(NCMP):
            for j in range(9):
                o = min(16 * n + 32, 64 * j + 64) - max(16 * n, 64 * j)
                c[g * NCMP + n, C_OVL + j] = max(o, 0) / CL
    c[:, C_IOTA:C_IOTA + 7] = np.arange(1, 8)
    c[:, C_VIS] = row >= CL - 1
    c[:, C_EPS] = EPS
    c[:, C_MSK:C_MSK + 64] = np.eye(8).reshape(1, 64)
    return c


def bucket_onehots():
    d = np.arange(512, -513, -1)
    df = np.maximum(d, 16).astype(np.float32)
    large = 16 + (np.log(df / np.float32(16)) / np.float32(np.log(128 / 16)) * np.float32(16)).astype(np.int32)
    bucket = np.where(d < 16, np.maximum(d, 0), np.minimum(large, 31))
    bucket = np.where(d < 0, 32, bucket)
    fall = (np.arange(33)[:, None] == bucket[None, :]).astype(np.float32)
    return np.concatenate([fall, fall[:, ::-1]], axis=1)


def wait(eng, sem, value):
    if not (isinstance(value, int) and value <= 0):
        eng.wait_ge(sem, value)


class Own:

    def __init__(self, eng, sem):
        self.eng, self.sem, self.base, self.n = eng, sem, 0, 0

    def __call__(self, ins):
        self.n += 1
        ins.then_inc(self.sem, 1)
        self.eng.wait_ge(self.sem, self.base + self.n)

    def turn(self, i, body):
        if isinstance(i, int) and i == 0:
            self.start = self.base + self.n
            self.base, self.n = self.start, 0
            body(i)
            self.per = self.n
            self.base, self.n = self.start + self.per, 0
        else:
            self.base, self.n = self.start + i * self.per, 0
            body(i)
            assert self.n == self.per

    def ended(self, turns):
        self.base, self.n = self.start + turns * self.per, 0


def looped(eng, own, turns, body, head=1, tail=0):
    for i in range(head):
        own.turn(i, body)
    if turns > head + tail:
        with eng.Fori(head, turns - tail) as i:
            own.turn(i, body)
    for i in range(turns - tail, turns):
        own.turn(i, body)
    own.ended(turns)


Q_ADA, Q_U, Q_Z, Q_MIX, Q_OA, Q_KV, Q_G, Q_H, Q_OB = 0, 48, 56, 64, 66, 74, 86, 87, 119
D_U, D_Z, D_MIX, D_OA, D_KV, D_G, D_H, D_OB = 0, 8, 16, 24, 32, 44, 45, 77
Q_END = 127


def ahead(q):
    return [(q, 1), (q, 2), (q, 3), (q + 1, 0)]


def build(nc, ins, outs):
    A = ins
    (y_prompt, y_sample, pool_p, k_cmp_p, v_cmp_p, k_slc_p, v_slc_p, k_win_p, v_win_p,
     pool_s, k_cmp_s, v_cmp_s, k_slc_s, v_slc_s, k_win_s, v_win_s) = outs

    with ExitStack() as ctx:
        def sem(name):
            return ctx.enter_context(nc.semaphore(name))

        def dram(name, shape):
            return nc.dram_tensor(name, shape, F32, kind="Internal").ap()

        BASE = 16512
        cursor = [BASE]

        def place(name, shape, dt=F32):
            n = int(np.prod(shape[1:])) * 4
            t = nc.alloc_sbuf_tensor_at(name, list(shape), dt, offset=cursor[0])
            cursor[0] += (n + 31) // 32 * 32
            return t

        RAW = [place(f"raw{i}", [P, 4, 256]) for i in range(4)]
        HI = [place(f"w_hi{i}", [P, 4, 256], F32R) for i in range(2)]
        LO = [place(f"w_lo{i}", [P, 4, 256], F32R) for i in range(2)]
        CON = place("consts", [P, NCONST])
        MODT = place("modT", [P, 2 * ML, NC])
        AMOD = place("a_mod", [P, 2, KT, NC])
        VECT = place("vecT", [P, 80])
        PTAB = place("page_tab", [1, 32], I32)
        h_at = cursor[0]
        HH = place("h_hi", [P, KT, T], F32R)
        HL = place("h_lo", [P, KT, T], F32R)
        h_end = y_at = cursor[0]
        Y = place("y", [P, KT, T])
        x_at = cursor[0]
        X = place("x", [P, KT, T])
        c_at = cursor[0]
        END = 229368

        cursor[0] = h_at
        CROW = place("c_rows", [NC, DM])
        CSIL = place("c_silu", [NC, DM])
        XN = [place(f"x_nat{i}", [P, DM]) for i in range(2)]
        VEC = place("vec_rows", [80, P])
        RELA = place("rel_rows", [33, NH])
        ONEH = place("onehots", [33, 2 * GLEN])
        GROW = place("bias_rows", [NH, 2 * GLEN])
        assert cursor[0] <= h_end
        cursor[0] = y_at
        CST = place("c_split", [P, KT, P], F32R)
        CTF = place("c_cols", [P, KT, NC])
        MROW = place("mod_rows", [19, 2, 256])
        RAW += [place(f"raw{i}", [P, 4, 256]) for i in range(4, 8)]
        assert cursor[0] <= x_at
        cursor[0] = c_at
        HI += [place(f"w_hi{i}", [P, 4, 256], F32R) for i in range(2, 4)]
        LO += [place(f"w_lo{i}", [P, 4, 256], F32R) for i in range(2, 4)]
        cursor[0] = c_at
        SQ = [place(f"squares{i}", [P, T]) for i in range(2)]
        TN = [place(f"normed{i}", [P, T]) for i in range(2)]
        HF = [place(f"h_full{i}", [P, T]) for i in range(3)]
        RMS = nc.alloc_sbuf_tensor_at("rms", [P, T], F32, offset=cursor[0] - T * 4)
        c_norm_end = cursor[0]
        RSTD = nc.alloc_sbuf_tensor_at("rstd", [P, T], F32, offset=(END - 2112) // 32 * 32)
        c_top = (END - 2112) // 32 * 32
        assert cursor[0] <= c_top
        cursor[0] = c_at
        PHI = [place("pooled_hi0", [P, 4, T], F32R)]
        PLO = [place("pooled_lo0", [P, 4, T], F32R)]
        PHI += [place("pooled_hi1", [P, 4, T], F32R)]
        PLO += [place("pooled_lo1", [P, 4, T], F32R)]
        assert cursor[0] <= END, cursor[0]
        cursor[0] = c_at + 2 * 4 * T * 4
        SPN = place("state_rows", [TS * PB, DM])
        PAD = [place(f"window_sum{i}", [P, 16 + TP]) for i in range(2)]
        STMP = place("sample_tmp", [P, 4, TS])
        assert cursor[0] <= END, cursor[0]
        UT = nc.alloc_sbuf_tensor_at("u_rows", [23, DM], F32, offset=c_at)
        cursor[0] = c_at
        cursor[0] = c_at + 2 * T * 4
        RT = [place(f"resid_tmp{i}", [P, TS]) for i in range(2)]
        ZS = nc.alloc_sbuf_tensor_at("z_pool", [P, KT, T], F32, offset=x_at)
        cursor[0] = c_norm_end
        KS = place("k_slc_T", [P, NKV, T])
        KW = place("k_win_T", [P, NKV, T])
        KCP = place("kc_prompt_T", [P, NKV * NCMP])
        KCS = place("kc_sample_T", [P, TS, NKV * NCMP])
        assert cursor[0] <= c_top, (cursor[0], c_top)
        keep_end = cursor[0]
        VCS = nc.alloc_sbuf_tensor_at("vc_sample", [NKV * NCMP, TS, P], F32, offset=c_at)
        cursor[0] = y_at
        KCF = place("k_cmp_T", [P, NKV, T])
        VCF = place("v_cmp_T", [P, NKV, T])
        VF = place("v_T", [P, NKV, T])
        TM = [place(f"token_rows{i}", [P, 512]) for i in range(4)]
        assert cursor[0] <= x_at
        cursor[0] = h_at
        W1 = [place(f"w_c1_{i}", [P, CL, P]) for i in range(2)]
        PG = [place(f"pages{i}", [P, NPG, 512]) for i in range(2)]
        RT_T = [place(f"rows_T{i}", [P, NKV, TP]) for i in range(2)]
        CSIL2 = [place(f"c_hidden{i}", [P, NKV * NCMP]) for i in range(2)]
        assert cursor[0] <= h_end, (cursor[0], h_end)
        cursor[0] = y_at + 2 * NKV * T * 4
        W2 = [place(f"w_c2_{i}", [P, P]) for i in range(2)]
        PE_ = [place(f"pe{i}", [CL, P]) for i in range(2)]
        PET = [place(f"pe_T{i}", [P, CL]) for i in range(2)]
        PEC = place("pe_term", [P, 2])
        VCP = place("vc_prompt", [NCMP, NKV, P])
        assert cursor[0] <= y_at + 3 * NKV * T * 4 + 0
        cursor[0] = x_at
        PR = place("probs", [P, 1280])
        PT = place("probs_T", [P, 1280])
        VG = place("v_group", [P, 2, NT, P])
        BH = place("bias_heads", [P, 2, 512])
        ZB = place("z_silu", [P, NBR, 2, T])
        TMP = place("o_times_z", [P, TP])
        assert cursor[0] <= c_at
        cursor[0] = c_at + TS * P * 4
        QS = place("q_heads", [P, 2, TP])
        BC = place("bias_cmp", [NCMP, 2, TP])
        VCG = place("vc_group", [NCMP, P])
        GT = place("gate_rows", [P, NT, 48])
        assert cursor[0] <= c_norm_end, (cursor[0], c_norm_end)
        cursor[0] = keep_end
        SZD = place("z_silu_sample", [P, NBR, NH, TS])
        QD = place("q_sample", [P, NH, TS])
        STAT = place("row_stats", [P, 16])
        GF = nc.alloc_sbuf_tensor_at("gates_T", [48, T], F32, offset=y_at)
        assert cursor[0] <= END, cursor[0]
        cursor[0] = h_at
        cursor[0] = h_at
        QPAD = [place(f"q_one_sample{i}", [P, NKV, 32]) for i in range(2)]
        KN = [place(f"k_new{i}", [P, NKV]) for i in range(2)]
        KCB = [place(f"kc_one_sample{i}", [P, NKV * NCMP]) for i in range(2)]
        PTD = [place(f"probs_T_sample{i}", [P, NPG, P]) for i in range(2)]
        PTN = place("probs_T_new", [1, 2, P])
        PTC = place("probs_T_cmp", [NKV * NCMP, P])
        PTG = place("probs_T_cmp_gated", [NKV * NCMP, P])
        SD = [place(f"scores_sample{i}", [P, 513]) for i in range(2)]
        SC = place("scores_cmp", [P, NCMP])
        PX = place("probs_cmp_spread", [P, NKV * NCMP])
        BD = place("bias_sample", [P, 513])
        BCD = place("bias_cmp_sample", [P, NCMP])
        IMP = place("importance", [P, 9])
        DRP = place("dropped", [P, 3, 7])
        GD = place("gates_sample", [P, NBR])
        SST = place("sample_stats", [P, 16])
        VN = [place(f"v_new{i}", [1, 512]) for i in range(2)]
        OD = [place(f"o_sample{i}", [P, TS, NH]) for i in range(NBR)]
        OM = place("o_sample_tmp", [P, NH, TS])
        ZERO = place("zeros", [P, P])
        assert cursor[0] <= h_at + 2 * CL * P * 4, cursor[0] - h_at
        cursor[0] = x_at
        PG += [place(f"pages{i}", [P, NPG, 512]) for i in range(2, 4)]
        cursor[0] = y_at
        YN = [place(f"y_rows{i}", [P, DM]) for i in range(2)]

        def bank(name):
            return ctx.enter_context(nc.psum_tensor(name, [P, 512], F32))

        D = [bank(f"acc{i}") for i in range(4)]
        S = [bank(f"work{i}") for i in range(3)]
        O = bank("out_acc")

        g_scr = dram("g_scr", (NH, 2 * GLEN))
        b_scr = dram("b_scr", (NH, P, 512))
        c_scr = dram("c_scr", (NH, NCMP, TP))
        x_scr = dram("x_scr", (P, KT * T))
        vc_scr = dram("vc_scr", (NCMP, NKV * P))
        gd_scr = dram("gd_scr", (NBR, P))

        ident = CON[:, C_ID:C_ID + P]
        ones = CON[:, C_ONE:C_ONE + P]

        raw_full = [sem(f"raw_full{i}") for i in range(8)]
        hi_ready = sem("hi_ready")
        lo_ready = sem("lo_ready")
        w_used = sem("w_used")
        first_done = sem("first_tile_done")
        acc_free = sem("acc_free")
        own = {e: sem(f"own_{e}") for e in ("act", "dve", "pool", "pe")}
        s_con = sem("consts_in")
        s_rows = sem("setup_rows_in")
        s_x = [sem(f"x_rows_in{i}") for i in range(2)]
        s_rel = sem("rel_in")
        s_negrow = sem("neg_row")
        s_t = sem("setup_transposed")
        s_te = sem("setup_copied")
        s_csil = sem("c_silu_done")
        s_cz = sem("c_split_zero")
        s_cs = sem("c_split_done")
        s_gscr = sem("bias_rows_out")
        s_bscr = sem("bias_tables_out")
        mr_ready = sem("mod_rows_ready")
        s_brow = [sem(f"b_row_in{i}") for i in range(2)]
        tr_done = sem("mod_turned")
        mt_ready = sem("mod_ready")
        amod = sem("a_mod_ready")
        sq_ready = sem("square_ready")
        sq_used = sem("square_used")
        rms_ready = sem("rms_ready")
        rstd_ready = sem("rstd_ready")
        tn_ready = sem("normed_ready")
        hf_ready = sem("h_full_ready")
        hfs_ready = sem("h_full_samples_ready")
        hhi_ready = sem("h_hi_ready")
        h_ready = sem("h_ready")
        s_sp = sem("state_rows_in")
        s_ut = sem("u_turned")
        s_ute = sem("u_rows_ready")
        s_uo = sem("u_rows_out")
        s_ps = sem("prefix_sums")
        s_pooled = sem("pooled_ready")
        s_pooled_s = sem("pooled_samples_ready")
        s_x0 = sem("x_first_out")
        s_x1 = sem("x_first_back")
        s_ph = sem("pooled_hi_ready")
        s_pl = sem("pooled_split")
        kv_copied = sem("kv_tiles_copied")
        kv_tr = sem("kv_turned")
        tm_ready = sem("token_rows_ready")
        tm_out = [sem(f"token_rows_out{i}") for i in range(4)]
        s_copy = sem("states_copied")
        s_cw = sem("small_compress_weights_in")
        s_cw1 = sem("compress_weights_in")
        s_pt = sem("page_table_in")
        s_pe = sem("pe_turned")
        s_pee = sem("pe_copied")
        s_pg = [sem(f"pages_in{i}") for i in range(4)]
        ctr = sem("pages_turned")
        ctre = [sem(f"pages_turned_copied{i}") for i in range(2)]
        cw1 = sem("hidden_done")
        csr = sem("hidden_silu_done")
        cw2 = sem("compressed_done")
        cout = sem("compressed_copied")
        s_vcp = sem("vc_prompt_out")
        s_xs = sem("x_spilled")
        g_tr = sem("gates_turned")
        gt_ready = sem("gate_rows_ready")
        s_gd = sem("gates_sample_out")
        hd_in = sem("head_data_in")
        q_ready = sem("q_ready")
        z_ready = sem("z_ready")
        a_done = sem("scores_done")
        negm = sem("max_ready")
        e_done = sem("exp_done")
        r_ready = sem("row_factor_ready")
        p_ready = sem("probs_ready")
        b_done = sem("probs_turned")
        pt_ready = sem("probs_T_ready")
        c_done = sem("values_done")
        o_used = sem("values_used")
        s_dm = sem("sample_consts_ready")
        s_bd = sem("sample_bias_in")
        qp_ready = sem("q_one_sample_ready")
        kst = sem("sample_keys_staged")
        dsc = sem("sample_scores_done")
        sd_step = sem("sample_softmax_step")
        sd_exp = sem("sample_exp")
        sd_pe = sem("sample_pe_step")
        sd_ev = sem("sample_copied")
        s_vn = [sem(f"v_new_in{i}") for i in range(2)]
        pv = sem("sample_values_done")
        pve = sem("sample_values_copied")
        ydec = sem("y_sample_ready")
        ys_hi = sem("y_hi_ready")
        ys = sem("y_split")
        s_xb = sem("x_back")
        yn_tr = sem("y_turned")
        yn_ready = sem("y_rows_ready")
        yn_out = [sem(f"y_rows_out{i}") for i in range(2)]

        def vec(v, k):
            return VECT[:, v * KT + k:v * KT + k + 1]

        def halves(ap):
            return [ap[:, 0:HT], ap[:, HT:T]]

        def dyn(t, i, n=1):
            return t[:, bass.ds(i, n)] if not isinstance(i, int) else t[:, i:i + n]

        def flat(ap):
            return ap.rearrange("p a n -> p (a n)")

        def cols(w, j, at, n=256):
            w = w.rearrange("(k p) n -> p k n", p=P)[:, 4 * j:4 * j + 4]
            return w[:, :, bass.ds(at, n)] if not isinstance(at, int) else w[:, :, at:at + n]

        w_a, w_oa, w_kv, w_b, w_ob = A["w_in_a"][0], A["w_out_a"][0], A["w_kv"], A["w_in_b"][0], A["w_out_b"][0]
        kv_out_p = [x[0].rearrange("t g d -> t (g d)") for x in (k_cmp_p, v_cmp_p, k_slc_p, v_slc_p, k_win_p, v_win_p)]
        kv_out_s = [x[:, x.shape[1] - 1].rearrange("b g d -> b (g d)") for x in (k_cmp_s, v_cmp_s, k_slc_s, v_slc_s, k_win_s, v_win_s)]

        block = ctx.enter_context(nc.Block())

        @block.sync
        def _(sp):
            o = Own(sp, own["pe"])

            def load(q, j, src, n=256):
                wait(sp, lo_ready, 4 * q + j - 3)
                sp.dma_start(RAW[j][:, :, 0:n], src).then_inc(raw_full[j], 16)

            def quads(q0, w, n, at=lambda i: i * 256, first=0):
                def body(i):
                    if not (isinstance(i, int) and i < first):
                        for j in range(4):
                            load(q0 + i, j, cols(w, j, at(i)))
                looped(sp, o, n, body)

            for l in range(2):
                def ada(i, l=l):
                    for s in range(2):
                        for j in range(4):
                            wait(sp, lo_ready, 4 * (2 * i + s + 24 * l) + j - 7)
                            sp.dma_start(RAW[4 * s + j][:, :, :], cols(A["w_ada"][l], j, (2 * i + s) * 256)).then_inc(raw_full[4 * s + j], 16)
                looped(sp, o, 12, ada)
            quads(Q_U, w_a, 8)
            quads(Q_Z, w_a, 8, lambda i: DM + i * 256)
            for g in range(4):
                for c in range(2):
                    load(Q_MIX + g // 2, 2 * (g % 2) + c, cols(A["w_grp"][0][g], 0, 256 * c))
            quads(Q_OA, w_oa, 8)
            quads(Q_KV, w_kv, 12)
            for j in range(4):
                load(Q_G, j, cols(w_b, j, 4 * DM, 48), 48)

            sp.wait_ge(w_used, 4 * Q_G)
            for i, n in enumerate("kv"):
                sp.dma_start(W1[i][:, :, :], A[f"w_c{n}1"].rearrange("(l p) n -> p l n", p=P)).then_inc(s_cw1, 16)
            sp.wait_ge(s_pt, 16)

            def page_loads(i, b, free, value, cache):
                page = [sp.value_load(PTAB[0:1, bass.ds(b * NPG + t, 1)], min_val=0, max_val=cache.shape[0] - 1) for t in range(NPG)]
                wait(sp, free, value)
                for t in range(NPG):
                    sp.dma_start(PG[i][:, t, :], cache[bass.ds(page[t], 1)].rearrange("o t g d -> (o t) (g d)")).then_inc(s_pg[i], 16)

            def pages(b):
                for kv, cache in enumerate((A["cache_k_cmp"], A["cache_v_cmp"])):
                    page_loads(kv, b, ctr, 4 * (2 * b + kv) - 4, cache)
            looped(sp, o, TS, pages)

            def heads(i):
                for blk in range(4):
                    for j in range(4):
                        load(Q_H + 4 * i + blk, j, cols(w_b, j, blk * DM + i * 256))
            looped(sp, o, 8, heads)
            for j in range(4):
                load(Q_OB, j, cols(w_ob, j, 0))

            sp.wait_ge(w_used, 4 * Q_OB)
            sp.wait_ge(c_done, 48)

            def state_load(i, b, state):
                src = state.rearrange("b (t p) g d -> b p t (g d)", p=P)
                src = src[bass.ds(b, 1)] if not isinstance(b, int) else src[b:b + 1]
                sp.dma_start(PG[i][:, :, :], src.rearrange("o p t n -> (o p) t n")).then_inc(s_pg[i], 16)

            for br in range(2):
                def keys(i, br=br):
                    for s in range(4):
                        b = 4 * i + s
                        free = 64 + 4 * (8 * br + b) - 12
                        if br == 0:
                            page_loads(s, b, ctr, free, A["cache_k_slc"])
                        else:
                            sp.wait_ge(ctr, free)
                            state_load(s, b, A["state_k_win"])
                looped(sp, o, 2, keys)
            for br in range(2):
                def vals(i, br=br):
                    for s in range(4):
                        b = 4 * i + s
                        m = 8 * br + b
                        if isinstance(m, int) and m < 4:
                            sp.wait_ge(ctr, 64 + 4 * (13 + m))
                        if br == 0:
                            page_loads(s, b, pv, m - 3, A["cache_v_slc"])
                        else:
                            sp.wait_ge(pv, m - 3)
                            state_load(s, b, A["state_v_win"])
                looped(sp, o, 2, vals)
            quads(Q_OB, w_ob, 8, first=1)

        @block.gpsimd
        def _(pool):
            o = Own(pool, own["pool"])
            pool.dma_start(CON[:, :], A["consts"]).then_inc(s_con, 16)
            pool.dma_start(CROW[0:1, :], A["c_prompt"]).then_inc(s_rows, 16)
            pool.dma_start(CROW[1:NC, :], A["c_sample"]).then_inc(s_rows, 16)
            for v, src in enumerate((A["g_norm"][0:1], A["g_norm"][1:2], A["g_kv"].rearrange("(o n) -> o n", o=1),
                                     A["g_final"].rearrange("(o n) -> o n", o=1), A["pool_scale"])):
                pool.dma_start(VEC[KT * v:KT * v + KT, :], src.rearrange("o (k p) -> (o k) p", p=P)).then_inc(s_rows, 16)
            pool.dma_start(RELA[0:32, :], A["rel_bias"]).then_inc(s_rel, 16)
            pool.dma_start(ONEH[:, :], A["onehots"]).then_inc(s_rel, 16)
            pool.dma_start(PTAB[:, :], A["page_table"].rearrange("b n -> (b n)").rearrange("(o n) -> o n", o=1)).then_inc(s_pt, 16)
            nc.gpsimd.memset(CST[:, :, :].bitcast(F32), 0.0).then_inc(s_cz, 1)
            for t in range(5):
                if t >= 2:
                    pool.wait_ge(s_t, 2 + 4 * (t - 1))
                src = A["x_prompt"][0][t * P:(t + 1) * P] if t < NT else A["x_sample"].rearrange("b s d -> (b s) d")
                pool.dma_start(XN[t % 2][0:src.shape[0], :], src).then_inc(s_x[t % 2], 16)
            pool.wait_ge(s_te, 22)
            pool.dma_start(x_scr, flat(X[:, :, :])).then_inc(s_x0, 16)
            pool.dma_start(SPN[:, :], A["state_pool"][0].rearrange("b t d -> (b t) d")).then_inc(s_sp, 16)
            pool.wait_ge(s_te, 2 + 20 + 6)
            pool.dma_start(g_scr, GROW[:, :]).then_inc(s_gscr, 16)
            pool.wait_ge(s_gscr, 16)
            pool.dma_start(b_scr, bass.AP(tensor=g_scr.tensor, offset=P, ap=[[2 * GLEN, NH], [-1, P], [1, 512]])).then_inc(s_bscr, 16)
            pool.dma_start(c_scr, bass.AP(tensor=g_scr.tensor, offset=GLEN + 481, ap=[[2 * GLEN, NH], [-16, NCMP], [1, TP]])).then_inc(s_bscr, 16)

            def b_rows(l):
                def body(i):
                    for s in range(2):
                        p = 2 * i + s + 24 * l
                        wait(pool, tr_done, p - 1)
                        b = A["b_ada"][l:l + 1]
                        at = (2 * i + s) * 256
                        b = b[:, bass.ds(at, 256)] if not isinstance(at, int) else b[:, at:at + 256]
                        pool.dma_start(MROW[18:19, s, :], b).then_inc(s_brow[s], 16)
                return body
            for l in range(2):
                looped(pool, o, 12, b_rows(l))
            pool.dma_start(pool_s[0][:, 0:PB - 1, :], A["state_pool"][0][:, 1:PB, :]).then_inc(s_copy, 16)
            pool.dma_start(k_win_s[:, 0:TP - 1], A["state_k_win"][:, 1:TP]).then_inc(s_copy, 16)
            pool.dma_start(v_win_s[:, 0:TP - 1], A["state_v_win"][:, 1:TP]).then_inc(s_copy, 16)

            def apply(a):
                l = (0, None, 1)[a]
                for k in range(KT):
                    pool.wait_ge(tn_ready, KT * a + k + 1)
                    wait(pool, h_ready, KT * a + k - 2)
                    tn, hf = TN[k % 2][:, TP:T], HF[k % 3][:, TP:T]
                    o(nc.gpsimd.tensor_tensor(hf, tn, AMOD[:, l, k, 1:NC], ALU.mult))
                    nc.gpsimd.tensor_tensor(hf, hf, MODT[:, ML * l + k, 1:NC], ALU.add).then_inc(hfs_ready, 1)

            pool.wait_ge(amod, 1)
            apply(0)
            pool.wait_ge(s_ute, 4)
            pool.dma_start(pool_p[0, 0], UT[0:PB, :]).then_inc(s_uo, 16)
            pool.dma_start(pool_s[0][:, PB - 1, :], UT[PB:PB + TS, :]).then_inc(s_uo, 16)
            for i in range(2):
                o(nc.gpsimd.memset(PAD[i][:, 0:16], 0.0))
            for g, w in enumerate(WINDOWS):
                for k in range(4 * g, 4 * g + 4):
                    u = Y[:, k, 0:TP]
                    o(nc.gpsimd.tensor_tensor(PAD[0][:, 17:16 + TP], u[:, 1:TP], u[:, 0:TP - 1], ALU.add))
                    o(nc.gpsimd.tensor_copy(PAD[0][:, 16:17], u[:, 0:1]))
                    src, step = 0, 2
                    while step < w:
                        o(nc.gpsimd.tensor_tensor(PAD[1 - src][:, 16:16 + TP], PAD[src][:, 16:16 + TP], PAD[src][:, 16 - step:16 + TP - step], ALU.add))
                        src, step = 1 - src, 2 * step
                    s_ = PAD[src]
                    o(nc.gpsimd.tensor_tensor(s_[:, 16:32], s_[:, 16:32], CON[:, C_CNT + 16 * g:C_CNT + 16 * g + 16], ALU.mult))
                    o(nc.gpsimd.tensor_scalar(s_[:, 32:16 + TP], s_[:, 32:16 + TP], 1.0 / w, None, ALU.mult))
                    last = nc.gpsimd.tensor_tensor(u, s_[:, 16:16 + TP], u, ALU.subtract)
                    if k < 4 * g + 3:
                        o(last)
                last.then_inc(s_pooled, 1)
                pool.wait_ge(s_pooled, g + 1)
            pool.wait_ge(acc_free, 2 * D_OA)
            pool.wait_ge(s_x0, 16)
            pool.dma_start(flat(X[:, :, :]), x_scr).then_inc(s_x1, 16)

            def kv_rows(i):
                for t in range(5):
                    n = 5 * i + t
                    pool.wait_ge(tm_ready, n + 1)
                    rows = P if t < NT else TS
                    dst = kv_out_p[i][t * P:(t + 1) * P] if t < NT else kv_out_s[i]
                    pool.dma_start(dst, TM[n % 4][0:rows, :]).then_inc(tm_out[n % 4], 16)
            for i in range(5):
                kv_rows(i)
            kv_rows(5)
            pool.wait_ge(kv_tr, 30)
            for i, n in enumerate("kv"):
                pool.dma_start(W2[i][:, :], A[f"w_c{n}2"]).then_inc(s_cw, 16)
                pool.dma_start(PE_[i][:, :], A[f"pe_{n}"]).then_inc(s_cw, 16)
            pool.wait_ge(cout, 18)
            pool.dma_start(vc_scr, VCP[:, :, :].rearrange("p g d -> p (g d)")).then_inc(s_vcp, 16)
            apply(2)
            pool.wait_ge(tn_ready, 3 * KT)
            pool.dma_start(x_scr, flat(X[:, :, :])).then_inc(s_xs, 16)
            pool.wait_ge(acc_free, 2 * (D_G + 1))
            for br in range(NBR):
                for g in range(NKV):
                    pool.dma_start(bass.AP(tensor=gd_scr.tensor, offset=br * P + g * 32, ap=[[1, REP], [4, TS]]),
                                   GF[br * NH + g * REP:br * NH + g * REP + REP, TP:T],
                                   allow_slow_non_contiguous=True).then_inc(s_gd, 16)
            pool.wait_ge(s_gd, 16 * 12)
            pool.wait_ge(s_xs, 16)
            pool.wait_ge(s_vcp, 16)
            pool.wait_ge(s_bscr, 32)
            for s in range(4):
                pool.wait_ge(tm_out[s], 16 * len([n for n in range(30) if n % 4 == s]))

            def head_loads(i):
                wait(pool, c_done, 6 * i)
                g = i // 2
                gd = lambda w: w.rearrange("(t p) (g d) -> g p t d", p=P, d=P)
                for br, v in enumerate((kv_out_p[3], kv_out_p[5])):
                    src = gd(v)
                    src = src[bass.ds(g, 1)] if not isinstance(g, int) else src[g:g + 1]
                    pool.dma_start(VG[:, br, :, :], src.rearrange("o p t d -> (o p) t d")).then_inc(hd_in, 16)
                vs = vc_scr.rearrange("n (g d) -> g n d", d=P)
                vs = vs[bass.ds(g, 1)] if not isinstance(g, int) else vs[g:g + 1]
                pool.dma_start(VCG[:, :], vs.rearrange("o n d -> (o n) d")).then_inc(hd_in, 16)
                h2 = lambda w: (w[bass.ds(i * 2, 2)] if not isinstance(i, int) else w[2 * i:2 * i + 2]).rearrange("h p n -> p h n")
                pool.dma_start(BH[:, :, :], h2(b_scr)).then_inc(hd_in, 16)
                pool.dma_start(BC[:, :, :], h2(c_scr)).then_inc(hd_in, 16)
                for u in range(6):
                    n = 6 * i + u
                    pool.wait_ge(r_ready, n + 1)
                    if u < 2:
                        last = nc.gpsimd.tensor_tensor(
                            PR[:, 0:NT * NCMP].rearrange("p (t n) -> p t n", n=NCMP), PR[:, 0:NT * NCMP].rearrange("p (t n) -> p t n", n=NCMP),
                            STAT[:, 8:12].unsqueeze(2).broadcast_to([P, NT, NCMP]), ALU.mult)
                    else:
                        at = 0
                        for t in range(NT):
                            w = P * (t + 1)
                            last = nc.gpsimd.tensor_tensor(PR[:, at:at + w], PR[:, at:at + w],
                                                           STAT[:, 8 + t:9 + t].broadcast_to([P, w]), ALU.mult)
                            at += w
                    last.then_inc(p_ready, 1)
            looped(pool, o, 8, head_loads)

            pool.wait_ge(w_used, 4 * Q_OB)
            nc.gpsimd.memset(PX[:, :], 0.0)
            nc.gpsimd.memset(ZERO[:, :], 0.0).then_inc(s_dm, 1)
            pool.dma_start(GD[:, :], bass.AP(tensor=gd_scr.tensor, offset=0, ap=[[1, P], [P, NBR]]),
                           allow_slow_non_contiguous=True).then_inc(s_bd, 16)
            for g in range(NKV):
                for b in range(TS):
                    r = 32 * g + 4 * b
                    pool.dma_start(BD[r:r + 4, :], g_scr[4 * g:4 * g + 4, 0:513]).then_inc(s_bd, 16)
                    pool.dma_start(BCD[r:r + 4, :], g_scr[4 * g:4 * g + 4, 31:31 + 16 * NCMP:16],
                                   allow_slow_non_contiguous=True).then_inc(s_bd, 16)

            for br in range(2):
                def queries(i, br=br):
                    for s in range(4):
                        b = 4 * i + s
                        pool.wait_ge(dsc, 8 * br + b + 1)
                        q = QD[:, :, :].rearrange("p (g r) b -> p g b r", g=NKV)
                        mk = CON[:, bass.ds(b * 8 + C_MSK, 8)] if not isinstance(b, int) else CON[:, C_MSK + 8 * b:C_MSK + 8 * b + 8]
                        mk = mk.unsqueeze(1).unsqueeze(3).broadcast_to([P, NKV, TS, REP])
                        nc.gpsimd.tensor_tensor(QPAD[s % 2][:, :, :].rearrange("p g (b r) -> p g b r", b=TS), q, mk, ALU.mult).then_inc(qp_ready, 1)
                looped(pool, o, 2, queries)
            for br in range(2):
                def new_values(i, br=br):
                    for s in range(2):
                        b = 2 * i + s
                        wait(pool, pv, 8 * br + b - 1)
                        src = kv_out_s[3 if br == 0 else 5]
                        src = src[bass.ds(b, 1)] if not isinstance(b, int) else src[b:b + 1]
                        pool.dma_start(VN[s][:, :], src).then_inc(s_vn[s], 16)
                looped(pool, o, 4, new_values)
            pool.wait_ge(ydec, 1)
            pool.dma_start(flat(X[:, :, :]), x_scr).then_inc(s_xb, 16)
            for t in range(5):
                pool.wait_ge(yn_ready, 4 * (t + 1))
                rows = P if t < NT else TS
                dst = y_prompt[0, t * P:(t + 1) * P] if t < NT else y_sample[:, 0]
                pool.dma_start(dst, YN[t % 2][0:rows, :]).then_inc(yn_out[t % 2], 16)
            pool.wait_ge(yn_out[0], 48)
            pool.wait_ge(yn_out[1], 32)
            pool.wait_ge(s_copy, 48)
            pool.wait_ge(s_uo, 32)

        @block.scalar
        def _(act):
            o = Own(act, own["act"])

            def hi(q, j):
                act.wait_ge(raw_full[j], 16 * (q - 23))
                wait(act, w_used, 4 * q + j - 1)
                nc.scalar.activation(HI[j % 2][:, :, :], RAW[j][:, :, :], ACT.Copy).then_inc(hi_ready, 1)

            act.wait_ge(s_rows, 16 * 7)
            nc.scalar.activation(CSIL[:, :], CROW[:, :], ACT.Silu).then_inc(s_csil, 1)
            act.wait_ge(s_te, 2)
            act.wait_ge(s_cz, 1)
            nc.scalar.activation(CST[:, :, 0:NC], CTF[:, :, :], ACT.Copy).then_inc(s_cs, 1)

            def mod_rows(p, s):
                act.wait_ge(w_used, 4 * p + 4)
                wait(act, tr_done, p - 1)
                nc.scalar.activation(MROW[0:18, s, :], D[s][0:18, 0:256], ACT.Copy).then_inc(mr_ready, 1)

            def ada(l):
                def body(i):
                    for s in range(2):
                        p = 2 * i + s + 24 * l
                        for j in range(4):
                            act.wait_ge(raw_full[4 * s + j], 16 * (i + 12 * l + 1))
                            wait(act, w_used, 4 * p + j - 3)
                            nc.scalar.activation(HI[j][:, :, :], RAW[4 * s + j][:, :, :], ACT.Copy).then_inc(hi_ready, 1)
                            if j == 1 and not (isinstance(p, int) and p == 0):
                                mod_rows(p - 1, 1 - s)
                return body
            for l in range(2):
                looped(act, o, 12, ada(l))
            mod_rows(47, 1)
            hi(Q_U, 0)

            def square(r, k, slot):
                if r:
                    act.wait_ge(acc_free, 2 * (0, D_OA, D_OB)[r] + k + 1)
                wait(act, sq_used, KT * r + k - 1)
                nc.scalar.activation(SQ[slot][:, :], dyn(X, k).rearrange("p o t -> p (o t)"), ACT.Square).then_inc(sq_ready, 1)

            def squares(r, i):
                for mm in range(2):
                    square(r, 2 * i + mm, mm)

            def rms(r):
                act.wait_ge(sq_used, KT * (r + 1))
                for half in range(2):
                    last = nc.scalar.activation(RMS[:, half * HT:(half + 1) * HT], S[half][:, 0:HT], ACT.Sqrt,
                                                scale=1.0 / DM, bias=CON[:, C_EPS:C_EPS + 1])
                last.then_inc(rms_ready, 1)

            def apply(a):
                l = (0, None, 1, None)[a]
                for k in range(KT + 1):
                    if k < KT:
                        act.wait_ge(tn_ready, KT * a + k + 1)
                        if a == 3:
                            nc.scalar.activation(X[:, k, :], TN[k % 2][:, :], ACT.Copy, scale=vec(3, k)).then_inc(hf_ready, 1)
                            continue
                        wait(act, h_ready, KT * a + k - 2)
                        if l is None:
                            nc.scalar.activation(HF[k % 3][:, :], TN[k % 2][:, :], ACT.Copy, scale=vec(2, k)).then_inc(hf_ready, 1)
                        else:
                            nc.scalar.activation(HF[k % 3][:, 0:TP], TN[k % 2][:, 0:TP], ACT.Identity,
                                                 scale=AMOD[:, l, k, 0:1], bias=MODT[:, ML * l + k, 0:1]).then_inc(hf_ready, 1)
                    if k and a < 3:
                        act.wait_ge(hf_ready, KT * a + k)
                        if l is not None:
                            act.wait_ge(hfs_ready, KT * (a // 2) + k)
                        nc.scalar.activation(HH[:, k - 1, :], HF[(k - 1) % 3][:, :], ACT.Copy).then_inc(hhi_ready, 1)

            act.wait_ge(s_te, 22)
            for i in range(8):
                squares(0, i)
            rms(0)
            act.wait_ge(amod, 1)
            apply(0)

            def dense_tile(q, d, mm):
                if mm == 0:
                    act.wait_ge(first_done, d + 1)
                else:
                    act.wait_ge(w_used, 4 * q + 4)

            def evac(dst, mm):
                for half, h in enumerate(halves(dst)):
                    last = nc.scalar.activation(h, D[2 * mm + half][:, 0:HT], ACT.Copy)
                last.then_inc(acc_free, 1)

            def u_pairs(i):
                for q, j in ahead(Q_U + i):
                    hi(q, j)
                for mm in range(2):
                    dense_tile(Q_U + i, D_U + i, mm)
                    evac(dyn(Y, 2 * i + mm).rearrange("p o t -> p (o t)"), mm)
            looped(act, o, 8, u_pairs)

            act.wait_ge(s_x0, 16)

            def z_pairs(i):
                for q, j in ahead(Q_Z + i):
                    hi(q, j)
                for mm in range(2):
                    dense_tile(Q_Z + i, D_Z + i, mm)
                    for half, h in enumerate(halves(dyn(ZS, 2 * i + mm).rearrange("p o t -> p (o t)"))):
                        last = nc.scalar.activation(h, D[2 * mm + half][:, 0:HT], ACT.Silu)
                    last.then_inc(acc_free, 1)
            looped(act, o, 8, z_pairs)

            def pooled_hi(g):
                wait(act, w_used, 4 * Q_MIX + 2 * (g - 1))
                nc.scalar.activation(PHI[g % 2][:, :, :], Y[:, 4 * g:4 * g + 4, :], ACT.Copy).then_inc(s_ph, 1)

            def y_hi(n, k):
                nc.scalar.activation(HH[:, k, :], Y[:, k, :], ACT.Copy).then_inc(ys_hi, 1)

            act.wait_ge(s_uo, 32)
            act.wait_ge(s_pooled, 4)
            act.wait_ge(s_pooled_s, 1)
            pooled_hi(0)
            pooled_hi(1)
            for n in range(8):
                if n in (2, 4):
                    pooled_hi(n // 2 + 1)
                hi(Q_MIX + (n + 1) // 4, (n + 1) % 4)
                if n:
                    for k in (2 * n - 2, 2 * n - 1):
                        act.wait_ge(acc_free, 2 * D_MIX + k + 1)
                        y_hi(0, k)
            for k in (14, 15):
                act.wait_ge(acc_free, 2 * D_MIX + k + 1)
                y_hi(0, k)

            def resid_pairs(r, q0, skip):
                def body(i):
                    for q, j in ahead(q0 + i):
                        if not (skip and isinstance(i, int) and i == 7 and j == 0):
                            hi(q, j)
                        if j == 1 and not (isinstance(i, int) and i == 0):
                            squares(r, i - 1)
                looped(act, o, 8, body, 2, 1)
                squares(r, 7)
                rms(r)
            resid_pairs(1, Q_OA, False)
            act.wait_ge(w_used, 4 * Q_KV)
            apply(1)
            for i, dst in enumerate((KCF, VCF, KS, VF, KW, VF)):
                if i == 5:
                    act.wait_ge(kv_tr, 20)

                def kv_pair(pp, i=i, dst=dst):
                    q, d = Q_KV + 2 * i + pp, D_KV + 2 * i + pp
                    for qq, j in ahead(q):
                        hi(qq, j)
                    for mm in range(2):
                        dense_tile(q, d, mm)
                        for half in range(2):
                            to = dyn(dst, 2 * pp + mm)[:, :, half * HT:(half + 1) * HT].rearrange("p o t -> p (o t)")
                            last = nc.scalar.activation(to, D[2 * mm + half][:, 0:HT], ACT.Copy)
                        last.then_inc(acc_free, 1)
                looped(act, o, 2, kv_pair)

            def hidden(n, kv, base):
                act.wait_ge(cw1, n + 1)
                if base:
                    act.wait_ge(cw2, n - 1)
                nc.scalar.activation(CSIL2[kv][:, :], S[2][:, 0:NKV * NCMP], ACT.Silu, bias=PEC[:, kv:kv + 1]).then_inc(csr, 1)

            act.wait_ge(s_pee, 3)

            def pages_out(n, slot):
                for g in (1, 3):
                    act.wait_ge(ctr, 4 * n + g + 1)
                    nc.scalar.activation(RT_T[slot][:, g, :], S[1][:, :], ACT.Copy).then_inc(ctre[1], 1)

            def hiddens(b):
                for kv in range(2):
                    wait(act, cw1, 2 * b + kv - 1)
                    pages_out(2 * b + kv, kv)
                    hidden(2 * b + kv, kv, not isinstance(b, int))
            looped(act, o, TS, hiddens)
            for kv in range(2):
                hidden(16 + kv, kv, True)
            act.wait_ge(cw2, 18)
            apply(2)
            for q, j in ahead(Q_G):
                hi(q, j)
            act.wait_ge(w_used, 4 * (Q_G + 1))
            for half in range(2):
                last = nc.scalar.activation(GF[:, half * HT:(half + 1) * HT], D[half][0:48, 0:HT], ACT.Sigmoid)
            last.then_inc(acc_free, 2)

            def exps(n, u):
                act.wait_ge(negm, n + 1)
                if u < 2:
                    nc.scalar.activation(PR[:, 0:NT * NCMP], PR[:, 0:NT * NCMP], ACT.Exp).then_inc(e_done, 1)
                else:
                    at = 0
                    for t in range(NT):
                        w = P * (t + 1)
                        last = nc.scalar.activation(PR[:, at:at + w], PR[:, at:at + w], ACT.Exp,
                                                    bias=STAT[:, t:t + 1], accum_out=STAT[:, 4 + t:5 + t])
                        at += w
                    last.then_inc(e_done, 1)

            def turned(n, u):
                act.wait_ge(b_done, n + 1)
                wait(act, c_done, n)
                if u < 2:
                    nc.scalar.activation(PT[0:NCMP, 0:512], S[0][0:NCMP, :], ACT.Copy).then_inc(pt_ready, 1)
                else:
                    nc.scalar.activation(PT[:, 0:512], S[0][:, :], ACT.Copy)
                    nc.scalar.activation(PT[:, 512:1024], S[1][:, :], ACT.Copy)
                    nc.scalar.activation(PT[:, 1024:1280], S[2][:, 0:256], ACT.Copy).then_inc(pt_ready, 1)

            act.wait_ge(s_xs, 16)

            def heads(i):
                for s in range(17):
                    if s < 16:
                        hi(Q_H + 4 * i + (s + 1) // 4, (s + 1) % 4)
                    if s >= 4 and s % 4 == 0:
                        blk = s // 4 - 1
                        for mm in range(2):
                            dense_tile(Q_H + 4 * i + blk, D_H + 4 * i + blk, mm)
                            if blk == 0:
                                wait(act, a_done, 6 * i)
                                nc.scalar.activation(QS[:, mm, 0:HT], D[2 * mm][:, 0:HT], ACT.Copy, scale=SCALE)
                                nc.scalar.activation(QS[:, mm, HT:TP], D[2 * mm + 1][:, 0:TP - HT], ACT.Copy, scale=SCALE)
                                to = dyn(QD, 2 * i + mm).rearrange("p o b -> p (o b)")
                                nc.scalar.activation(to, D[2 * mm + 1][:, TP - HT:HT], ACT.Copy, scale=SCALE).then_inc(acc_free, 1)
                            else:
                                wait(act, o_used, 6 * i)
                                for half in range(2):
                                    nc.scalar.activation(ZB[:, blk - 1, mm, half * HT:(half + 1) * HT], D[2 * mm + half][:, 0:HT], ACT.Silu)
                                to = SZD[:, blk - 1]
                                to = dyn(to, 2 * i + mm).rearrange("p o b -> p (o b)")
                                nc.scalar.activation(to, D[2 * mm + 1][:, TP - HT:HT], ACT.Silu).then_inc(acc_free, 1)
                    u = (s - 4) // 2
                    if s >= 4 and s % 2 == 0 and u < 6:
                        exps(6 * i + u, u)
                    if s >= 5 and s % 2 == 1:
                        turned(6 * i + (s - 5) // 2, (s - 5) // 2)
            looped(act, o, 8, heads)

            for br in range(2):
                def stage(i, br=br):
                    for s in range(2):
                        b = 2 * i + s
                        m = 8 * br + b
                        pages_out(16 + m, s)
                        act.wait_ge(dsc, m + 1)
                        if br == 0:
                            nc.scalar.activation(KCB[s][:, :], dyn(KCS, b).rearrange("p o n -> p (o n)"), ACT.Copy)
                        kt_ = (KS if br == 0 else KW)
                        kn = kt_[:, :, bass.ds(b + TP, 1)] if not isinstance(b, int) else kt_[:, :, b + TP:b + TP + 1]
                        nc.scalar.activation(KN[s][:, :], kn.rearrange("p g o -> p (g o)"), ACT.Copy).then_inc(kst, 1)
                looped(act, o, 4, stage)
            for n in range(3):
                act.wait_ge(sd_step, n + 1)
                src = (SC[:, :], SD[0][:, :], SD[1][:, :])[n]
                nc.scalar.activation(src, src, ACT.Exp, bias=SST[:, n:n + 1], accum_out=SST[:, 4 + n:5 + n]).then_inc(sd_exp, 1)
            act.wait_ge(ydec, 1)
            for k in range(KT):
                y_hi(1, k)
            act.wait_ge(s_xb, 16)
            resid_pairs(2, Q_OB, True)
            apply(3)

        @block.vector
        def _(dve):
            o = Own(dve, own["dve"])
            V = nc.vector

            def lo(q, j):
                dve.wait_ge(hi_ready, 4 * q + j + 1)
                V.tensor_tensor(LO[j % 2][:, :, :], RAW[j][:, :, :], HI[j % 2][:, :, :].bitcast(F32), ALU.subtract).then_inc(lo_ready, 1)

            V.memset(RELA[32:33, :], NEG).then_inc(s_negrow, 1)
            dve.wait_ge(s_t, 1)
            V.tensor_copy(VECT[:, :], S[0][:, 0:80]).then_inc(s_te, 1)
            dve.wait_ge(s_t, 2)
            V.tensor_copy(flat(CTF[:, :, :]), S[1][:, 0:KT * NC]).then_inc(s_te, 1)
            dve.wait_ge(s_cs, 1)
            V.tensor_tensor(CST[:, :, NC:2 * NC], CTF[:, :, :], CST[:, :, 0:NC].bitcast(F32), ALU.subtract).then_inc(s_cs, 1)
            for t in range(5):
                n = P if t < NT else TS
                for k4 in range(4):
                    dve.wait_ge(s_t, 2 + 4 * t + k4 + 1)
                    V.tensor_copy(X[:, 4 * k4:4 * k4 + 4, t * P:t * P + n],
                                  S[k4 % 2][:, :].rearrange("p (k t) -> p k t", k=4)[:, :, 0:n]).then_inc(s_te, 1)
            for n in range(6):
                dve.wait_ge(s_t, 22 + n + 1)
                at = (n // 3) * GLEN + (n % 3) * 512
                w = min(512, GLEN - (n % 3) * 512)
                V.tensor_copy(GROW[:, at:at + w], S[n % 2][0:NH, 0:w]).then_inc(s_te, 1)

            def mod_out(p, s):
                dve.wait_ge(tr_done, p + 1)
                V.tensor_copy(dyn(MODT, 2 * p, 2), S[s][:, 0:2 * NC].rearrange("p (a n) -> p a n", a=2)).then_inc(mt_ready, 1)

            def ada(l):
                def body(i):
                    for s in range(2):
                        p = 2 * i + s + 24 * l
                        for j in range(4):
                            dve.wait_ge(hi_ready, 4 * p + j + 1)
                            V.tensor_tensor(LO[j][:, :, :], RAW[4 * s + j][:, :, :], HI[j][:, :, :].bitcast(F32), ALU.subtract).then_inc(lo_ready, 1)
                            if j == 2 and not (isinstance(p, int) and p == 0):
                                mod_out(p - 1, 1 - s)
                return body
            for l in range(2):
                looped(dve, o, 12, ada(l))
            mod_out(47, 1)
            lo(Q_U, 0)
            dve.wait_ge(mt_ready, 48)
            last = None
            for l in range(2):
                if last is not None:
                    o(last)
                o(V.tensor_scalar(AMOD[:, l, :, :], MODT[:, ML * l + KT:ML * l + 2 * KT, :], 1.0, None, ALU.add))
                last = V.tensor_tensor(AMOD[:, l, :, :], AMOD[:, l, :, :],
                                       VECT[:, KT * l:KT * l + KT].unsqueeze(2).broadcast_to([P, KT, NC]), ALU.mult)
            last.then_inc(amod, 1)

            def rstd(r):
                dve.wait_ge(rms_ready, r + 1)
                V.reciprocal(RSTD[:, :], RMS[:, :]).then_inc(rstd_ready, 1)
                dve.wait_ge(rstd_ready, r + 1)

            def apply(a):
                for k in range(KT + 2):
                    if k < KT:
                        if a or k >= 2:
                            dve.wait_ge(hf_ready, KT * a + k - 1)
                            if a in (0, 2):
                                wait(dve, hfs_ready, KT * (a // 2) + k - 1)
                        V.tensor_tensor(TN[k % 2][:, :], X[:, k, :], RSTD[:, :], ALU.mult).then_inc(tn_ready, 1)
                    if k >= 2 and a < 3:
                        dve.wait_ge(hhi_ready, KT * a + k - 1)
                        V.tensor_tensor(HL[:, k - 2, :], HF[(k - 2) % 3][:, :], HH[:, k - 2, :].bitcast(F32), ALU.subtract).then_inc(h_ready, 1)

            rstd(0)
            apply(0)

            def los(q0, n):
                def body(i):
                    for q, j in ahead(q0 + i):
                        lo(q, j)
                looped(dve, o, n, body)
            los(Q_U, 8)
            for k4 in range(4):
                dve.wait_ge(s_ut, k4 + 1)
                V.tensor_copy(UT[:, 512 * k4:512 * k4 + 512], S[k4 % 2][0:23, :]).then_inc(s_ute, 1)
            dve.wait_ge(s_ps, 1)
            for g, w in enumerate(WINDOWS):
                us = Y[:, 4 * g:4 * g + 4, TP:T]
                ps = O[:, 32 * g:32 * g + 32].rearrange("p (k b) -> p k b", k=4)
                o(V.tensor_tensor(STMP[:, :, :], ps, us, ALU.add))
                last = V.scalar_tensor_tensor(out=us, in0=STMP[:, :, :], scalar=1.0 / w, in1=us, op0=ALU.mult, op1=ALU.subtract)
                if g < 3:
                    o(last)
            last.then_inc(s_pooled_s, 1)
            los(Q_Z, 8)

            def pooled_lo(g):
                dve.wait_ge(s_ph, g + 1)
                V.tensor_tensor(PLO[g % 2][:, :, :], Y[:, 4 * g:4 * g + 4, :], PHI[g % 2][:, :, :].bitcast(F32), ALU.subtract).then_inc(s_pl, 1)

            def y_lo(n, k):
                dve.wait_ge(ys_hi, KT * n + k + 1)
                V.tensor_tensor(HL[:, k, :], Y[:, k, :], HH[:, k, :].bitcast(F32), ALU.subtract).then_inc(ys, 1)

            pooled_lo(0)
            pooled_lo(1)
            for n in range(8):
                if n in (2, 4):
                    pooled_lo(n // 2 + 1)
                lo(Q_MIX + (n + 1) // 4, (n + 1) % 4)
                for mm in range(2):
                    if mm == 0:
                        dve.wait_ge(first_done, D_MIX + n + 1)
                    else:
                        dve.wait_ge(w_used, 4 * Q_MIX + n + 1)
                    m = 2 * n + mm
                    for half, h in enumerate(halves(Y[:, m, :])):
                        last = V.scalar_tensor_tensor(out=h, in0=D[2 * mm + half][:, 0:HT], scalar=vec(4, m),
                                                      in1=halves(ZS[:, m, :])[half], op0=ALU.mult, op1=ALU.mult)
                    last.then_inc(acc_free, 1)
                if n:
                    for k in (2 * n - 2, 2 * n - 1):
                        y_lo(0, k)
            y_lo(0, 14)
            y_lo(0, 15)

            def resid(l, q0, d0):
                def body(i):
                    for q, j in ahead(q0 + i):
                        if not (l == 1 and isinstance(i, int) and i == 7 and j == 0):
                            lo(q, j)
                    for mm in range(2):
                        m = 2 * i + mm
                        if mm == 0:
                            dve.wait_ge(first_done, d0 + i + 1)
                        else:
                            dve.wait_ge(w_used, 4 * (q0 + i) + 4)
                        x = dyn(X, m).rearrange("p o t -> p (o t)")
                        gate = dyn(MODT, m + ML * l + 2 * KT).rearrange("p o n -> p (o n)")
                        a, b = D[2 * mm], D[2 * mm + 1]
                        V.scalar_tensor_tensor(out=x[:, 0:HT], in0=a[:, 0:HT], scalar=gate[:, 0:1], in1=x[:, 0:HT], op0=ALU.mult, op1=ALU.add)
                        V.scalar_tensor_tensor(out=x[:, HT:TP], in0=b[:, 0:TP - HT], scalar=gate[:, 0:1], in1=x[:, HT:TP], op0=ALU.mult, op1=ALU.add)
                        dve.wait_ge(acc_free, 2 * (d0 + i) + mm - 1)
                        o(V.tensor_tensor(RT[mm][:, :], b[:, TP - HT:HT], gate[:, 1:NC], ALU.mult))
                        V.tensor_tensor(x[:, TP:T], x[:, TP:T], RT[mm][:, :], ALU.add).then_inc(acc_free, 1)
                return body
            dve.wait_ge(s_x1, 16)
            looped(dve, o, 8, resid(0, Q_OA, D_OA))
            rstd(1)
            apply(1)

            for i, src in enumerate((KCF, VCF, KS, VF, KW, VF)):
                los(Q_KV + 2 * i, 2)
                for t in range(5):
                    n = 5 * i + t
                    rows = P if t < NT else TS
                    dve.wait_ge(kv_tr, n + 1)
                    if n >= 4:
                        dve.wait_ge(tm_out[n % 4], 16 * (n // 4))
                    V.tensor_copy(TM[n % 4][0:rows, :], S[n % 2][0:rows, :]).then_inc(tm_ready, 1)

            for kv in range(2):
                dve.wait_ge(s_pe, kv + 1)
                V.tensor_copy(PET[kv][:, :], S[kv][:, 0:CL]).then_inc(s_pee, 1)
            dve.wait_ge(s_pe, 3)
            V.tensor_copy(PEC[:, :], O[:, 0:2]).then_inc(s_pee, 1)

            def compress_out(n, kv, b):
                dve.wait_ge(cw2, n + 1)
                if kv == 0:
                    dst = dyn(KCS, b).rearrange("p o n -> p (o n)")
                    V.tensor_copy(dst, O[:, 0:NKV * NCMP]).then_inc(cout, 1)
                else:
                    dst = VCS[:, bass.ds(b, 1), :] if not isinstance(b, int) else VCS[:, b:b + 1, :]
                    V.tensor_copy(dst.rearrange("p o n -> p (o n)"), O[0:NKV * NCMP, 0:P]).then_inc(cout, 1)

            def pages_out(n, slot):
                for g in (0, 2):
                    dve.wait_ge(ctr, 4 * n + g + 1)
                    V.tensor_copy(RT_T[slot][:, g, :], S[0][:, :]).then_inc(ctre[0], 1)

            def compress(b):
                for kv in range(2):
                    pages_out(2 * b + kv, kv)
                    compress_out(2 * b + kv, kv, b)
            looped(dve, o, TS, compress)
            dve.wait_ge(cw2, 17)
            V.tensor_copy(KCP[:, :], O[:, 0:NKV * NCMP]).then_inc(cout, 1)
            dve.wait_ge(cw2, 18)
            V.tensor_copy(flat(VCP[:, :, :]), O[0:NCMP, :]).then_inc(cout, 1)

            apply(2)
            for q, j in ahead(Q_G):
                lo(q, j)
            dve.wait_ge(g_tr, 1)
            V.tensor_copy(flat(GT[:, :, :]), S[0][:, 0:NT * 48]).then_inc(gt_ready, 1)
            dve.wait_ge(gt_ready, 1)
            dve.wait_ge(s_xs, 16)

            W_AT = [0, 1, 3, 6]

            def softmax(i, u):
                n, br, hh = 6 * i + u, u // 2, u % 2
                dve.wait_ge(a_done, n + 1)
                if u == 0:
                    dve.wait_ge(hd_in, 80 * (i + 1))
                wait(dve, b_done, n)
                if u < 2:
                    sc = S[0][:, 0:NT * NCMP].rearrange("p (t n) -> p t n", n=NCMP)
                    pr = PR[:, 0:NT * NCMP].rearrange("p (t n) -> p t n", n=NCMP)
                    o(V.tensor_reduce(STAT[:, 0:4], sc, AX.X, ALU.max))
                    V.tensor_tensor(pr, sc, STAT[:, 0:4].unsqueeze(2).broadcast_to([P, NT, NCMP]), ALU.subtract).then_inc(negm, 1)
                else:
                    where = (S[1][:, 384:512], S[2][:, 0:256], S[1][:, 0:384], S[0][:, :])
                    V.memset(STAT[:, 12:13], 0.0)
                    for t in range(NT):
                        w = P * (t + 1)
                        at = W_AT[t] * P
                        last = V.tensor_tensor_reduce(PR[:, at:at + w], where[t], BH[:, hh, (3 - t) * P:512], 1.0, -3e38,
                                                      ALU.add, ALU.max, STAT[:, t:t + 1])
                    o(last)
                    V.tensor_scalar(STAT[:, 0:4], STAT[:, 0:4], -1.0, None, ALU.mult).then_inc(negm, 1)

            def factor(i, u):
                n, br, hh = 6 * i + u, u // 2, u % 2
                dve.wait_ge(e_done, n + 1)
                if u < 2:
                    o(V.tensor_reduce(STAT[:, 4:8], PR[:, 0:NT * NCMP].rearrange("p (t n) -> p t n", n=NCMP), AX.X, ALU.add))
                o(V.reciprocal(STAT[:, 8:12], STAT[:, 4:8]))
                at = 2 * i + (br * NH + hh)
                gate = GT[:, :, bass.ds(at, 1)] if not isinstance(at, int) else GT[:, :, at:at + 1]
                mul = V.tensor_tensor(STAT[:, 8:12], STAT[:, 8:12], gate.rearrange("p t o -> p (t o)"), ALU.mult)
                if u < 2:
                    o(mul)
                    mul = V.tensor_tensor(STAT[:, 8:9], STAT[:, 8:9], CON[:, C_VIS:C_VIS + 1], ALU.mult)
                mul.then_inc(r_ready, 1)

            def values(i, u):
                n, br, hh = 6 * i + u, u // 2, u % 2
                dve.wait_ge(c_done, n + 1)
                dve.wait_ge(acc_free, 2 * (D_H + 4 * i + br + 1) + hh + 1)
                y = dyn(Y, 2 * i + hh)[:, :, 0:TP].rearrange("p o t -> p (o t)")
                if br == 0:
                    V.tensor_tensor(y, O[:, :], ZB[:, br, hh, 0:TP], ALU.mult).then_inc(o_used, 1)
                else:
                    V.tensor_tensor(TMP[:, :], O[:, :], ZB[:, br, hh, 0:TP], ALU.mult).then_inc(o_used, 1)
                    dve.wait_ge(o_used, n + 1)
                    o(V.tensor_tensor(y, y, TMP[:, :], ALU.add))

            def heads(i):
                for s in range(17):
                    if s < 16:
                        lo(Q_H + 4 * i + (s + 1) // 4, (s + 1) % 4)
                    if s >= 4 and s % 2 == 0 and s < 16:
                        softmax(i, (s - 4) // 2)
                        factor(i, (s - 4) // 2)
                    if s >= 8 and s % 2 == 0:
                        values(i, (s - 8) // 2)
                values(i, 5)
            looped(dve, o, 8, heads)

            dve.wait_ge(s_bd, 16 * 65)
            dve.wait_ge(s_dm, 1)
            for br in range(2):
                def keys(i, br=br):
                    for s in range(2):
                        pages_out(16 + 8 * br + 2 * i + s, s)
                looped(dve, o, 4, keys)
            dve.wait_ge(sd_pe, 1)
            o(V.tensor_tensor(SC[:, :], D[3][:, 0:NCMP], BCD[:, :], ALU.add))
            o(V.tensor_reduce(SST[:, 0:1], SC[:, :], AX.X, ALU.max))
            V.tensor_scalar(SST[:, 0:1], SST[:, 0:1], -1.0, None, ALU.mult).then_inc(sd_step, 1)
            dve.wait_ge(sd_exp, 1)
            o(V.reciprocal(SST[:, 8:9], SST[:, 4:5]))
            o(V.tensor_scalar(SC[:, :], SC[:, :], SST[:, 8:9], None, ALU.mult))
            for g in range(NKV):
                last = V.tensor_copy(PX[32 * g:32 * g + 32, NCMP * g:NCMP * g + NCMP], SC[32 * g:32 * g + 32, :])
            last.then_inc(sd_ev, 1)
            dve.wait_ge(sd_pe, 2)
            V.tensor_copy(PTC[:, :], S[0][0:NKV * NCMP, 0:P]).then_inc(sd_ev, 1)
            V.tensor_scalar(PX[:, :], PX[:, :], GD[:, 0:1], None, ALU.mult).then_inc(sd_ev, 1)
            dve.wait_ge(sd_pe, 3)
            V.tensor_copy(IMP[:, :], S[1][:, 0:9]).then_inc(sd_ev, 1)
            dve.wait_ge(sd_pe, 4)
            V.tensor_copy(PTG[:, :], S[0][0:NKV * NCMP, P:2 * P]).then_inc(sd_ev, 1)
            dve.wait_ge(sd_pe, 5)
            o(V.tensor_copy(DRP[:, 0, :], S[2][:, 1:8]))
            o(V.tensor_reduce(SST[:, 12:13], DRP[:, 0, :], AX.X, ALU.min))
            o(V.tensor_scalar(DRP[:, 1, :], DRP[:, 0, :], SST[:, 12:13], None, ALU.is_equal))
            o(V.tensor_tensor(DRP[:, 1, :], DRP[:, 1, :], CON[:, C_IOTA:C_IOTA + 7], ALU.mult))
            o(V.tensor_reduce(SST[:, 13:14], DRP[:, 1, :], AX.X, ALU.max))
            o(V.tensor_scalar(DRP[:, 2, :], DRP[:, 1, :], SST[:, 13:14], NEG, ALU.is_equal, ALU.mult))
            for br in range(2):
                o(V.tensor_tensor(SD[br][:, 0:512], D[br][:, :], BD[:, 0:512], ALU.add))
                o(V.tensor_tensor(SD[br][:, 512:513], D[2][:, br:br + 1], BD[:, 512:513], ALU.add))
                if br == 0:
                    blocks = SD[0][:, 64:512].rearrange("p (j n) -> p j n", j=7)
                    o(V.tensor_tensor(blocks, blocks, DRP[:, 2, :].unsqueeze(2).broadcast_to([P, 7, 64]), ALU.add))
                else:
                    o(V.tensor_scalar(SD[1][:, 0:1], SD[1][:, 0:1], NEG, None, ALU.add))
                o(V.tensor_reduce(SST[:, 1 + br:2 + br], SD[br][:, :], AX.X, ALU.max))
                V.tensor_scalar(SST[:, 1 + br:2 + br], SST[:, 1 + br:2 + br], -1.0, None, ALU.mult).then_inc(sd_step, 1)
            for br in range(2):
                dve.wait_ge(sd_exp, 2 + br)
                o(V.reciprocal(SST[:, 9 + br:10 + br], SST[:, 5 + br:6 + br]))
                o(V.tensor_tensor(SST[:, 9 + br:10 + br], SST[:, 9 + br:10 + br], GD[:, 1 + br:2 + br], ALU.mult))
                V.tensor_scalar(SD[br][:, :], SD[br][:, :], SST[:, 9 + br:10 + br], None, ALU.mult).then_inc(sd_ev, 1)
            for br in range(2):
                dve.wait_ge(sd_pe, 7)
                V.tensor_copy(flat(PTD[br][:, :, :]), S[br][:, :])
                V.tensor_copy(PTN[:, br, :], S[2][0:1, P * br:P * br + P]).then_inc(sd_ev, 1)
            dve.wait_ge(sd_pe, 8)
            V.tensor_copy(OD[0][:, :, :].rearrange("p b h -> p (b h)"), O[:, 0:P]).then_inc(sd_ev, 1)
            for br in range(2):
                def vals(i, br=br):
                    for s in range(2):
                        b = 2 * i + s
                        m = 8 * br + b
                        dve.wait_ge(pv, m + 1)
                        V.tensor_copy(dyn(OD[1 + br], b).rearrange("p o h -> p (o h)"), S[s][:, 0:NH]).then_inc(pve, 1)
                looped(dve, o, 4, vals)
            dve.wait_ge(pve, 16)
            dve.wait_ge(sd_ev, 10)
            yd = Y[:, :, TP:T]
            for br in range(NBR):
                dst = yd if br == 0 else OM[:, :, :]
                o(V.tensor_tensor(dst, OD[br][:, :, :].rearrange("p b h -> p h b"), SZD[:, br, :, :], ALU.mult))
                if br:
                    last = V.tensor_tensor(yd, yd, OM[:, :, :], ALU.add)
                    if br == 1:
                        o(last)
            last.then_inc(ydec, 1)
            for k in range(KT):
                y_lo(1, k)
            dve.wait_ge(s_xb, 16)
            looped(dve, o, 8, resid(1, Q_OB, D_OB), 1, 1)
            rstd(2)
            apply(3)
            for t in range(5):
                rows = P if t < NT else TS
                for k4 in range(4):
                    n = 4 * t + k4
                    dve.wait_ge(yn_tr, n + 1)
                    if t >= 2 and k4 == 0:
                        dve.wait_ge(yn_out[t % 2], 16 * (t // 2))
                    V.tensor_copy(YN[t % 2][0:rows, 512 * k4:512 * k4 + 512], S[n % 2][0:rows, :]).then_inc(yn_ready, 1)

        @block.tensor
        def _(pe):
            o = Own(pe, own["pe"])
            mm_, tr = nc.tensor.matmul, nc.tensor.transpose

            pe.wait_ge(s_con, 16)
            pe.wait_ge(s_rows, 16 * 7)
            tr(S[0][:, 0:80], VEC[:, :], ident[0:80, 0:80]).then_inc(s_t, 1)
            pe.wait_ge(s_csil, 1)
            for k in range(KT):
                last = tr(S[1][:, NC * k:NC * k + NC], CSIL[:, P * k:P * k + P], ident[0:NC, 0:NC])
            last.then_inc(s_t, 1)
            for t in range(5):
                rows = P if t < NT else TS
                pe.wait_ge(s_x[t % 2], 16 * (t // 2 + 1))
                for k4 in range(4):
                    pe.wait_ge(s_te, 4 * t + k4 + 1)
                    for k in range(4):
                        at = (4 * k4 + k) * P
                        last = tr(S[k4 % 2][:, P * k:P * k + rows], XN[t % 2][0:rows, at:at + P], ident[0:rows, 0:rows])
                    last.then_inc(s_t, 1)
            pe.wait_ge(s_rel, 32)
            pe.wait_ge(s_negrow, 1)
            for n in range(6):
                pe.wait_ge(s_te, 21 + n)
                at = (n // 3) * GLEN + (n % 3) * 512
                w = min(512, GLEN - (n % 3) * 512)
                mm_(S[n % 2][0:NH, 0:w], RELA[:, :], ONEH[:, at:at + w], start=True, stop=True).then_inc(s_t, 1)
            pe.wait_ge(s_te, 28)

            pe.wait_ge(s_cs, 2)

            def turn_rows(p, i, s, l):
                pe.wait_ge(mr_ready, p + 1)
                pe.wait_ge(s_brow[s], 16 * (i + 1 + 12 * l))
                wait(pe, mt_ready, p - 1)
                for h in range(2):
                    last = mm_(S[s][:, NC * h:NC * h + NC], MROW[0:19, s, P * h:P * h + P],
                               CON[0:19, C_SEL19:C_SEL19 + NC], start=True, stop=True)
                last.then_inc(tr_done, 1)

            def ada(l):
                def body(i):
                    for s in range(2):
                        p = 2 * i + s + 24 * l
                        wait(pe, mr_ready, p - 1)
                        for j in range(4):
                            pe.wait_ge(lo_ready, 4 * p + j + 1)
                            for kk in range(4):
                                k = 4 * j + kk
                                mm_(D[s][:, 0:256], CST[:, k, :], HI[j][:, kk, :], start=(k == 0), stop=False)
                                last = mm_(D[s][:, 0:256], CST[:, k, :], LO[j][:, kk, :], start=False, stop=(k == KT - 1))
                            last.then_inc(w_used, 1)
                            if j == 1 and not (isinstance(p, int) and p == 0):
                                turn_rows(p - 1, i - 1 + s, 1 - s, l)
                return body
            for l in range(2):
                looped(pe, o, 12, ada(l))
            turn_rows(47, 11, 1, 1)

            def stat(r, k, par):
                pe.wait_ge(sq_ready, KT * r + k + 1)
                first, end = isinstance(k, int) and k == 0, isinstance(k, int) and k == KT - 1
                for half in range(2):
                    last = mm_(S[half][:, 0:HT], ones, SQ[par][:, half * HT:(half + 1) * HT], start=first, stop=end)
                last.then_inc(sq_used, 1)

            def products(out, slot, kk, mm, hi_src, lo_src, k, first, end, n=P):
                cols_ = slice(mm * P, mm * P + n)
                for part, src in ((HI, hi_src), (HI, lo_src), (LO, hi_src)):
                    for half in range(2):
                        last = mm_(out[half][0:n, 0:HT], part[slot][:, kk, cols_], src[:, k, half * HT:(half + 1) * HT],
                                   start=(first and part is HI and src is hi_src), stop=(end and part is LO))
                return last

            def quad(q, d, j, ready=None):
                pe.wait_ge(lo_ready, 4 * q + j + 1)
                if ready is not None:
                    pe.wait_ge(ready[0], ready[1] + 4 * (j + 1))
                for mm in range(2):
                    if j == 0:
                        wait(pe, acc_free, 2 * d + mm - 1)
                    for kk in range(4):
                        last = products(D[2 * mm:2 * mm + 2], j % 2, kk, mm, HH, HL, 4 * j + kk, j == 0 and kk == 0, j == 3 and kk == 3)
                    if mm == 0 and j == 3:
                        last.then_inc(first_done, 1)
                last.then_inc(w_used, 1)

            def pairs(q0, d0, n, ready):
                def body(i):
                    for j in range(4):
                        quad(q0 + i, d0 + i, j, ready if isinstance(i, int) and i == 0 else None)
                looped(pe, o, n, body)

            pe.wait_ge(mt_ready, 48)
            for k in range(KT):
                stat(0, k, k % 2)
            pairs(Q_U, D_U, 8, (h_ready, 0))
            pe.wait_ge(acc_free, 16)
            pe.wait_ge(rms_ready, 1)
            for k4 in range(4):
                if k4 >= 2:
                    pe.wait_ge(s_ute, k4 - 1)
                for k in range(4):
                    last = tr(S[k4 % 2][0:23, P * k:P * k + P], Y[:, 4 * k4 + k, TP - PB:T], ident)
                last.then_inc(s_ut, 1)
            pe.wait_ge(s_sp, 16)
            for k in range(KT):
                last = mm_(O[:, 8 * k:8 * k + 8], SPN[:, P * k:P * k + P], CON[0:TS * PB, C_SELP + 8 * (k // 4):C_SELP + 8 * (k // 4) + 8],
                           start=True, stop=True)
            last.then_inc(s_ps, 1)
            pairs(Q_Z, D_Z, 8, None)
            for n in range(8):
                g = n // 2
                if n % 2 == 0:
                    pe.wait_ge(s_pl, g + 1)
                pe.wait_ge(lo_ready, 4 * Q_MIX + n + 1)
                for mm in range(2):
                    pe.wait_ge(acc_free, 2 * (D_MIX + n) + mm - 1)
                    for kk in range(4):
                        last = products(D[2 * mm:2 * mm + 2], n % 2, kk, mm, PHI[g % 2], PLO[g % 2], kk, kk == 0, kk == 3)
                    if mm == 0:
                        last.then_inc(first_done, 1)
                last.then_inc(w_used, 1)

            def resid_pairs(r, q0, d0, ready):
                def body(i):
                    for j in range(4):
                        quad(q0 + i, d0 + i, j, ready if isinstance(i, int) and i == 0 else None)
                        if j == 2 and not (isinstance(i, int) and i == 0):
                            for mm in range(2):
                                stat(r, 2 * (i - 1) + mm, mm)
                looped(pe, o, 8, body, 2, 1)
                for mm in range(2):
                    stat(r, 14 + mm, mm)
            resid_pairs(1, Q_OA, D_OA, (ys, 0))
            for i, src in enumerate((KCF, VCF, KS, VF, KW, VF)):
                pairs(Q_KV + 2 * i, D_KV + 2 * i, 2, (h_ready, KT) if i == 0 else None)
                pe.wait_ge(acc_free, 2 * (D_KV + 2 * i + 2))
                if i == 0:
                    pe.wait_ge(rms_ready, 2)
                for t in range(5):
                    rows = P if t < NT else TS
                    n = 5 * i + t
                    if n >= 2:
                        pe.wait_ge(tm_ready, n - 1)
                    for g in range(NKV):
                        last = tr(S[n % 2][0:rows, P * g:P * g + P], src[:, g, t * P:t * P + rows], ident)
                    last.then_inc(kv_tr, 1)

            pe.wait_ge(s_cw, 16 * 4)
            pe.wait_ge(s_cw1, 16 * 2)
            pe.wait_ge(tm_ready, 30)
            for kv in range(2):
                tr(S[kv][:, 0:CL], PE_[kv][:, :], ident[0:CL, 0:CL]).then_inc(s_pe, 1)
            for kv in range(2):
                pe.wait_ge(s_pee, kv + 1)
                for l in range(CL):
                    last = mm_(O[:, kv:kv + 1], W1[kv][:, l, :], PET[kv][:, l:l + 1], start=(l == 0), stop=(l == CL - 1))
            last.then_inc(s_pe, 1)
            pe.wait_ge(s_pee, 3)

            def turn_pages(n, slot):
                for g in range(NKV):
                    wait(pe, ctre[g % 2], 2 * n + g // 2)
                    for t in range(NPG):
                        last = tr(S[g % 2][:, P * t:P * t + P], PG[slot][:, t, P * g:P * g + P], ident)
                    last.then_inc(ctr, 1)

            def hidden(n, kv, src, peeled=False):
                wait(pe, csr, n)
                for l in range(CL):
                    at = [src[:, :, l:l + 16 * (NCMP - 1) + 1:16]]
                    last = mm_(S[2][:, 0:NKV * NCMP], W1[kv][:, l, :], at[0], start=(l == 0), stop=(l == CL - 1))
                last.then_inc(cw1, 1)

            def second(n, kv, prompt=False):
                pe.wait_ge(csr, n + 1)
                wait(pe, cout, n)
                if kv == 0:
                    last = mm_(O[:, 0:NKV * NCMP], W2[0][:, :], CSIL2[0][:, :], start=True, stop=True)
                elif not prompt:
                    last = mm_(O[0:NKV * NCMP, 0:P], CSIL2[1][:, :], W2[1][:, :], start=True, stop=True)
                else:
                    for g in range(NKV):
                        last = mm_(O[0:NCMP, P * g:P * g + P], CSIL2[1][:, NCMP * g:NCMP * g + NCMP], W2[1][:, :], start=True, stop=True)
                last.then_inc(cw2, 1)

            def compress(b):
                for kv in range(2):
                    n = 2 * b + kv
                    pe.wait_ge(s_pg[kv], 64 * (b + 1))
                    turn_pages(n, kv)
                    for c in ctre:
                        pe.wait_ge(c, 2 * n + 2)
                    hidden(n, kv, RT_T[kv])
                    second(n, kv)
            looped(pe, o, TS, compress)
            for kv in range(2):
                hidden(16 + kv, kv, KCF if kv == 0 else VCF)
                second(16 + kv, kv, True)

            for j in range(4):
                pe.wait_ge(lo_ready, 4 * Q_G + j + 1)
                pe.wait_ge(h_ready, 2 * KT + 4 * (j + 1))
                for kk in range(4):
                    last = products(D[0:2], j % 2, kk, 0, HH, HL, 4 * j + kk, j == 0 and kk == 0, j == 3 and kk == 3)
                    if j == 3 and kk == 2:
                        last.then_inc(first_done, 1)
                last.then_inc(w_used, 1)
            pe.wait_ge(acc_free, 2 * (D_G + 1))
            pe.wait_ge(cout, 18)
            for t in range(NT):
                last = tr(S[0][:, 48 * t:48 * t + 48], GF[:, P * t:P * t + P], ident[0:48, 0:48])
            last.then_inc(g_tr, 1)
            pe.wait_ge(gt_ready, 1)

            def scores(i, u):
                n, br, hh = 6 * i + u, u // 2, u % 2
                g = i // 2
                if u == 0:
                    pe.wait_ge(acc_free, 2 * (D_H + 4 * i + 1))
                    pe.wait_ge(hd_in, 80 * (i + 1))
                wait(pe, pt_ready, n)
                qs = lambda t: QS[:, hh, P * t:P * t + P]
                if br == 0:
                    at = g * NCMP
                    kc = KCP[:, bass.ds(at, NCMP)] if not isinstance(at, int) else KCP[:, at:at + NCMP]
                    for t in range(NT):
                        out = S[0][:, NCMP * t:NCMP * t + NCMP]
                        mm_(out, BC[:, hh, P * t:P * t + P], ident[0:NCMP, 0:NCMP], start=True, stop=False)
                        last = mm_(out, qs(t), kc, start=False, stop=True)
                else:
                    kt_ = KS if br == 1 else KW
                    kt_ = dyn(kt_, g)
                    where = (S[1][:, 384:512], S[2][:, 0:256], S[1][:, 0:384], S[0][:, :])
                    for t in (3, 2, 1, 0):
                        last = mm_(where[t], qs(t), kt_[:, :, 0:P * (t + 1)].rearrange("p o t -> p (o t)"), start=True, stop=True)
                last.then_inc(a_done, 1)

            W_AT = [0, 1, 3, 6]

            def turn(i, u):
                n = 6 * i + u
                pe.wait_ge(p_ready, n + 1)
                if u < 2:
                    for t in range(NT):
                        last = tr(S[0][0:NCMP, P * t:P * t + P], PR[:, NCMP * t:NCMP * t + NCMP], ident)
                else:
                    for b, at, j in ((0, 0, 0), (1, 0, 1), (1, 3, 3), (2, 0, 2)):
                        for t in range(j, NT):
                            c = (at + t - j) * P
                            src = (W_AT[t] + j) * P
                            last = tr(S[b][:, c:c + P], PR[:, src:src + P], ident)
                last.then_inc(b_done, 1)

            def values(i, u):
                n, br = 6 * i + u, u // 2
                pe.wait_ge(pt_ready, n + 1)
                wait(pe, o_used, n)
                if br == 0:
                    last = mm_(O[:, :], VCG[:, :], PT[0:NCMP, 0:512], start=True, stop=True)
                else:
                    for j, at in ((0, 0), (1, 512), (2, 1024), (3, 512 + 384)):
                        last = mm_(O[:, P * j:512], VG[:, br - 1, j, :], PT[:, at:at + 512 - P * j], start=(j == 0), stop=(j == 3),
                                   skip_group_check=True)
                last.then_inc(c_done, 1)

            def heads(i):
                for s in range(16):
                    quad(Q_H + 4 * i + s // 4, D_H + 4 * i + s // 4, s % 4)
                    if s >= 6 and s % 2 == 0:
                        values(i, (s - 6) // 2)
                    if s >= 4 and s % 2 == 0:
                        u = (s - 4) // 2
                        if u < 6:
                            turn(i, u)
                    if s >= 3 and s % 2 == 1:
                        u = (s - 3) // 2
                        if u < 6:
                            scores(i, u)
                values(i, 5)
            looped(pe, o, 8, heads)

            pe.wait_ge(s_dm, 1)
            pe.wait_ge(acc_free, 2 * D_OB)
            for b in range(4):
                last = mm_(D[b][:, :], ZERO[:, :], Y[:, 0, 0:512], start=True, stop=(b < 0), skip_group_check=True)
            last.then_inc(dsc, 2)
            for br in range(2):
                def keys(i, br=br):
                    for s in range(4):
                        b = 4 * i + s
                        m = 8 * br + b
                        base = 512 if s < 2 else 0
                        pe.wait_ge(s_pg[s], base + 64 * (i + 1) if br == 0 else base + 128 + 16 * (i + 1))
                        turn_pages(16 + m, s)
                        pe.wait_ge(qp_ready, m + 1)
                        for c in ctre:
                            pe.wait_ge(c, 32 + 2 * m + 2)
                        pe.wait_ge(kst, m + 1)
                        for g in range(NKV):
                            r = slice(32 * g, 32 * g + 32)
                            q = QPAD[s % 2][:, g, :]
                            mm_(D[br][r, :], q, RT_T[s % 2][:, g, :], start=False, stop=False, skip_group_check=True)
                            last = mm_(D[2][r, br:br + 1], q, KN[s % 2][:, g:g + 1], start=False, stop=False, skip_group_check=True)
                            if br == 0:
                                last = mm_(D[3][r, 0:NCMP], q, KCB[s % 2][:, NCMP * g:NCMP * g + NCMP], start=False, stop=False, skip_group_check=True)
                        last.then_inc(dsc, 1)
                looped(pe, o, 2, keys)
            for b in range(4):
                last = mm_(D[b][:, :], ZERO[:, :], Y[:, 0, 0:512], start=False, stop=True, skip_group_check=True)
            last.then_inc(sd_pe, 1)
            pe.wait_ge(sd_ev, 1)
            tr(S[0][0:NKV * NCMP, 0:P], PX[:, :], ident).then_inc(sd_pe, 1)
            pe.wait_ge(sd_ev, 2)
            mm_(S[1][:, 0:9], PTC[:, :], CON[0:NKV * NCMP, C_OVL:C_OVL + 9], start=True, stop=True).then_inc(sd_pe, 1)
            pe.wait_ge(sd_ev, 3)
            tr(S[0][0:NKV * NCMP, P:2 * P], PX[:, :], ident).then_inc(sd_pe, 1)
            pe.wait_ge(sd_ev, 4)
            mm_(S[2][:, 0:9], CON[:, C_RSUM:C_RSUM + P], IMP[:, :], start=True, stop=True).then_inc(sd_pe, 1)
            for br in range(2):
                pe.wait_ge(sd_ev, 6 + br)
                for t in range(NPG):
                    tr(S[br][:, P * t:P * t + P], SD[br][:, P * t:P * t + P], ident)
                tr(S[2][0:1, P * br:P * br + P], SD[br][:, 512:513], ident).then_inc(sd_pe, 1)
            for b in range(TS):
                last = mm_(O[:, NH * b:NH * b + NH], VCS[:, b, :], PTG[:, :].rearrange("p (g n) -> p g n", g=NKV)[:, :, 4 * b:4 * b + 4],
                           start=True, stop=True)
            last.then_inc(sd_pe, 1)
            pe.wait_ge(sd_ev, 9)
            for br in range(2):
                def vals(i, br=br):
                    for s in range(4):
                        b = 4 * i + s
                        m = 8 * br + b
                        base = 512 if s < 2 else 0
                        pe.wait_ge(s_pg[s], base + 160 + 64 * (i + 1) if br == 0 else base + 288 + 16 * (i + 1))
                        pe.wait_ge(s_vn[s % 2], 16 * (4 * br + 2 * i + s // 2 + 1))
                        wait(pe, pve, m - 1)
                        for g in range(NKV):
                            out = S[s % 2][:, 4 * g:4 * g + 4]
                            at = b * 4 + 32 * g
                            for t in range(NPG):
                                rhs = PTD[br][:, t, bass.ds(at, 4)] if not isinstance(at, int) else PTD[br][:, t, at:at + 4]
                                mm_(out, PG[s][:, t, P * g:P * g + P], rhs, start=(t == 0), stop=False)
                            rhs = PTN[:, br, bass.ds(at, 4)] if not isinstance(at, int) else PTN[:, br, at:at + 4]
                            last = mm_(out, VN[s % 2][:, P * g:P * g + P], rhs, start=False, stop=True)
                        last.then_inc(pv, 1)
                looped(pe, o, 2, vals)

            resid_pairs(2, Q_OB, D_OB, (ys, KT))
            pe.wait_ge(rms_ready, 3)
            pe.wait_ge(hf_ready, 4 * KT)
            for t in range(5):
                rows = P if t < NT else TS
                for k4 in range(4):
                    n = 4 * t + k4
                    if n >= 2:
                        pe.wait_ge(yn_ready, n - 1)
                    for k in range(4):
                        last = tr(S[n % 2][0:rows, P * k:P * k + P], X[:, 4 * k4 + k, t * P:t * P + rows], ident)
                    last.then_inc(yn_tr, 1)


_OUTS = [(1, 512, 2048), (8, 1, 2048), (1, 1, 15, 2048)] + [(1, 512, 4, 128)] * 6 + \
    [(1, 8, 15, 2048)] + [(8, 1, 4, 128)] * 4 + [(8, 512, 4, 128)] * 2


def kernel(**inputs):
    import concourse.bacc as bacc
    from concourse.bass_utils import run_bass_kernel_spmd

    nc = bacc.Bacc("TRN2", target_bir_lowering=False, num_devices=1)
    arrays = {n: np.ascontiguousarray(a) for n, a in inputs.items()}
    arrays["consts"] = shape_constants()
    arrays["onehots"] = bucket_onehots()
    ins = {n: nc.dram_tensor(f"in_{n}", a.shape, mybir.dt.from_np(a.dtype), kind="ExternalInput").ap() for n, a in arrays.items()}
    outs = [nc.dram_tensor(f"out_{i}", s, F32, kind="ExternalOutput").ap() for i, s in enumerate(_OUTS)]
    build(nc, ins, outs)
    r = run_bass_kernel_spmd(nc, [{f"in_{n}": a for n, a in arrays.items()}], core_ids=[0])
    return tuple(r.results[0][f"out_{i}"] for i in range(len(_OUTS)))
```

```python
from contextlib import ExitStack

import numpy as np
import concourse.bass as bass
from concourse import mybir

F32 = mybir.dt.float32
F32R = mybir.dt.float32r
I32 = mybir.dt.int32
ALU = mybir.AluOpType
ACT = mybir.ActivationFunctionType
AX = mybir.AxisListType

P = 128
DM = 2048
KT = DM // P
TP, TS = 512, 8
T = TP + TS
HT = T // 2
NT = TP // P
ML = 48
NC = 9
NH, NKV, REP, HD = 16, 4, 4, 128
NBR = 3
PB = 15
WINDOWS = (2, 4, 8, 16)
NCMP = 31
CL, CS_ = 32, 16
NPG = 4
GLEN = 1025
SCALE = float(HD) ** -0.5
EPS = 1e-6
NEG = -1e30

C_ID, C_ONE, C_RSUM, C_CNT, C_SELP, C_SEL19, C_OVL, C_IOTA, C_VIS, C_EPS, C_MSK, C_ROW, C_PER = 0, 128, 256, 384, 448, 480, 489, 498, 505, 506, 507, 571, 579
NCONST = 579 + 2


def shape_constants():
    c = np.zeros((P, NCONST), np.float32)
    c[:, C_ID:C_ID + P] = np.eye(P)
    c[:, C_ONE:C_ONE + P] = 1.0
    row = np.arange(P)
    same = (row[:, None] // 4) == (row[None, :] // 4)
    c[:, C_RSUM:C_RSUM + P] = same
    for g, w in enumerate(WINDOWS):
        c[:, C_CNT + 16 * g:C_CNT + 16 * g + 16] = 1.0 / np.minimum(np.arange(16) + 1, w)
        for b in range(TS):
            for t in range(PB):
                c[b * PB + t, C_SELP + 8 * g + b] = float(t >= PB + 1 - w)
    for j in range(NC):
        c[j, C_SEL19 + j] = c[NC + j, C_SEL19 + j] = 1.0
    c[2 * NC, C_SEL19:C_SEL19 + NC] = 1.0
    for g in range(NKV):
        for n in range(NCMP):
            for j in range(9):
                o = min(16 * n + 32, 64 * j + 64) - max(16 * n, 64 * j)
                c[g * NCMP + n, C_OVL + j] = max(o, 0) / CL
    c[:, C_IOTA:C_IOTA + 7] = np.arange(1, 8)
    c[:, C_VIS] = row >= CL - 1
    c[:, C_EPS] = EPS
    c[:, C_MSK:C_MSK + 64] = np.eye(8).reshape(1, 64)
    c[:, C_ROW:C_ROW + TS] = (row[:, None] % 32) // 4 == np.arange(TS)[None, :]
    for r in range(0, P, 32):
        c[r, C_PER + r // 64] = 1.0
    return c


def bucket_onehots():
    d = np.arange(512, -513, -1)
    df = np.maximum(d, 16).astype(np.float32)
    large = 16 + (np.log(df / np.float32(16)) / np.float32(np.log(128 / 16)) * np.float32(16)).astype(np.int32)
    bucket = np.where(d < 16, np.maximum(d, 0), np.minimum(large, 31))
    bucket = np.where(d < 0, 32, bucket)
    fall = (np.arange(33)[:, None] == bucket[None, :]).astype(np.float32)
    return np.concatenate([fall, fall[:, ::-1]], axis=1)


def wait(eng, sem, value):
    if not (isinstance(value, int) and value <= 0):
        eng.wait_ge(sem, value)


class Own:

    def __init__(self, eng, sem):
        self.eng, self.sem, self.base, self.n = eng, sem, 0, 0

    def __call__(self, ins):
        self.n += 1
        ins.then_inc(self.sem, 1)
        self.eng.wait_ge(self.sem, self.base + self.n)

    def turn(self, i, body):
        if isinstance(i, int) and i == 0:
            self.start = self.base + self.n
            self.base, self.n = self.start, 0
            body(i)
            self.per = self.n
            self.base, self.n = self.start + self.per, 0
        else:
            self.base, self.n = self.start + i * self.per, 0
            body(i)
            assert self.n == self.per

    def ended(self, turns):
        self.base, self.n = self.start + turns * self.per, 0


def looped(eng, own, turns, body, head=1, tail=0):
    for i in range(head):
        own.turn(i, body)
    if turns > head + tail:
        with eng.Fori(head, turns - tail) as i:
            own.turn(i, body)
    for i in range(turns - tail, turns):
        own.turn(i, body)
    own.ended(turns)


Q_ADA, Q_U, Q_Z, Q_MIX, Q_OA, Q_KV, Q_G, Q_H, Q_OB = 0, 48, 56, 64, 66, 74, 86, 87, 119
D_U, D_Z, D_MIX, D_OA, D_KV, D_G, D_H, D_OB = 0, 8, 16, 24, 32, 44, 45, 77
Q_END = 127


def ahead(q):
    return [(q, 1), (q, 2), (q, 3), (q + 1, 0)]


def build(nc, ins, outs):
    A = ins
    (y_prompt, y_sample, pool_p, k_cmp_p, v_cmp_p, k_slc_p, v_slc_p, k_win_p, v_win_p,
     pool_s, k_cmp_s, v_cmp_s, k_slc_s, v_slc_s, k_win_s, v_win_s) = outs

    with ExitStack() as ctx:
        def sem(name):
            return ctx.enter_context(nc.semaphore(name))

        def dram(name, shape):
            return nc.dram_tensor(name, shape, F32, kind="Internal").ap()

        BASE = 16512
        cursor = [BASE]

        def place(name, shape, dt=F32):
            n = int(np.prod(shape[1:])) * 4
            t = nc.alloc_sbuf_tensor_at(name, list(shape), dt, offset=cursor[0])
            cursor[0] += (n + 31) // 32 * 32
            return t

        RAW = [place(f"raw{i}", [P, 4, 256]) for i in range(4)]
        HI = [place(f"w_hi{i}", [P, 4, 256], F32R) for i in range(2)]
        LO = [place(f"w_lo{i}", [P, 4, 256], F32R) for i in range(2)]
        CON = place("consts", [P, NCONST])
        MODT = place("modT", [P, 2 * ML, NC])
        AMOD = place("a_mod", [P, 2, KT, NC])
        VECT = place("vecT", [P, 80])
        PTAB = place("page_tab", [1, 32], I32)
        h_at = cursor[0]
        HH = place("h_hi", [P, KT, T], F32R)
        HL = place("h_lo", [P, KT, T], F32R)
        h_end = y_at = cursor[0]
        Y = place("y", [P, KT, T])
        x_at = cursor[0]
        X = place("x", [P, KT, T])
        c_at = cursor[0]
        END = 229368

        cursor[0] = h_at
        CROW = place("c_rows", [NC, DM])
        CSIL = place("c_silu", [NC, DM])
        XN = [place(f"x_nat{i}", [P, DM]) for i in range(2)]
        VEC = place("vec_rows", [80, P])
        RELA = place("rel_rows", [33, NH])
        ONEH = place("onehots", [33, 2 * GLEN])
        GROW = place("bias_rows", [NH, 2 * GLEN])
        assert cursor[0] <= h_end
        cursor[0] = y_at
        CST = place("c_split", [P, KT, P], F32R)
        CTF = place("c_cols", [P, KT, NC])
        MROW = place("mod_rows", [19, 2, 256])
        RAW += [place(f"raw{i}", [P, 4, 256]) for i in range(4, 8)]
        SQ0 = [place(f"squares_x{i}", [P, T]) for i in range(2)]
        assert cursor[0] <= x_at
        cursor[0] = c_at
        HI += [place(f"w_hi{i}", [P, 4, 256], F32R) for i in range(2, 4)]
        LO += [place(f"w_lo{i}", [P, 4, 256], F32R) for i in range(2, 4)]
        cursor[0] = c_at
        SQ = [place(f"squares{i}", [P, T]) for i in range(2)]
        TN = [place(f"normed{i}", [P, T]) for i in range(2)]
        HF = [place(f"h_full{i}", [P, T]) for i in range(3)]
        RMS = nc.alloc_sbuf_tensor_at("rms", [P, T], F32, offset=cursor[0] - T * 4)
        c_norm_end = cursor[0]
        RSTD = nc.alloc_sbuf_tensor_at("rstd", [P, T], F32, offset=(END - 2112) // 32 * 32)
        c_top = (END - 2112) // 32 * 32
        assert cursor[0] <= c_top
        cursor[0] = c_at
        PHI = [place("pooled_hi0", [P, 4, T], F32R)]
        PLO = [place("pooled_lo0", [P, 4, T], F32R)]
        PHI += [place("pooled_hi1", [P, 4, T], F32R)]
        PLO += [place("pooled_lo1", [P, 4, T], F32R)]
        assert cursor[0] <= END, cursor[0]
        cursor[0] = c_at + 2 * 4 * T * 4
        SPN = place("state_rows", [TS * PB, DM])
        PAD = [place(f"window_sum{i}", [P, 16 + TP]) for i in range(2)]
        STMP = place("sample_tmp", [P, 4, TS])
        assert cursor[0] <= END, cursor[0]
        UT = nc.alloc_sbuf_tensor_at("u_rows", [23, DM], F32, offset=c_at)
        cursor[0] = c_at
        cursor[0] = c_at + 2 * T * 4
        RT = [place(f"resid_tmp{i}", [P, TS]) for i in range(2)]
        ZS = nc.alloc_sbuf_tensor_at("z_pool", [P, KT, T], F32, offset=x_at)
        cursor[0] = c_norm_end
        KS = place("k_slc_T", [P, NKV, T])
        KW = place("k_win_T", [P, NKV, T])
        KCP = place("kc_prompt_T", [P, NKV * NCMP])
        KCS = place("kc_sample_T", [P, TS, NKV * NCMP])
        assert cursor[0] <= c_top, (cursor[0], c_top)
        keep_end = cursor[0]
        VCS = nc.alloc_sbuf_tensor_at("vc_sample", [NKV * NCMP, TS, P], F32, offset=c_at)
        cursor[0] = y_at
        KCF = place("k_cmp_T", [P, NKV, T])
        VCF = place("v_cmp_T", [P, NKV, T])
        VF = place("v_T", [P, NKV, T])
        TM = [place(f"token_rows{i}", [P, 512]) for i in range(4)]
        assert cursor[0] <= x_at
        cursor[0] = h_at
        W1 = [place(f"w_c1_{i}", [P, CL, P]) for i in range(2)]
        PG = [place(f"pages{i}", [P, NPG, 512]) for i in range(2)]
        RT_T = [place(f"rows_T{i}", [P, NKV, TP]) for i in range(2)]
        CSIL2 = [place(f"c_hidden{i}", [P, NKV * NCMP]) for i in range(2)]
        assert cursor[0] <= h_end, (cursor[0], h_end)
        VCP = nc.alloc_sbuf_tensor_at("vc_prompt", [NCMP, NKV, P], F32, offset=y_at + 2 * NKV * T * 4)
        cursor[0] = c_at + TS * P * 4
        W2 = [place(f"w_c2_{i}", [P, P]) for i in range(2)]
        PE_ = [place(f"pe{i}", [CL, P]) for i in range(2)]
        PET = [place(f"pe_T{i}", [P, CL]) for i in range(2)]
        PEC = place("pe_term", [P, 2])
        PER = place("pe_term_rows", [P, P])
        assert cursor[0] <= c_norm_end
        cursor[0] = x_at
        PR = place("probs", [P, 1280])
        PT = place("probs_T", [P, 1280])
        VG = place("v_group", [P, 2, NT, P])
        BH = place("bias_heads", [P, 2, 512])
        ZB = place("z_silu", [P, NBR, 2, T])
        TMP = place("o_times_z", [P, TP])
        assert cursor[0] <= c_at
        cursor[0] = c_at + TS * P * 4
        QS = place("q_heads", [P, 2, TP])
        BC = place("bias_cmp", [NCMP, 2, TP])
        VCG = place("vc_group", [NCMP, P])
        GT = place("gate_rows", [P, NT, 48])
        assert cursor[0] <= c_norm_end, (cursor[0], c_norm_end)
        cursor[0] = keep_end
        SZD = place("z_silu_sample", [P, NBR, NH, TS])
        QD = place("q_sample", [P, NH, TS])
        STAT = place("row_stats", [P, 16])
        GF = nc.alloc_sbuf_tensor_at("gates_T", [48, T], F32, offset=y_at)
        assert cursor[0] <= END, cursor[0]
        cursor[0] = h_at
        cursor[0] = h_at
        QPAD = [place(f"q_one_sample{i}", [P, NKV, 32]) for i in range(2)]
        KN = [place(f"k_new{i}", [P, NKV]) for i in range(2)]
        KCB = [place(f"kc_one_sample{i}", [P, NKV * NCMP]) for i in range(2)]
        PTD = [place(f"probs_T_sample{i}", [P, NPG, P]) for i in range(2)]
        PTN = place("probs_T_new", [TS, 2, P])
        PNEW = [place(f"probs_new{i}", [P, TS]) for i in range(2)]
        PTC = place("probs_T_cmp", [NKV * NCMP, P])
        PTG = place("probs_T_cmp_gated", [NKV * NCMP, P])
        SD = [place(f"scores_sample{i}", [P, 513]) for i in range(2)]
        SC = place("scores_cmp", [P, NCMP])
        PX = place("probs_cmp_spread", [P, NKV * NCMP])
        BD = place("bias_sample", [P, 513])
        BCD = place("bias_cmp_sample", [P, NCMP])
        IMP = place("importance", [P, 9])
        DRP = place("dropped", [P, 3, 7])
        GD = place("gates_sample", [P, NBR])
        SST = place("sample_stats", [P, 16])
        OD = [place(f"o_sample{i}", [P, TS, NH]) for i in range(NBR)]
        OM = place("o_sample_tmp", [P, NH, TS])
        ZERO = place("zeros", [P, P])
        assert cursor[0] <= h_at + 2 * CL * P * 4, cursor[0] - h_at
        cursor[0] = x_at
        PG += [place(f"pages{i}", [P, NPG, 512]) for i in range(2, 4)]
        VN = [place(f"v_new{i}", [TS, 512]) for i in range(2)]
        PPAD = [place(f"probs_T_one_sample{i}", [P, NPG, P]) for i in range(2)]
        ACC = [place(f"o_rows_sample{i}", [P, P]) for i in range(2)]
        assert cursor[0] <= c_at
        cursor[0] = y_at
        cursor[0] = h_at
        YN = [place(f"y_rows{i}", [P, DM]) for i in range(5)]
        assert cursor[0] <= h_end

        def bank(name):
            return ctx.enter_context(nc.psum_tensor(name, [P, 512], F32))

        D = [bank(f"acc{i}") for i in range(4)]
        S = [bank(f"work{i}") for i in range(3)]
        O = bank("out_acc")

        g_scr = dram("g_scr", (NH, 2 * GLEN))
        b_scr = dram("b_scr", (NH, P, 512))
        c_scr = dram("c_scr", (NH, NCMP, TP))
        x_scr = dram("x_scr", (P, KT * T))
        vc_scr = dram("vc_scr", (NCMP, NKV * P))
        gd_scr = dram("gd_scr", (NBR, P))
        bd_scr = dram("bd_scr", (P, 513))
        bcd_scr = dram("bcd_scr", (P, NCMP))

        ident = CON[:, C_ID:C_ID + P]
        ones = CON[:, C_ONE:C_ONE + P]

        raw_full = [sem(f"raw_full{i}") for i in range(8)]
        hi_ready = sem("hi_ready")
        lo_ready = sem("lo_ready")
        w_used = sem("w_used")
        first_done = sem("first_tile_done")
        acc_free = sem("acc_free")
        own = {e: sem(f"own_{e}") for e in ("act", "dve", "pool", "pe")}
        s_con = sem("consts_in")
        s_rows = sem("setup_rows_in")
        s_x = [sem(f"x_rows_in{i}") for i in range(2)]
        s_rel = sem("rel_in")
        s_negrow = sem("neg_row")
        s_t = sem("setup_transposed")
        s_te = sem("setup_copied")
        s_csil = sem("c_silu_done")
        s_cz = sem("c_split_zero")
        s_cs = sem("c_split_done")
        s_gscr = sem("bias_rows_out")
        s_bscr = sem("bias_tables_out")
        mr_ready = sem("mod_rows_ready")
        s_brow = [sem(f"b_row_in{i}") for i in range(2)]
        tr_done = sem("mod_turned")
        mt_ready = sem("mod_ready")
        amod = sem("a_mod_ready")
        sq_ready = sem("square_ready")
        sq_used = sem("square_used")
        rms_ready = sem("rms_ready")
        rstd_ready = sem("rstd_ready")
        tn_ready = sem("normed_ready")
        hf_ready = sem("h_full_ready")
        hfs_ready = sem("h_full_samples_ready")
        hhi_ready = sem("h_hi_ready")
        h_ready = sem("h_ready")
        s_sp = sem("state_rows_in")
        s_ut = sem("u_turned")
        s_ute = sem("u_rows_ready")
        s_uo = sem("u_rows_out")
        s_ps = sem("prefix_sums")
        s_pooled = sem("pooled_ready")
        s_pooled_s = sem("pooled_samples_ready")
        s_x0 = sem("x_first_out")
        s_x1 = sem("x_first_back")
        s_ph = sem("pooled_hi_ready")
        s_pl = sem("pooled_split")
        kv_copied = sem("kv_tiles_copied")
        kv_tr = sem("kv_turned")
        tm_ready = sem("token_rows_ready")
        tm_out = [sem(f"token_rows_out{i}") for i in range(4)]
        s_copy = sem("states_copied")
        s_cw = sem("small_compress_weights_in")
        s_cw1 = sem("compress_weights_in")
        s_pt = sem("page_table_in")
        s_pe = sem("pe_turned")
        s_pee = sem("pe_copied")
        s_pez = sem("pe_rows_cleared")
        s_pg = [sem(f"pages_in{i}") for i in range(4)]
        ctr = sem("pages_turned")
        ctre = [sem(f"pages_turned_copied{i}") for i in range(2)]
        cw1 = sem("hidden_done")
        csr = sem("hidden_silu_done")
        cw2 = sem("compressed_done")
        cout = sem("compressed_copied")
        s_vcp = sem("vc_prompt_out")
        s_xs = sem("x_spilled")
        g_tr = sem("gates_turned")
        gt_ready = sem("gate_rows_ready")
        s_gd = sem("gates_sample_out")
        hd_in = sem("head_data_in")
        q_ready = sem("q_ready")
        z_ready = sem("z_ready")
        a_done = sem("scores_done")
        negm = sem("max_ready")
        e_done = sem("exp_done")
        r_ready = sem("row_factor_ready")
        p_ready = sem("probs_ready")
        b_done = sem("probs_turned")
        pt_ready = sem("probs_T_ready")
        pt2_ready = sem("probs_T_rest_ready")
        c_done = sem("values_done")
        o_used = sem("values_used")
        s_dm = sem("sample_consts_ready")
        s_bd = sem("sample_bias_in")
        s_bds = sem("sample_bias_rows_out")
        qp_ready = sem("q_one_sample_ready")
        kst = sem("sample_keys_staged")
        dsc = sem("sample_scores_done")
        sd_step = sem("sample_softmax_step")
        sd_exp = sem("sample_exp")
        sd_pe = sem("sample_pe_step")
        sd_ev = sem("sample_copied")
        s_vn = [sem(f"v_new_in{i}") for i in range(2)]
        pv = sem("sample_values_done")
        pp_ready = sem("one_sample_probs_ready")
        ydec = sem("y_sample_ready")
        ys_hi = sem("y_hi_ready")
        ys = sem("y_split")
        s_xb = sem("x_back")
        yn_tr = sem("y_turned")
        yn_ready = [sem(f"y_rows_ready{i}") for i in range(2)]
        yn_out = sem("y_rows_out")

        def vec(v, k):
            return VECT[:, v * KT + k:v * KT + k + 1]

        def halves(ap):
            return [ap[:, 0:HT], ap[:, HT:T]]

        def dyn(t, i, n=1):
            return t[:, bass.ds(i, n)] if not isinstance(i, int) else t[:, i:i + n]

        def flat(ap):
            return ap.rearrange("p a n -> p (a n)")

        def cols(w, j, at, n=256):
            w = w.rearrange("(k p) n -> p k n", p=P)[:, 4 * j:4 * j + 4]
            return w[:, :, bass.ds(at, n)] if not isinstance(at, int) else w[:, :, at:at + n]

        w_a, w_oa, w_kv, w_b, w_ob = A["w_in_a"][0], A["w_out_a"][0], A["w_kv"], A["w_in_b"][0], A["w_out_b"][0]
        kv_out_p = [x[0].rearrange("t g d -> t (g d)") for x in (k_cmp_p, v_cmp_p, k_slc_p, v_slc_p, k_win_p, v_win_p)]
        kv_out_s = [x[:, x.shape[1] - 1].rearrange("b g d -> b (g d)") for x in (k_cmp_s, v_cmp_s, k_slc_s, v_slc_s, k_win_s, v_win_s)]

        block = ctx.enter_context(nc.Block())

        @block.sync
        def _(sp):
            o = Own(sp, own["pe"])

            def load(q, j, src, n=256):
                wait(sp, lo_ready, 4 * q + j - 3)
                sp.dma_start(RAW[j][:, :, 0:n], src).then_inc(raw_full[j], 16)

            def quads(q0, w, n, at=lambda i: i * 256, first=0):
                def body(i):
                    if not (isinstance(i, int) and i < first):
                        for j in range(4):
                            load(q0 + i, j, cols(w, j, at(i)))
                looped(sp, o, n, body)

            for l in range(2):
                def ada(i, l=l):
                    for s in range(2):
                        for j in range(4):
                            wait(sp, lo_ready, 4 * (2 * i + s + 24 * l) + j - 7)
                            sp.dma_start(RAW[4 * s + j][:, :, :], cols(A["w_ada"][l], j, (2 * i + s) * 256)).then_inc(raw_full[4 * s + j], 16)
                looped(sp, o, 12, ada)
            quads(Q_U, w_a, 8)
            quads(Q_Z, w_a, 8, lambda i: DM + i * 256)
            for g in range(4):
                for c in range(2):
                    load(Q_MIX + g // 2, 2 * (g % 2) + c, cols(A["w_grp"][0][g], 0, 256 * c))
            quads(Q_OA, w_oa, 8)
            quads(Q_KV, w_kv, 12)
            for j in range(4):
                load(Q_G, j, cols(w_b, j, 4 * DM, 48), 48)

            sp.wait_ge(w_used, 4 * Q_G)
            sp.wait_ge(s_pt, 16)

            def page_loads(i, b, free, value, cache):
                page = [sp.value_load(PTAB[0:1, bass.ds(b * NPG + t, 1)], min_val=0, max_val=cache.shape[0] - 1) for t in range(NPG)]
                wait(sp, free, value)
                for t in range(NPG):
                    sp.dma_start(PG[i][:, t, :], cache[bass.ds(page[t], 1)].rearrange("o t g d -> (o t) (g d)")).then_inc(s_pg[i], 16)

            def pages(b):
                for kv, cache in enumerate((A["cache_k_cmp"], A["cache_v_cmp"])):
                    page_loads(kv, b, ctr, 4 * (2 * b + kv) - 4, cache)
                    if isinstance(b, int) and b == 0:
                        w = A["w_c" + "kv"[kv] + "1"]
                        sp.dma_start(W1[kv][:, :, :], w.rearrange("(l p) n -> p l n", p=P)).then_inc(s_cw1, 16)
            looped(sp, o, TS, pages)

            def heads(i):
                for blk in range(4):
                    for j in range(4):
                        load(Q_H + 4 * i + blk, j, cols(w_b, j, blk * DM + i * 256))
            looped(sp, o, 8, heads)
            for j in range(4):
                load(Q_OB, j, cols(w_ob, j, 0))

            sp.wait_ge(w_used, 4 * Q_OB)
            sp.wait_ge(c_done, 48)

            def state_load(i, b, state):
                src = state.rearrange("b (t p) g d -> b p t (g d)", p=P)
                src = src[bass.ds(b, 1)] if not isinstance(b, int) else src[b:b + 1]
                sp.dma_start(PG[i][:, :, :], src.rearrange("o p t n -> (o p) t n")).then_inc(s_pg[i], 16)

            for br in range(2):
                def keys(i, br=br):
                    for s in range(4):
                        b = 4 * i + s
                        free = 64 + 4 * (8 * br + b) - 12
                        if br == 0:
                            page_loads(s, b, ctr, free, A["cache_k_slc"])
                        else:
                            sp.wait_ge(ctr, free)
                            state_load(s, b, A["state_k_win"])
                looped(sp, o, 2, keys)
            for br in range(2):
                def vals(i, br=br):
                    for s in range(4):
                        b = 4 * i + s
                        m = 8 * br + b
                        if isinstance(m, int) and m < 4:
                            sp.wait_ge(ctr, 64 + 4 * (13 + m))
                        if br == 0:
                            page_loads(s, b, pv, m - 3, A["cache_v_slc"])
                        else:
                            sp.wait_ge(pv, m - 3)
                            state_load(s, b, A["state_v_win"])
                looped(sp, o, 2, vals)
            quads(Q_OB, w_ob, 8, first=1)
            for t in range(5):
                for n in (10 + t, 15 + t):
                    sp.wait_ge(yn_ready[n % 2], n // 2 + 1)
                rows = P if t < NT else TS
                dst = y_prompt[0, t * P:(t + 1) * P] if t < NT else y_sample[:, 0]
                sp.dma_start(dst, YN[t][0:rows, :]).then_inc(yn_out, 16)
            sp.wait_ge(yn_out, 80)

        @block.gpsimd
        def _(pool):
            o = Own(pool, own["pool"])
            pool.dma_start(CON[:, :], A["consts"]).then_inc(s_con, 16)
            pool.dma_start(CROW[0:1, :], A["c_prompt"]).then_inc(s_rows, 16)
            pool.dma_start(CROW[1:NC, :], A["c_sample"]).then_inc(s_rows, 16)
            for v, src in enumerate((A["g_norm"][0:1], A["g_norm"][1:2], A["g_kv"].rearrange("(o n) -> o n", o=1),
                                     A["g_final"].rearrange("(o n) -> o n", o=1), A["pool_scale"])):
                pool.dma_start(VEC[KT * v:KT * v + KT, :], src.rearrange("o (k p) -> (o k) p", p=P)).then_inc(s_rows, 16)
            pool.dma_start(RELA[0:32, :], A["rel_bias"]).then_inc(s_rel, 16)
            pool.dma_start(ONEH[:, :], A["onehots"]).then_inc(s_rel, 16)
            pool.dma_start(PTAB[:, :], A["page_table"].rearrange("b n -> (b n)").rearrange("(o n) -> o n", o=1)).then_inc(s_pt, 16)
            nc.gpsimd.memset(CST[:, :, :].bitcast(F32), 0.0).then_inc(s_cz, 1)
            for t in range(5):
                if t >= 2:
                    pool.wait_ge(s_t, 2 + 4 * (t - 1))
                src = A["x_prompt"][0][t * P:(t + 1) * P] if t < NT else A["x_sample"].rearrange("b s d -> (b s) d")
                pool.dma_start(XN[t % 2][0:src.shape[0], :], src).then_inc(s_x[t % 2], 16)
            pool.dma_start(SPN[:, :], A["state_pool"][0].rearrange("b t d -> (b t) d")).then_inc(s_sp, 16)
            pool.wait_ge(s_te, 2 + 20 + 6)
            pool.dma_start(g_scr, GROW[:, :]).then_inc(s_gscr, 16)
            pool.wait_ge(s_gscr, 16)

            def b_rows(l):
                def body(i):
                    for s in range(2):
                        p = 2 * i + s + 24 * l
                        wait(pool, tr_done, p - 1)
                        b = A["b_ada"][l:l + 1]
                        at = (2 * i + s) * 256
                        b = b[:, bass.ds(at, 256)] if not isinstance(at, int) else b[:, at:at + 256]
                        pool.dma_start(MROW[18:19, s, :], b).then_inc(s_brow[s], 16)
                return body
            for l in range(2):
                looped(pool, o, 12, b_rows(l))
            def apply(a):
                l = (0, None, 1)[a]
                for k in range(KT):
                    pool.wait_ge(tn_ready, KT * a + k + 1)
                    wait(pool, h_ready, KT * a + k - 2)
                    tn, hf = TN[k % 2][:, TP:T], HF[k % 3][:, TP:T]
                    o(nc.gpsimd.tensor_tensor(hf, tn, AMOD[:, l, k, 1:NC], ALU.mult))
                    nc.gpsimd.tensor_tensor(hf, hf, MODT[:, ML * l + k, 1:NC], ALU.add).then_inc(hfs_ready, 1)

            pool.wait_ge(amod, 1)
            apply(0)
            pool.dma_start(x_scr, flat(X[:, :, :])).then_inc(s_x0, 16)
            pool.dma_start(c_scr, bass.AP(tensor=g_scr.tensor, offset=GLEN + 481, ap=[[2 * GLEN, NH], [-16, NCMP], [1, TP]])).then_inc(s_bscr, 16)
            pool.dma_start(pool_s[0][:, 0:PB - 1, :], A["state_pool"][0][:, 1:PB, :]).then_inc(s_copy, 16)
            for n in range(NH // 4 + 2 * TS):
                pool.wait_ge(w_used, 4 * Q_U + n + 1)
                if n < NH // 4:
                    pool.dma_start(b_scr[4 * n:4 * n + 4], bass.AP(tensor=g_scr.tensor, offset=4 * n * 2 * GLEN + P,
                                                                   ap=[[2 * GLEN, 4], [-1, P], [1, 512]])).then_inc(s_bscr, 16)
                else:
                    c, b = divmod(n - NH // 4, TS)
                    pool.dma_start((k_win_s, v_win_s)[c][b, 0:TP - 1], A[("state_k_win", "state_v_win")[c]][b, 1:TP]).then_inc(s_copy, 16)
            pool.wait_ge(s_ute, 4)
            pool.dma_start(pool_p[0, 0], UT[0:PB, :]).then_inc(s_uo, 16)
            pool.dma_start(pool_s[0][:, PB - 1, :], UT[PB:PB + TS, :]).then_inc(s_uo, 16)
            for i in range(2):
                o(nc.gpsimd.memset(PAD[i][:, 0:16], 0.0))
            for g, w in enumerate(WINDOWS):
                for k in range(4 * g, 4 * g + 4):
                    u = Y[:, k, 0:TP]
                    o(nc.gpsimd.tensor_tensor(PAD[0][:, 17:16 + TP], u[:, 1:TP], u[:, 0:TP - 1], ALU.add))
                    o(nc.gpsimd.tensor_copy(PAD[0][:, 16:17], u[:, 0:1]))
                    src, step = 0, 2
                    while step < w:
                        o(nc.gpsimd.tensor_tensor(PAD[1 - src][:, 16:16 + TP], PAD[src][:, 16:16 + TP], PAD[src][:, 16 - step:16 + TP - step], ALU.add))
                        src, step = 1 - src, 2 * step
                    s_ = PAD[src]
                    o(nc.gpsimd.tensor_tensor(s_[:, 16:32], s_[:, 16:32], CON[:, C_CNT + 16 * g:C_CNT + 16 * g + 16], ALU.mult))
                    o(nc.gpsimd.tensor_scalar(s_[:, 32:16 + TP], s_[:, 32:16 + TP], 1.0 / w, None, ALU.mult))
                    last = nc.gpsimd.tensor_tensor(u, s_[:, 16:16 + TP], u, ALU.subtract)
                    if k < 4 * g + 3:
                        o(last)
                last.then_inc(s_pooled, 1)
                pool.wait_ge(s_pooled, g + 1)
            pool.wait_ge(acc_free, 2 * D_OA)
            pool.wait_ge(s_x0, 16)
            pool.dma_start(flat(X[:, :, :]), x_scr).then_inc(s_x1, 16)
            for g in range(NKV):
                for b in range(TS):
                    r = 32 * g + 4 * b
                    pool.dma_start(bd_scr[r:r + 4, :], g_scr[4 * g:4 * g + 4, 0:513]).then_inc(s_bds, 16)
                    pool.dma_start(bcd_scr[r:r + 4, :], g_scr[4 * g:4 * g + 4, 31:31 + 16 * NCMP:16],
                                   allow_slow_non_contiguous=True).then_inc(s_bds, 16)

            def kv_rows(i):
                for t in range(5):
                    n = 5 * i + t
                    pool.wait_ge(tm_ready, n + 1)
                    rows = P if t < NT else TS
                    dst = kv_out_p[i][t * P:(t + 1) * P] if t < NT else kv_out_s[i]
                    pool.dma_start(dst, TM[n % 4][0:rows, :]).then_inc(tm_out[n % 4], 16)
            pool.wait_ge(h_ready, 2 * KT)
            for i, n in enumerate("kv"):
                pool.dma_start(W2[i][:, :], A[f"w_c{n}2"]).then_inc(s_cw, 16)
                pool.dma_start(PE_[i][:, :], A[f"pe_{n}"]).then_inc(s_cw, 16)
            for i in range(6):
                kv_rows(i)
            pool.wait_ge(cout, 18)
            pool.dma_start(vc_scr, VCP[:, :, :].rearrange("p g d -> p (g d)")).then_inc(s_vcp, 16)
            apply(2)
            pool.wait_ge(tn_ready, 3 * KT)
            pool.dma_start(x_scr, flat(X[:, :, :])).then_inc(s_xs, 16)
            pool.wait_ge(acc_free, 2 * (D_G + 1))
            for br in range(NBR):
                for g in range(NKV):
                    pool.dma_start(bass.AP(tensor=gd_scr.tensor, offset=br * P + g * 32, ap=[[1, REP], [4, TS]]),
                                   GF[br * NH + g * REP:br * NH + g * REP + REP, TP:T],
                                   allow_slow_non_contiguous=True).then_inc(s_gd, 16)
            pool.wait_ge(s_gd, 16 * 12)
            pool.wait_ge(s_xs, 16)
            pool.wait_ge(s_vcp, 16)
            pool.wait_ge(s_bscr, 16 * (1 + NH // 4))
            for s in range(4):
                pool.wait_ge(tm_out[s], 16 * len([n for n in range(30) if n % 4 == s]))

            def head_loads(i):
                wait(pool, c_done, 6 * i)
                g = i // 2
                gd = lambda w: w.rearrange("(t p) (g d) -> g p t d", p=P, d=P)
                for br, v in enumerate((kv_out_p[3], kv_out_p[5])):
                    src = gd(v)
                    src = src[bass.ds(g, 1)] if not isinstance(g, int) else src[g:g + 1]
                    pool.dma_start(VG[:, br, :, :], src.rearrange("o p t d -> (o p) t d")).then_inc(hd_in, 16)
                vs = vc_scr.rearrange("n (g d) -> g n d", d=P)
                vs = vs[bass.ds(g, 1)] if not isinstance(g, int) else vs[g:g + 1]
                pool.dma_start(VCG[:, :], vs.rearrange("o n d -> (o n) d")).then_inc(hd_in, 16)
                h2 = lambda w: (w[bass.ds(i * 2, 2)] if not isinstance(i, int) else w[2 * i:2 * i + 2]).rearrange("h p n -> p h n")
                pool.dma_start(BH[:, :, :], h2(b_scr)).then_inc(hd_in, 16)
                pool.dma_start(BC[:, :, :], h2(c_scr)).then_inc(hd_in, 16)
                for u in range(6):
                    n = 6 * i + u
                    pool.wait_ge(r_ready, n + 1)
                    if u < 2:
                        last = nc.gpsimd.tensor_tensor(
                            PR[:, 0:NT * NCMP].rearrange("p (t n) -> p t n", n=NCMP), PR[:, 0:NT * NCMP].rearrange("p (t n) -> p t n", n=NCMP),
                            STAT[:, 8:12].unsqueeze(2).broadcast_to([P, NT, NCMP]), ALU.mult)
                    else:
                        at = 0
                        for t in range(NT):
                            w = P * (t + 1)
                            last = nc.gpsimd.tensor_tensor(PR[:, at:at + w], PR[:, at:at + w],
                                                           STAT[:, 8 + t:9 + t].broadcast_to([P, w]), ALU.mult)
                            at += w
                    last.then_inc(p_ready, 1)
            looped(pool, o, 8, head_loads)

            pool.wait_ge(w_used, 4 * Q_OB)
            nc.gpsimd.memset(PX[:, :], 0.0)
            nc.gpsimd.memset(ZERO[:, :], 0.0).then_inc(s_dm, 1)
            pool.dma_start(GD[:, :], bass.AP(tensor=gd_scr.tensor, offset=0, ap=[[1, P], [P, NBR]]),
                           allow_slow_non_contiguous=True).then_inc(s_bd, 16)
            pool.wait_ge(s_bds, 16 * 64)
            pool.dma_start(BD[:, :], bd_scr).then_inc(s_bd, 16)
            pool.dma_start(BCD[:, :], bcd_scr).then_inc(s_bd, 16)
            for br in range(2):
                def queries(i, br=br):
                    for s in range(4):
                        b = 4 * i + s
                        pool.wait_ge(dsc, 8 * br + b + 1)
                        q = QD[:, :, :].rearrange("p (g r) b -> p g b r", g=NKV)
                        mk = CON[:, bass.ds(b * 8 + C_MSK, 8)] if not isinstance(b, int) else CON[:, C_MSK + 8 * b:C_MSK + 8 * b + 8]
                        mk = mk.unsqueeze(1).unsqueeze(3).broadcast_to([P, NKV, TS, REP])
                        nc.gpsimd.tensor_tensor(QPAD[s % 2][:, :, :].rearrange("p g (b r) -> p g b r", b=TS), q, mk, ALU.mult).then_inc(qp_ready, 1)
                looped(pool, o, 2, queries)
            pool.wait_ge(sd_step, 1)
            for br in range(2):
                pool.dma_start(VN[br][:, :], kv_out_s[3 + 2 * br]).then_inc(s_vn[br], 16)
            pool.wait_ge(sd_ev, 9)
            for br in range(2):
                def probs(i, br=br):
                    for s in range(4):
                        b = 4 * i + s
                        wait(pool, pv, 8 * br + b - 1)
                        mk = CON[:, bass.ds(b * 8 + C_MSK, 8)] if not isinstance(b, int) else CON[:, C_MSK + 8 * b:C_MSK + 8 * b + 8]
                        mk = mk.unsqueeze(1).unsqueeze(3).broadcast_to([P, NPG * NKV, TS, REP])
                        cut = lambda x: x[:, :, :].rearrange("p t (g b r) -> p (t g) b r", g=NKV, b=TS)
                        nc.gpsimd.tensor_tensor(cut(PPAD[s % 2]), cut(PTD[br]), mk, ALU.mult).then_inc(pp_ready, 1)
                looped(pool, o, 2, probs)
            pool.wait_ge(ydec, 1)
            pool.dma_start(flat(X[:, :, :]), x_scr).then_inc(s_xb, 16)
            pool.wait_ge(s_copy, 16 * (1 + 2 * TS))
            pool.wait_ge(s_uo, 32)

        @block.scalar
        def _(act):
            o = Own(act, own["act"])

            def hi(q, j):
                act.wait_ge(raw_full[j], 16 * (q - 23))
                wait(act, w_used, 4 * q + j - 1)
                nc.scalar.activation(HI[j % 2][:, :, :], RAW[j][:, :, :], ACT.Copy).then_inc(hi_ready, 1)

            act.wait_ge(s_rows, 16 * 7)
            nc.scalar.activation(CSIL[:, :], CROW[:, :], ACT.Silu).then_inc(s_csil, 1)
            act.wait_ge(s_te, 2)
            act.wait_ge(s_cz, 1)
            nc.scalar.activation(CST[:, :, 0:NC], CTF[:, :, :], ACT.Copy).then_inc(s_cs, 1)

            def mod_rows(p, s):
                act.wait_ge(w_used, 4 * p + 4)
                wait(act, tr_done, p - 1)
                nc.scalar.activation(MROW[0:18, s, :], D[s][0:18, 0:256], ACT.Copy).then_inc(mr_ready, 1)

            def square(r, k, slot):
                if r:
                    act.wait_ge(acc_free, 2 * (0, D_OA, D_OB)[r] + k + 1)
                wait(act, sq_used, KT * r + k - 1)
                nc.scalar.activation((SQ if r else SQ0)[slot][:, :], dyn(X, k).rearrange("p o t -> p (o t)"), ACT.Square).then_inc(sq_ready, 1)

            def squares(r, i):
                for mm in range(2):
                    square(r, 2 * i + mm, mm)

            def rms(r):
                act.wait_ge(sq_used, KT * (r + 1))
                bank, to = (S, RMS) if r else ((O, S[2]), RSTD)
                for half in range(2):
                    last = nc.scalar.activation(to[:, half * HT:(half + 1) * HT], bank[half][:, 0:HT], ACT.Sqrt,
                                                scale=1.0 / DM, bias=CON[:, C_EPS:C_EPS + 1])
                last.then_inc(rms_ready, 1)

            def ada(l, i0=0, stats=False):
                def body(i):
                    i = i + i0
                    for s in range(2):
                        p = 2 * i + s + 24 * l
                        for j in range(4):
                            act.wait_ge(raw_full[4 * s + j], 16 * (i + 12 * l + 1))
                            wait(act, w_used, 4 * p + j - 3)
                            nc.scalar.activation(HI[j][:, :, :], RAW[4 * s + j][:, :, :], ACT.Copy).then_inc(hi_ready, 1)
                            if j == 1 and not (isinstance(p, int) and p == 0):
                                mod_rows(p - 1, 1 - s)
                            if j == 2 and stats:
                                square(0, 2 * i + s, s)
                return body
            looped(act, o, 12, ada(0))
            act.wait_ge(s_te, 22)
            looped(act, o, 8, ada(1, 0, True), 1, 1)
            rms(0)
            looped(act, o, 4, ada(1, 8))
            mod_rows(47, 1)
            hi(Q_U, 0)

            def apply(a):
                l = (0, None, 1, None)[a]
                for k in range(KT + 1):
                    if k < KT:
                        act.wait_ge(tn_ready, KT * a + k + 1)
                        if a == 3:
                            nc.scalar.activation(X[:, k, :], TN[k % 2][:, :], ACT.Copy, scale=vec(3, k)).then_inc(hf_ready, 1)
                            if k % 4 == 3 and k > 3:
                                y_rows(k // 4 - 1)
                            continue
                        wait(act, h_ready, KT * a + k - 2)
                        if l is None:
                            nc.scalar.activation(HF[k % 3][:, :], TN[k % 2][:, :], ACT.Copy, scale=vec(2, k)).then_inc(hf_ready, 1)
                        else:
                            nc.scalar.activation(HF[k % 3][:, 0:TP], TN[k % 2][:, 0:TP], ACT.Identity,
                                                 scale=AMOD[:, l, k, 0:1], bias=MODT[:, ML * l + k, 0:1]).then_inc(hf_ready, 1)
                    if k and a < 3:
                        act.wait_ge(hf_ready, KT * a + k)
                        if l is not None:
                            act.wait_ge(hfs_ready, KT * (a // 2) + k)
                        nc.scalar.activation(HH[:, k - 1, :], HF[(k - 1) % 3][:, :], ACT.Copy).then_inc(hhi_ready, 1)

            def y_rows(k4):
                for n in range(5 * k4, 5 * k4 + 5):
                    if n % 2 == 1:
                        t = n % 5
                        rows = P if t < NT else TS
                        act.wait_ge(yn_tr, n + 1)
                        nc.scalar.activation(YN[t][0:rows, 512 * k4:512 * k4 + 512], S[1][0:rows, :], ACT.Copy).then_inc(yn_ready[1], 1)

            act.wait_ge(amod, 1)
            apply(0)

            def dense_tile(q, d, mm):
                if mm == 0:
                    act.wait_ge(first_done, d + 1)
                else:
                    act.wait_ge(w_used, 4 * q + 4)

            def evac(dst, mm):
                for half, h in enumerate(halves(dst)):
                    last = nc.scalar.activation(h, D[2 * mm + half][:, 0:HT], ACT.Copy)
                last.then_inc(acc_free, 1)

            def u_pairs(i):
                for q, j in ahead(Q_U + i):
                    hi(q, j)
                for mm in range(2):
                    dense_tile(Q_U + i, D_U + i, mm)
                    evac(dyn(Y, 2 * i + mm).rearrange("p o t -> p (o t)"), mm)
            looped(act, o, 8, u_pairs)

            act.wait_ge(s_x0, 16)

            def z_pairs(i):
                for q, j in ahead(Q_Z + i):
                    hi(q, j)
                for mm in range(2):
                    dense_tile(Q_Z + i, D_Z + i, mm)
                    for half, h in enumerate(halves(dyn(ZS, 2 * i + mm).rearrange("p o t -> p (o t)"))):
                        last = nc.scalar.activation(h, D[2 * mm + half][:, 0:HT], ACT.Silu)
                    last.then_inc(acc_free, 1)
            looped(act, o, 8, z_pairs)

            def pooled_hi(g):
                wait(act, w_used, 4 * Q_MIX + 2 * (g - 1))
                nc.scalar.activation(PHI[g % 2][:, :, :], Y[:, 4 * g:4 * g + 4, :], ACT.Copy).then_inc(s_ph, 1)

            def y_hi(n, k):
                nc.scalar.activation(HH[:, k, :], Y[:, k, :], ACT.Copy).then_inc(ys_hi, 1)

            act.wait_ge(s_uo, 32)
            act.wait_ge(s_pooled, 4)
            act.wait_ge(s_pooled_s, 1)
            pooled_hi(0)
            pooled_hi(1)
            for n in range(8):
                if n in (2, 4):
                    pooled_hi(n // 2 + 1)
                hi(Q_MIX + (n + 1) // 4, (n + 1) % 4)
                if n:
                    for k in (2 * n - 2, 2 * n - 1):
                        act.wait_ge(acc_free, 2 * D_MIX + k + 1)
                        y_hi(0, k)
            for k in (14, 15):
                act.wait_ge(acc_free, 2 * D_MIX + k + 1)
                y_hi(0, k)

            def resid_pairs(r, q0, skip):
                def body(i):
                    for q, j in ahead(q0 + i):
                        if not (skip and isinstance(i, int) and i == 7 and j == 0):
                            hi(q, j)
                        if j == 1 and not (isinstance(i, int) and i == 0):
                            squares(r, i - 1)
                looped(act, o, 8, body, 2, 1)
                squares(r, 7)
                rms(r)
            resid_pairs(1, Q_OA, False)
            act.wait_ge(w_used, 4 * Q_KV)
            apply(1)
            for i, dst in enumerate((KCF, VCF, KS, VF, KW, VF)):
                if i == 5:
                    act.wait_ge(kv_tr, 20)

                def kv_pair(pp, i=i, dst=dst):
                    q, d = Q_KV + 2 * i + pp, D_KV + 2 * i + pp
                    for qq, j in ahead(q):
                        hi(qq, j)
                    for mm in range(2):
                        dense_tile(q, d, mm)
                        for half in range(2):
                            to = dyn(dst, 2 * pp + mm)[:, :, half * HT:(half + 1) * HT].rearrange("p o t -> p (o t)")
                            last = nc.scalar.activation(to, D[2 * mm + half][:, 0:HT], ACT.Copy)
                        last.then_inc(acc_free, 1)
                looped(act, o, 2, kv_pair)

            def hidden(n, kv, base):
                act.wait_ge(cw1, n + 1)
                if base:
                    act.wait_ge(cw2, n - 1)
                nc.scalar.activation(CSIL2[kv][:, :], S[2][:, 0:NKV * NCMP], ACT.Silu, bias=PEC[:, kv:kv + 1]).then_inc(csr, 1)

            def pages_out(n, slot, used=None):
                if used is None:
                    wait(act, cw1, n - 1)
                else:
                    act.wait_ge(dsc, used)
                for g in (1, 3):
                    act.wait_ge(ctr, 4 * n + g + 1)
                    nc.scalar.activation(RT_T[slot][:, g, :], S[1][:, :], ACT.Copy).then_inc(ctre[1], 1)

            pages_out(0, 0)
            act.wait_ge(s_pee, 4)

            def hiddens(b):
                for kv in range(2):
                    if not (isinstance(b, int) and 2 * b + kv == 15):
                        pages_out(2 * b + kv + 1, 1 - kv)
                    hidden(2 * b + kv, kv, not (isinstance(b, int) and b == 0))
            looped(act, o, TS, hiddens, 1, 1)
            for kv in range(2):
                hidden(16 + kv, kv, True)
            act.wait_ge(cw2, 18)
            apply(2)
            for q, j in ahead(Q_G):
                hi(q, j)
            act.wait_ge(w_used, 4 * (Q_G + 1))
            for half in range(2):
                last = nc.scalar.activation(GF[:, half * HT:(half + 1) * HT], D[half][0:48, 0:HT], ACT.Sigmoid)
            last.then_inc(acc_free, 2)

            def exps(n, u):
                act.wait_ge(negm, n + 1)
                if u < 2:
                    nc.scalar.activation(PR[:, 0:NT * NCMP], PR[:, 0:NT * NCMP], ACT.Exp).then_inc(e_done, 1)
                else:
                    at = 0
                    for t in range(NT):
                        w = P * (t + 1)
                        last = nc.scalar.activation(PR[:, at:at + w], PR[:, at:at + w], ACT.Exp,
                                                    bias=STAT[:, t:t + 1], accum_out=STAT[:, 4 + t:5 + t])
                        at += w
                    last.then_inc(e_done, 1)

            def turned(n, u):
                act.wait_ge(b_done, n + 1)
                wait(act, c_done, n)
                if u < 2:
                    nc.scalar.activation(PT[0:NCMP, 0:512], S[0][0:NCMP, :], ACT.Copy).then_inc(pt_ready, 1)
                else:
                    nc.scalar.activation(PT[:, 0:512], S[0][:, :], ACT.Copy).then_inc(pt_ready, 1)

            act.wait_ge(s_xs, 16)

            def heads(i):
                for s in range(17):
                    if s < 16:
                        hi(Q_H + 4 * i + (s + 1) // 4, (s + 1) % 4)
                    if s >= 3 and s % 4 in (3, 0):
                        mm, blk = (0, s // 4) if s % 4 == 3 else (1, s // 4 - 1)
                        dense_tile(Q_H + 4 * i + blk, D_H + 4 * i + blk, mm)
                        if blk == 0:
                            wait(act, a_done, 6 * i)
                            nc.scalar.activation(QS[:, mm, 0:HT], D[2 * mm][:, 0:HT], ACT.Copy, scale=SCALE)
                            nc.scalar.activation(QS[:, mm, HT:TP], D[2 * mm + 1][:, 0:TP - HT], ACT.Copy, scale=SCALE)
                            to = dyn(QD, 2 * i + mm).rearrange("p o b -> p (o b)")
                            nc.scalar.activation(to, D[2 * mm + 1][:, TP - HT:HT], ACT.Copy, scale=SCALE).then_inc(acc_free, 1)
                        else:
                            wait(act, o_used, 6 * i)
                            for half in range(2):
                                nc.scalar.activation(ZB[:, blk - 1, mm, half * HT:(half + 1) * HT], D[2 * mm + half][:, 0:HT], ACT.Silu)
                            to = dyn(SZD[:, blk - 1], 2 * i + mm).rearrange("p o b -> p (o b)")
                            nc.scalar.activation(to, D[2 * mm + 1][:, TP - HT:HT], ACT.Silu).then_inc(acc_free, 1)
                    u = (s - 4) // 2
                    if s >= 4 and s % 2 == 0 and u < 6:
                        exps(6 * i + u, u)
                    if s >= 5 and s % 2 == 1:
                        turned(6 * i + (s - 5) // 2, (s - 5) // 2)
            looped(act, o, 8, heads)

            pages_out(16, 0, 1)
            for br in range(2):
                def stage(i, br=br):
                    for s in range(2):
                        b = 2 * i + s
                        m = 8 * br + b
                        if m < 15:
                            pages_out(17 + m, 1 - s, m + 2)
                        act.wait_ge(dsc, m + 1)
                        if br == 0:
                            nc.scalar.activation(KCB[s][:, :], dyn(KCS, b).rearrange("p o n -> p (o n)"), ACT.Copy)
                        kt_ = (KS if br == 0 else KW)
                        kn = kt_[:, :, bass.ds(b + TP, 1)] if not isinstance(b, int) else kt_[:, :, b + TP:b + TP + 1]
                        nc.scalar.activation(KN[s][:, :], kn.rearrange("p g o -> p (g o)"), ACT.Copy).then_inc(kst, 1)
                looped(act, o, 4, stage, 4)
            for n in range(3):
                act.wait_ge(sd_step, n + 1)
                src = (SC[:, :], SD[0][:, :], SD[1][:, :])[n]
                nc.scalar.activation(src, src, ACT.Exp, bias=SST[:, n:n + 1], accum_out=SST[:, 4 + n:5 + n]).then_inc(sd_exp, 1)
            act.wait_ge(ydec, 1)
            for k in range(KT):
                y_hi(1, k)
            act.wait_ge(s_xb, 16)
            resid_pairs(2, Q_OB, True)
            apply(3)
            y_rows(3)

        @block.vector
        def _(dve):
            o = Own(dve, own["dve"])
            V = nc.vector

            def lo(q, j):
                dve.wait_ge(hi_ready, 4 * q + j + 1)
                V.tensor_tensor(LO[j % 2][:, :, :], RAW[j][:, :, :], HI[j % 2][:, :, :].bitcast(F32), ALU.subtract).then_inc(lo_ready, 1)

            V.memset(RELA[32:33, :], NEG).then_inc(s_negrow, 1)
            dve.wait_ge(s_t, 1)
            V.tensor_copy(VECT[:, :], S[0][:, 0:80]).then_inc(s_te, 1)
            dve.wait_ge(s_t, 2)
            V.tensor_copy(flat(CTF[:, :, :]), S[1][:, 0:KT * NC]).then_inc(s_te, 1)
            dve.wait_ge(s_cs, 1)
            V.tensor_tensor(CST[:, :, NC:2 * NC], CTF[:, :, :], CST[:, :, 0:NC].bitcast(F32), ALU.subtract).then_inc(s_cs, 1)
            for t in range(5):
                n = P if t < NT else TS
                for k4 in range(4):
                    dve.wait_ge(s_t, 2 + 4 * t + k4 + 1)
                    V.tensor_copy(X[:, 4 * k4:4 * k4 + 4, t * P:t * P + n],
                                  S[k4 % 2][:, :].rearrange("p (k t) -> p k t", k=4)[:, :, 0:n]).then_inc(s_te, 1)
            for n in range(6):
                dve.wait_ge(s_t, 22 + n + 1)
                at = (n // 3) * GLEN + (n % 3) * 512
                w = min(512, GLEN - (n % 3) * 512)
                V.tensor_copy(GROW[:, at:at + w], S[n % 2][0:NH, 0:w]).then_inc(s_te, 1)

            def mod_out(p, s):
                dve.wait_ge(tr_done, p + 1)
                V.tensor_copy(dyn(MODT, 2 * p, 2), S[s][:, 0:2 * NC].rearrange("p (a n) -> p a n", a=2)).then_inc(mt_ready, 1)

            def rstd(r):
                dve.wait_ge(rms_ready, r + 1)
                V.reciprocal(RSTD[:, :], (RMS if r else RSTD)[:, :]).then_inc(rstd_ready, 1)
                dve.wait_ge(rstd_ready, r + 1)

            def ada(l, i0=0, stats=False):
                def body(i):
                    i = i + i0
                    for s in range(2):
                        p = 2 * i + s + 24 * l
                        for j in range(4):
                            dve.wait_ge(hi_ready, 4 * p + j + 1)
                            V.tensor_tensor(LO[j][:, :, :], RAW[4 * s + j][:, :, :], HI[j][:, :, :].bitcast(F32), ALU.subtract).then_inc(lo_ready, 1)
                            if j == 2 and not (isinstance(p, int) and p == 0):
                                mod_out(p - 1, 1 - s)
                return body
            looped(dve, o, 12, ada(0))
            looped(dve, o, 8, ada(1, 0, True), 1, 1)
            rstd(0)
            looped(dve, o, 4, ada(1, 8))
            mod_out(47, 1)
            lo(Q_U, 0)
            dve.wait_ge(mt_ready, 48)
            last = None
            for l in range(2):
                if last is not None:
                    o(last)
                o(V.tensor_scalar(AMOD[:, l, :, :], MODT[:, ML * l + KT:ML * l + 2 * KT, :], 1.0, None, ALU.add))
                last = V.tensor_tensor(AMOD[:, l, :, :], AMOD[:, l, :, :],
                                       VECT[:, KT * l:KT * l + KT].unsqueeze(2).broadcast_to([P, KT, NC]), ALU.mult)
            last.then_inc(amod, 1)

            def y_rows(k4):
                for n in range(5 * k4, 5 * k4 + 5):
                    if n % 2 == 0:
                        t = n % 5
                        rows = P if t < NT else TS
                        dve.wait_ge(yn_tr, n + 1)
                        V.tensor_copy(YN[t][0:rows, 512 * k4:512 * k4 + 512], S[0][0:rows, :]).then_inc(yn_ready[0], 1)

            def apply(a):
                for k in range(KT + 2):
                    if k < KT:
                        if a or k >= 2:
                            dve.wait_ge(hf_ready, KT * a + k - 1)
                            if a in (0, 2):
                                wait(dve, hfs_ready, KT * (a // 2) + k - 1)
                        V.tensor_tensor(TN[k % 2][:, :], X[:, k, :], RSTD[:, :], ALU.mult).then_inc(tn_ready, 1)
                    if a == 3 and k in (7, 11, 15, 17):
                        y_rows({7: 0, 11: 1, 15: 2, 17: 3}[k])
                    if k >= 2 and a < 3:
                        dve.wait_ge(hhi_ready, KT * a + k - 1)
                        V.tensor_tensor(HL[:, k - 2, :], HF[(k - 2) % 3][:, :], HH[:, k - 2, :].bitcast(F32), ALU.subtract).then_inc(h_ready, 1)

            apply(0)

            def los(q0, n):
                def body(i):
                    for q, j in ahead(q0 + i):
                        lo(q, j)
                looped(dve, o, n, body)
            los(Q_U, 8)
            for k4 in range(4):
                dve.wait_ge(s_ut, k4 + 1)
                V.tensor_copy(UT[:, 512 * k4:512 * k4 + 512], S[k4 % 2][0:23, :]).then_inc(s_ute, 1)
            dve.wait_ge(s_ps, 1)
            for g, w in enumerate(WINDOWS):
                us = Y[:, 4 * g:4 * g + 4, TP:T]
                ps = O[:, 32 * g:32 * g + 32].rearrange("p (k b) -> p k b", k=4)
                o(V.tensor_tensor(STMP[:, :, :], ps, us, ALU.add))
                last = V.scalar_tensor_tensor(out=us, in0=STMP[:, :, :], scalar=1.0 / w, in1=us, op0=ALU.mult, op1=ALU.subtract)
                if g < 3:
                    o(last)
            last.then_inc(s_pooled_s, 1)
            los(Q_Z, 8)

            def pooled_lo(g):
                dve.wait_ge(s_ph, g + 1)
                V.tensor_tensor(PLO[g % 2][:, :, :], Y[:, 4 * g:4 * g + 4, :], PHI[g % 2][:, :, :].bitcast(F32), ALU.subtract).then_inc(s_pl, 1)

            def y_lo(n, k):
                dve.wait_ge(ys_hi, KT * n + k + 1)
                V.tensor_tensor(HL[:, k, :], Y[:, k, :], HH[:, k, :].bitcast(F32), ALU.subtract).then_inc(ys, 1)

            pooled_lo(0)
            pooled_lo(1)
            for n in range(8):
                if n in (2, 4):
                    pooled_lo(n // 2 + 1)
                lo(Q_MIX + (n + 1) // 4, (n + 1) % 4)
                for mm in range(2):
                    if mm == 0:
                        dve.wait_ge(first_done, D_MIX + n + 1)
                    else:
                        dve.wait_ge(w_used, 4 * Q_MIX + n + 1)
                    m = 2 * n + mm
                    for half, h in enumerate(halves(Y[:, m, :])):
                        last = V.scalar_tensor_tensor(out=h, in0=D[2 * mm + half][:, 0:HT], scalar=vec(4, m),
                                                      in1=halves(ZS[:, m, :])[half], op0=ALU.mult, op1=ALU.mult)
                    last.then_inc(acc_free, 1)
                if n:
                    for k in (2 * n - 2, 2 * n - 1):
                        y_lo(0, k)
            y_lo(0, 14)
            y_lo(0, 15)

            def resid(l, q0, d0):
                def body(i):
                    for q, j in ahead(q0 + i):
                        if not (l == 1 and isinstance(i, int) and i == 7 and j == 0):
                            lo(q, j)
                    for mm in range(2):
                        m = 2 * i + mm
                        if mm == 0:
                            dve.wait_ge(first_done, d0 + i + 1)
                        else:
                            dve.wait_ge(w_used, 4 * (q0 + i) + 4)
                        x = dyn(X, m).rearrange("p o t -> p (o t)")
                        gate = dyn(MODT, m + ML * l + 2 * KT).rearrange("p o n -> p (o n)")
                        a, b = D[2 * mm], D[2 * mm + 1]
                        V.scalar_tensor_tensor(out=x[:, 0:HT], in0=a[:, 0:HT], scalar=gate[:, 0:1], in1=x[:, 0:HT], op0=ALU.mult, op1=ALU.add)
                        V.scalar_tensor_tensor(out=x[:, HT:TP], in0=b[:, 0:TP - HT], scalar=gate[:, 0:1], in1=x[:, HT:TP], op0=ALU.mult, op1=ALU.add)
                        dve.wait_ge(acc_free, 2 * (d0 + i) + mm - 1)
                        o(V.tensor_tensor(RT[mm][:, :], b[:, TP - HT:HT], gate[:, 1:NC], ALU.mult))
                        V.tensor_tensor(x[:, TP:T], x[:, TP:T], RT[mm][:, :], ALU.add).then_inc(acc_free, 1)
                return body
            dve.wait_ge(s_x1, 16)
            looped(dve, o, 8, resid(0, Q_OA, D_OA))
            rstd(1)
            apply(1)

            for i, src in enumerate((KCF, VCF, KS, VF, KW, VF)):
                los(Q_KV + 2 * i, 2)
                for t in range(5):
                    n = 5 * i + t
                    rows = P if t < NT else TS
                    dve.wait_ge(kv_tr, n + 1)
                    if n >= 4:
                        dve.wait_ge(tm_out[n % 4], 16 * (n // 4))
                    V.tensor_copy(TM[n % 4][0:rows, :], S[n % 2][0:rows, :]).then_inc(tm_ready, 1)

            for kv in range(2):
                dve.wait_ge(s_pe, kv + 1)
                V.tensor_copy(PET[kv][:, :], S[kv][:, 0:CL]).then_inc(s_pee, 1)

            def compress_out(n, kv, b):
                dve.wait_ge(cw2, n + 1)
                if kv == 0:
                    dst = dyn(KCS, b).rearrange("p o n -> p (o n)")
                    V.tensor_copy(dst, O[:, 0:NKV * NCMP]).then_inc(cout, 1)
                else:
                    dst = VCS[:, bass.ds(b, 1), :] if not isinstance(b, int) else VCS[:, b:b + 1, :]
                    V.tensor_copy(dst.rearrange("p o n -> p (o n)"), O[0:NKV * NCMP, 0:P]).then_inc(cout, 1)

            def pages_out(n, slot, used=None):
                if used is None:
                    wait(dve, cw1, n - 1)
                else:
                    dve.wait_ge(dsc, used)
                for g in (0, 2):
                    dve.wait_ge(ctr, 4 * n + g + 1)
                    V.tensor_copy(RT_T[slot][:, g, :], S[0][:, :]).then_inc(ctre[0], 1)

            pages_out(0, 0)
            V.memset(PER[:, :], 0.0).then_inc(s_pez, 1)
            dve.wait_ge(s_pez, 1)
            dve.wait_ge(s_pe, 3)
            for r in (0, 32, 64, 96):
                last = V.tensor_copy(PER[r:r + 1, :], O[r:r + 1, 0:P])
            last.then_inc(s_pee, 1)
            dve.wait_ge(s_pe, 4)
            V.tensor_copy(PEC[:, :], S[2][:, 0:2]).then_inc(s_pee, 1)

            def compress(b):
                for kv in range(2):
                    if not (isinstance(b, int) and 2 * b + kv == 15):
                        pages_out(2 * b + kv + 1, 1 - kv)
                    if kv == 0 and not (isinstance(b, int) and b == 0):
                        compress_out(2 * b - 1, 1, b - 1)
                    if kv == 1:
                        compress_out(2 * b, 0, b)
            looped(dve, o, TS, compress, 1, 1)
            compress_out(15, 1, 7)
            dve.wait_ge(cw2, 17)
            V.tensor_copy(KCP[:, :], O[:, 0:NKV * NCMP]).then_inc(cout, 1)
            dve.wait_ge(cw2, 18)
            V.tensor_copy(flat(VCP[:, :, :]), O[0:NCMP, :]).then_inc(cout, 1)

            apply(2)
            for q, j in ahead(Q_G):
                lo(q, j)
            dve.wait_ge(g_tr, 1)
            V.tensor_copy(flat(GT[:, :, :]), S[0][:, 0:NT * 48]).then_inc(gt_ready, 1)
            dve.wait_ge(gt_ready, 1)
            dve.wait_ge(s_xs, 16)

            W_AT = [0, 1, 3, 6]

            def softmax(i, u):
                n, br, hh = 6 * i + u, u // 2, u % 2
                dve.wait_ge(a_done, n + 1)
                if u == 0:
                    dve.wait_ge(hd_in, 80 * (i + 1))
                wait(dve, b_done, n)
                if u < 2:
                    sc = S[0][:, 0:NT * NCMP].rearrange("p (t n) -> p t n", n=NCMP)
                    pr = PR[:, 0:NT * NCMP].rearrange("p (t n) -> p t n", n=NCMP)
                    o(V.tensor_reduce(STAT[:, 0:4], sc, AX.X, ALU.max))
                    V.tensor_tensor(pr, sc, STAT[:, 0:4].unsqueeze(2).broadcast_to([P, NT, NCMP]), ALU.subtract).then_inc(negm, 1)
                else:
                    where = (S[1][:, 384:512], S[2][:, 0:256], S[1][:, 0:384], S[0][:, :])
                    V.memset(STAT[:, 12:13], 0.0)
                    for t in range(NT):
                        w = P * (t + 1)
                        at = W_AT[t] * P
                        last = V.tensor_tensor_reduce(PR[:, at:at + w], where[t], BH[:, hh, (3 - t) * P:512], 1.0, -3e38,
                                                      ALU.add, ALU.max, STAT[:, t:t + 1])
                    o(last)
                    V.tensor_scalar(STAT[:, 0:4], STAT[:, 0:4], -1.0, None, ALU.mult).then_inc(negm, 1)

            def factor(i, u):
                n, br, hh = 6 * i + u, u // 2, u % 2
                dve.wait_ge(e_done, n + 1)
                if u < 2:
                    o(V.tensor_reduce(STAT[:, 4:8], PR[:, 0:NT * NCMP].rearrange("p (t n) -> p t n", n=NCMP), AX.X, ALU.add))
                o(V.reciprocal(STAT[:, 8:12], STAT[:, 4:8]))
                at = 2 * i + (br * NH + hh)
                gate = GT[:, :, bass.ds(at, 1)] if not isinstance(at, int) else GT[:, :, at:at + 1]
                mul = V.tensor_tensor(STAT[:, 8:12], STAT[:, 8:12], gate.rearrange("p t o -> p (t o)"), ALU.mult)
                if u < 2:
                    o(mul)
                    mul = V.tensor_tensor(STAT[:, 8:9], STAT[:, 8:9], CON[:, C_VIS:C_VIS + 1], ALU.mult)
                mul.then_inc(r_ready, 1)

            def turned(i, u):
                n = 6 * i + u
                dve.wait_ge(b_done, n + 1)
                dve.wait_ge(c_done, n)
                V.tensor_copy(PT[:, 512:1024], S[1][:, :])
                V.tensor_copy(PT[:, 1024:1280], S[2][:, 0:256]).then_inc(pt2_ready, 1)

            def values(i, u):
                n, br, hh = 6 * i + u, u // 2, u % 2
                dve.wait_ge(c_done, n + 1)
                dve.wait_ge(acc_free, 2 * (D_H + 4 * i + br + 1) + hh + 1)
                y = dyn(Y, 2 * i + hh)[:, :, 0:TP].rearrange("p o t -> p (o t)")
                if br == 0:
                    V.tensor_tensor(y, O[:, :], ZB[:, br, hh, 0:TP], ALU.mult).then_inc(o_used, 1)
                else:
                    V.tensor_tensor(TMP[:, :], O[:, :], ZB[:, br, hh, 0:TP], ALU.mult).then_inc(o_used, 1)
                    dve.wait_ge(o_used, n + 1)
                    o(V.tensor_tensor(y, y, TMP[:, :], ALU.add))

            def heads(i):
                for s in range(17):
                    if s < 16:
                        lo(Q_H + 4 * i + (s + 1) // 4, (s + 1) % 4)
                    if s >= 4 and s % 2 == 0 and s < 16:
                        softmax(i, (s - 4) // 2)
                        factor(i, (s - 4) // 2)
                    if s >= 9 and s % 2 == 1:
                        turned(i, (s - 5) // 2)
                    if s >= 8 and s % 2 == 0:
                        values(i, (s - 8) // 2)
                values(i, 5)
            looped(dve, o, 8, heads)

            dve.wait_ge(s_bd, 16 * 3)
            dve.wait_ge(s_dm, 1)
            for br in range(2):
                def keys(i, br=br):
                    for s in range(2):
                        pages_out(16 + 8 * br + 2 * i + s, s, 8 * br + 2 * i + s + 1)
                looped(dve, o, 4, keys)
            dve.wait_ge(sd_pe, 1)
            o(V.tensor_tensor(SC[:, :], D[3][:, 0:NCMP], BCD[:, :], ALU.add))
            o(V.tensor_reduce(SST[:, 0:1], SC[:, :], AX.X, ALU.max))
            V.tensor_scalar(SST[:, 0:1], SST[:, 0:1], -1.0, None, ALU.mult).then_inc(sd_step, 1)
            dve.wait_ge(sd_exp, 1)
            o(V.reciprocal(SST[:, 8:9], SST[:, 4:5]))
            o(V.tensor_scalar(SC[:, :], SC[:, :], SST[:, 8:9], None, ALU.mult))
            for g in range(NKV):
                last = V.tensor_copy(PX[32 * g:32 * g + 32, NCMP * g:NCMP * g + NCMP], SC[32 * g:32 * g + 32, :])
            last.then_inc(sd_ev, 1)
            dve.wait_ge(sd_pe, 2)
            V.tensor_copy(PTC[:, :], S[0][0:NKV * NCMP, 0:P]).then_inc(sd_ev, 1)
            V.tensor_scalar(PX[:, :], PX[:, :], GD[:, 0:1], None, ALU.mult).then_inc(sd_ev, 1)
            dve.wait_ge(sd_pe, 3)
            V.tensor_copy(IMP[:, :], S[1][:, 0:9]).then_inc(sd_ev, 1)
            dve.wait_ge(sd_pe, 4)
            V.tensor_copy(PTG[:, :], S[0][0:NKV * NCMP, P:2 * P]).then_inc(sd_ev, 1)
            dve.wait_ge(sd_pe, 5)
            o(V.tensor_copy(DRP[:, 0, :], S[2][:, 1:8]))
            o(V.tensor_reduce(SST[:, 12:13], DRP[:, 0, :], AX.X, ALU.min))
            o(V.tensor_scalar(DRP[:, 1, :], DRP[:, 0, :], SST[:, 12:13], None, ALU.is_equal))
            o(V.tensor_tensor(DRP[:, 1, :], DRP[:, 1, :], CON[:, C_IOTA:C_IOTA + 7], ALU.mult))
            o(V.tensor_reduce(SST[:, 13:14], DRP[:, 1, :], AX.X, ALU.max))
            o(V.tensor_scalar(DRP[:, 2, :], DRP[:, 1, :], SST[:, 13:14], NEG, ALU.is_equal, ALU.mult))
            for br in range(2):
                o(V.tensor_tensor(SD[br][:, 0:512], D[br][:, :], BD[:, 0:512], ALU.add))
                o(V.tensor_tensor(SD[br][:, 512:513], D[2][:, br:br + 1], BD[:, 512:513], ALU.add))
                if br == 0:
                    blocks = SD[0][:, 64:512].rearrange("p (j n) -> p j n", j=7)
                    o(V.tensor_tensor(blocks, blocks, DRP[:, 2, :].unsqueeze(2).broadcast_to([P, 7, 64]), ALU.add))
                else:
                    o(V.tensor_scalar(SD[1][:, 0:1], SD[1][:, 0:1], NEG, None, ALU.add))
                o(V.tensor_reduce(SST[:, 1 + br:2 + br], SD[br][:, :], AX.X, ALU.max))
                V.tensor_scalar(SST[:, 1 + br:2 + br], SST[:, 1 + br:2 + br], -1.0, None, ALU.mult).then_inc(sd_step, 1)
            for br in range(2):
                dve.wait_ge(sd_exp, 2 + br)
                o(V.reciprocal(SST[:, 9 + br:10 + br], SST[:, 5 + br:6 + br]))
                o(V.tensor_tensor(SST[:, 9 + br:10 + br], SST[:, 9 + br:10 + br], GD[:, 1 + br:2 + br], ALU.mult))
                o(V.tensor_scalar(SD[br][:, :], SD[br][:, :], SST[:, 9 + br:10 + br], None, ALU.mult))
                V.tensor_scalar(PNEW[br][:, :], CON[:, C_ROW:C_ROW + TS], SD[br][:, 512:513], None, ALU.mult).then_inc(sd_ev, 1)
            for br in range(2):
                dve.wait_ge(sd_pe, 7)
                V.tensor_copy(flat(PTD[br][:, :, :]), S[br][:, :])
                V.tensor_copy(PTN[:, br, :], S[2][0:TS, P * br:P * br + P]).then_inc(sd_ev, 1)
            dve.wait_ge(sd_pe, 8)
            V.tensor_copy(OD[0][:, :, :].rearrange("p b h -> p (b h)"), O[:, 0:P]).then_inc(sd_ev, 1)
            for br in range(2):
                dve.wait_ge(sd_pe, 9 + br)
                V.tensor_copy(ACC[br][:, :], D[br][:, 0:P]).then_inc(sd_ev, 1)
            dve.wait_ge(sd_pe, 11)
            for br in range(2):
                last = V.tensor_copy(OD[1 + br][:, :, :].rearrange("p b (g r) -> p g b r", g=NKV),
                                     S[0][:, P * br:P * br + P].rearrange("p (g b r) -> p g b r", g=NKV, b=TS))
                o(last)
            yd = Y[:, :, TP:T]
            for br in range(NBR):
                dst = yd if br == 0 else OM[:, :, :]
                o(V.tensor_tensor(dst, OD[br][:, :, :].rearrange("p b h -> p h b"), SZD[:, br, :, :], ALU.mult))
                if br:
                    last = V.tensor_tensor(yd, yd, OM[:, :, :], ALU.add)
                    if br == 1:
                        o(last)
            last.then_inc(ydec, 1)
            for k in range(KT):
                y_lo(1, k)
            dve.wait_ge(s_xb, 16)
            looped(dve, o, 8, resid(1, Q_OB, D_OB), 1, 1)
            rstd(2)
            apply(3)

        @block.tensor
        def _(pe):
            o = Own(pe, own["pe"])
            mm_, tr = nc.tensor.matmul, nc.tensor.transpose

            pe.wait_ge(s_con, 16)
            pe.wait_ge(s_rows, 16 * 7)
            tr(S[0][:, 0:80], VEC[:, :], ident[0:80, 0:80]).then_inc(s_t, 1)
            pe.wait_ge(s_csil, 1)
            for k in range(KT):
                last = tr(S[1][:, NC * k:NC * k + NC], CSIL[:, P * k:P * k + P], ident[0:NC, 0:NC])
            last.then_inc(s_t, 1)
            for t in range(5):
                rows = P if t < NT else TS
                pe.wait_ge(s_x[t % 2], 16 * (t // 2 + 1))
                for k4 in range(4):
                    pe.wait_ge(s_te, 4 * t + k4 + 1)
                    for k in range(4):
                        at = (4 * k4 + k) * P
                        last = tr(S[k4 % 2][:, P * k:P * k + rows], XN[t % 2][0:rows, at:at + P], ident[0:rows, 0:rows])
                    last.then_inc(s_t, 1)
            pe.wait_ge(s_rel, 32)
            pe.wait_ge(s_negrow, 1)
            for n in range(6):
                pe.wait_ge(s_te, 21 + n)
                at = (n // 3) * GLEN + (n % 3) * 512
                w = min(512, GLEN - (n % 3) * 512)
                mm_(S[n % 2][0:NH, 0:w], RELA[:, :], ONEH[:, at:at + w], start=True, stop=True).then_inc(s_t, 1)
            pe.wait_ge(s_te, 28)

            pe.wait_ge(s_cs, 2)

            def turn_rows(p, i, s, l):
                pe.wait_ge(mr_ready, p + 1)
                pe.wait_ge(s_brow[s], 16 * (i + 1 + 12 * l))
                wait(pe, mt_ready, p - 1)
                for h in range(2):
                    last = mm_(S[s][:, NC * h:NC * h + NC], MROW[0:19, s, P * h:P * h + P],
                               CON[0:19, C_SEL19:C_SEL19 + NC], start=True, stop=True)
                last.then_inc(tr_done, 1)

            def stat(r, k, par):
                pe.wait_ge(sq_ready, KT * r + k + 1)
                first, end = isinstance(k, int) and k == 0, isinstance(k, int) and k == KT - 1
                for half in range(2):
                    last = mm_(((S if r else (O, S[2]))[half])[:, 0:HT], ones, (SQ if r else SQ0)[par][:, half * HT:(half + 1) * HT], start=first, stop=end)
                last.then_inc(sq_used, 1)

            def ada(l, i0=0, stats=False):
                def body(i):
                    i = i + i0
                    for s in range(2):
                        p = 2 * i + s + 24 * l
                        wait(pe, mr_ready, p - 1)
                        for j in range(4):
                            pe.wait_ge(lo_ready, 4 * p + j + 1)
                            for kk in range(4):
                                k = 4 * j + kk
                                mm_(D[s][:, 0:256], CST[:, k, :], HI[j][:, kk, :], start=(k == 0), stop=False)
                                last = mm_(D[s][:, 0:256], CST[:, k, :], LO[j][:, kk, :], start=False, stop=(k == KT - 1))
                            last.then_inc(w_used, 1)
                            if j == 1 and not (isinstance(p, int) and p == 0):
                                turn_rows(p - 1, i - 1 + s, 1 - s, l)
                            if j == 3 and stats:
                                stat(0, 2 * i + s, s)
                return body
            looped(pe, o, 12, ada(0))
            looped(pe, o, 8, ada(1, 0, True), 1, 1)
            looped(pe, o, 4, ada(1, 8))
            turn_rows(47, 11, 1, 1)

            def products(out, slot, kk, mm, hi_src, lo_src, k, first, end, n=P):
                cols_ = slice(mm * P, mm * P + n)
                for part, src in ((HI, hi_src), (HI, lo_src), (LO, hi_src)):
                    for half in range(2):
                        last = mm_(out[half][0:n, 0:HT], part[slot][:, kk, cols_], src[:, k, half * HT:(half + 1) * HT],
                                   start=(first and part is HI and src is hi_src), stop=(end and part is LO))
                return last

            def quad(q, d, j, ready=None):
                pe.wait_ge(lo_ready, 4 * q + j + 1)
                if ready is not None:
                    pe.wait_ge(ready[0], ready[1] + 4 * (j + 1))
                for mm in range(2):
                    if j == 0:
                        wait(pe, acc_free, 2 * d + mm - 1)
                    for kk in range(4):
                        last = products(D[2 * mm:2 * mm + 2], j % 2, kk, mm, HH, HL, 4 * j + kk, j == 0 and kk == 0, j == 3 and kk == 3)
                    if mm == 0 and j == 3:
                        last.then_inc(first_done, 1)
                last.then_inc(w_used, 1)

            def pairs(q0, d0, n, ready):
                def body(i):
                    for j in range(4):
                        quad(q0 + i, d0 + i, j, ready if isinstance(i, int) and i == 0 else None)
                looped(pe, o, n, body)

            pairs(Q_U, D_U, 8, (h_ready, 0))
            pe.wait_ge(acc_free, 16)
            pe.wait_ge(rms_ready, 1)
            for k4 in range(4):
                if k4 >= 2:
                    pe.wait_ge(s_ute, k4 - 1)
                for k in range(4):
                    last = tr(S[k4 % 2][0:23, P * k:P * k + P], Y[:, 4 * k4 + k, TP - PB:T], ident)
                last.then_inc(s_ut, 1)
            pe.wait_ge(s_sp, 16)
            for k in range(KT):
                last = mm_(O[:, 8 * k:8 * k + 8], SPN[:, P * k:P * k + P], CON[0:TS * PB, C_SELP + 8 * (k // 4):C_SELP + 8 * (k // 4) + 8],
                           start=True, stop=True)
            last.then_inc(s_ps, 1)
            pairs(Q_Z, D_Z, 8, None)
            for n in range(8):
                g = n // 2
                if n % 2 == 0:
                    pe.wait_ge(s_pl, g + 1)
                pe.wait_ge(lo_ready, 4 * Q_MIX + n + 1)
                for mm in range(2):
                    pe.wait_ge(acc_free, 2 * (D_MIX + n) + mm - 1)
                    for kk in range(4):
                        last = products(D[2 * mm:2 * mm + 2], n % 2, kk, mm, PHI[g % 2], PLO[g % 2], kk, kk == 0, kk == 3)
                    if mm == 0:
                        last.then_inc(first_done, 1)
                last.then_inc(w_used, 1)

            def resid_pairs(r, q0, d0, ready):
                def body(i):
                    for j in range(4):
                        quad(q0 + i, d0 + i, j, ready if isinstance(i, int) and i == 0 else None)
                        if j == 2 and not (isinstance(i, int) and i == 0):
                            for mm in range(2):
                                stat(r, 2 * (i - 1) + mm, mm)
                looped(pe, o, 8, body, 2, 1)
                for mm in range(2):
                    stat(r, 14 + mm, mm)
            resid_pairs(1, Q_OA, D_OA, (ys, 0))
            for i, src in enumerate((KCF, VCF, KS, VF, KW, VF)):
                pairs(Q_KV + 2 * i, D_KV + 2 * i, 2, (h_ready, KT) if i == 0 else None)
                pe.wait_ge(acc_free, 2 * (D_KV + 2 * i + 2))
                if i == 0:
                    pe.wait_ge(rms_ready, 2)
                for t in range(5):
                    rows = P if t < NT else TS
                    n = 5 * i + t
                    if n >= 2:
                        pe.wait_ge(tm_ready, n - 1)
                    for g in range(NKV):
                        last = tr(S[n % 2][0:rows, P * g:P * g + P], src[:, g, t * P:t * P + rows], ident)
                    last.then_inc(kv_tr, 1)

            pe.wait_ge(s_cw, 16 * 4)
            pe.wait_ge(tm_ready, 30)
            for kv in range(2):
                tr(S[kv][:, 0:CL], PE_[kv][:, :], ident[0:CL, 0:CL]).then_inc(s_pe, 1)

            def turn_pages(n, slot):
                for g in range(NKV):
                    wait(pe, ctre[g % 2], 2 * n + g // 2)
                    for t in range(NPG):
                        last = tr(S[g % 2][:, P * t:P * t + P], PG[slot][:, t, P * g:P * g + P], ident)
                    last.then_inc(ctr, 1)

            def hidden(n, kv, src, peeled=False):
                wait(pe, csr, n)
                for l in range(CL):
                    at = [src[:, :, l:l + 16 * (NCMP - 1) + 1:16]]
                    last = mm_(S[2][:, 0:NKV * NCMP], W1[kv][:, l, :], at[0], start=(l == 0), stop=(l == CL - 1))
                last.then_inc(cw1, 1)

            def second(n, kv, prompt=False):
                pe.wait_ge(csr, n + 1)
                wait(pe, cout, n)
                if kv == 0:
                    last = mm_(O[:, 0:NKV * NCMP], W2[0][:, :], CSIL2[0][:, :], start=True, stop=True)
                elif not prompt:
                    last = mm_(O[0:NKV * NCMP, 0:P], CSIL2[1][:, :], W2[1][:, :], start=True, stop=True)
                else:
                    for g in range(NKV):
                        last = mm_(O[0:NCMP, P * g:P * g + P], CSIL2[1][:, NCMP * g:NCMP * g + NCMP], W2[1][:, :], start=True, stop=True)
                last.then_inc(cw2, 1)

            pe.wait_ge(s_pee, 2)
            pe.wait_ge(s_pg[0], 64)
            turn_pages(0, 0)
            pe.wait_ge(s_cw1, 16 * 2)
            for l in range(CL):
                for kv in range(2):
                    r = 64 * kv + 32 * (l % 2)
                    last = mm_(O[r:r + 1, 0:P], PET[kv][:, l:l + 1], W1[kv][:, l, :], start=(l < 2), stop=(l >= CL - 2),
                               skip_group_check=True, tile_position=(0, r))
            last.then_inc(s_pe, 1)
            pe.wait_ge(s_pee, 3)
            mm_(S[2][:, 0:2], PER[:, :], CON[:, C_PER:C_PER + 2], start=True, stop=True).then_inc(s_pe, 1)
            pe.wait_ge(s_pee, 4)

            def compress(b):
                for kv in range(2):
                    n = 2 * b + kv
                    if not (isinstance(b, int) and n == 15):
                        pe.wait_ge(s_pg[1 - kv], 64 * (b + 1 + kv))
                        turn_pages(n + 1, 1 - kv)
                    for c in ctre:
                        pe.wait_ge(c, 2 * n + 2)
                    hidden(n, kv, RT_T[kv])
                    if not (isinstance(b, int) and n == 0):
                        second(n - 1, 1 - kv)
            looped(pe, o, TS, compress, 1, 1)
            hidden(16, 0, KCF)
            second(15, 1)
            hidden(17, 1, VCF)
            second(16, 0, True)
            second(17, 1, True)

            for j in range(4):
                pe.wait_ge(lo_ready, 4 * Q_G + j + 1)
                pe.wait_ge(h_ready, 2 * KT + 4 * (j + 1))
                for kk in range(4):
                    last = products(D[0:2], j % 2, kk, 0, HH, HL, 4 * j + kk, j == 0 and kk == 0, j == 3 and kk == 3)
                    if j == 3 and kk == 2:
                        last.then_inc(first_done, 1)
                last.then_inc(w_used, 1)
            pe.wait_ge(acc_free, 2 * (D_G + 1))
            pe.wait_ge(cout, 18)
            for t in range(NT):
                last = tr(S[0][:, 48 * t:48 * t + 48], GF[:, P * t:P * t + P], ident[0:48, 0:48])
            last.then_inc(g_tr, 1)
            pe.wait_ge(gt_ready, 1)

            def scores(i, u):
                n, br, hh = 6 * i + u, u // 2, u % 2
                g = i // 2
                if br == 0:
                    pe.wait_ge(acc_free, 2 * (D_H + 4 * i) + hh + 1)
                if u == 0:
                    pe.wait_ge(hd_in, 80 * (i + 1))
                wait(pe, pt_ready, n)
                wait(pe, pt2_ready, 4 * i + max(0, u - 2))
                qs = lambda t: QS[:, hh, P * t:P * t + P]
                if br == 0:
                    at = g * NCMP
                    kc = KCP[:, bass.ds(at, NCMP)] if not isinstance(at, int) else KCP[:, at:at + NCMP]
                    for t in range(NT):
                        out = S[0][:, NCMP * t:NCMP * t + NCMP]
                        mm_(out, BC[:, hh, P * t:P * t + P], ident[0:NCMP, 0:NCMP], start=True, stop=False)
                        last = mm_(out, qs(t), kc, start=False, stop=True)
                else:
                    kt_ = KS if br == 1 else KW
                    kt_ = dyn(kt_, g)
                    where = (S[1][:, 384:512], S[2][:, 0:256], S[1][:, 0:384], S[0][:, :])
                    for t in (3, 2, 1, 0):
                        last = mm_(where[t], qs(t), kt_[:, :, 0:P * (t + 1)].rearrange("p o t -> p (o t)"), start=True, stop=True)
                last.then_inc(a_done, 1)

            W_AT = [0, 1, 3, 6]

            def turn(i, u):
                n = 6 * i + u
                pe.wait_ge(p_ready, n + 1)
                if u < 2:
                    for t in range(NT):
                        last = tr(S[0][0:NCMP, P * t:P * t + P], PR[:, NCMP * t:NCMP * t + NCMP], ident)
                else:
                    for b, at, j in ((0, 0, 0), (1, 0, 1), (1, 3, 3), (2, 0, 2)):
                        for t in range(j, NT):
                            c = (at + t - j) * P
                            src = (W_AT[t] + j) * P
                            last = tr(S[b][:, c:c + P], PR[:, src:src + P], ident)
                last.then_inc(b_done, 1)

            def values(i, u):
                n, br = 6 * i + u, u // 2
                pe.wait_ge(pt_ready, n + 1)
                if u >= 2:
                    pe.wait_ge(pt2_ready, 4 * i + u - 1)
                wait(pe, o_used, n)
                if br == 0:
                    last = mm_(O[:, :], VCG[:, :], PT[0:NCMP, 0:512], start=True, stop=True)
                else:
                    for j, at in ((0, 0), (1, 512), (2, 1024), (3, 512 + 384)):
                        last = mm_(O[:, P * j:512], VG[:, br - 1, j, :], PT[:, at:at + 512 - P * j], start=(j == 0), stop=(j == 3),
                                   skip_group_check=True)
                last.then_inc(c_done, 1)

            def heads(i):
                for s in range(16):
                    quad(Q_H + 4 * i + s // 4, D_H + 4 * i + s // 4, s % 4)
                    if s >= 6 and s % 2 == 0:
                        values(i, (s - 6) // 2)
                    if s >= 4 and s % 2 == 0:
                        u = (s - 4) // 2
                        if u < 6:
                            turn(i, u)
                    if s >= 3 and s % 2 == 1:
                        u = (s - 3) // 2
                        if u < 6:
                            scores(i, u)
                values(i, 5)
            looped(pe, o, 8, heads)

            pe.wait_ge(s_dm, 1)
            pe.wait_ge(acc_free, 2 * D_OB)
            for b in range(4):
                last = mm_(D[b][:, :], ZERO[:, :], Y[:, 0, 0:512], start=True, stop=(b < 0), skip_group_check=True)
            last.then_inc(dsc, 2)
            def turn_next(m):
                s, i = m % 4, m // 4
                base = 512 if s < 2 else 0
                pe.wait_ge(s_pg[s], base + (64 * (i + 1) if i < 2 else 128 + 16 * (i - 1)))
                turn_pages(16 + m, s)

            turn_next(0)
            for br in range(2):
                def keys(i, br=br):
                    for s in range(4):
                        b = 4 * i + s
                        m = 8 * br + b
                        if m < 15:
                            turn_next(m + 1)
                        pe.wait_ge(qp_ready, m + 1)
                        for c in ctre:
                            pe.wait_ge(c, 32 + 2 * m + 2)
                        pe.wait_ge(kst, m + 1)
                        for g in range(NKV):
                            r = slice(32 * g, 32 * g + 32)
                            q = QPAD[s % 2][:, g, :]
                            mm_(D[br][r, :], q, RT_T[s % 2][:, g, :], start=False, stop=False, skip_group_check=True)
                            last = mm_(D[2][r, br:br + 1], q, KN[s % 2][:, g:g + 1], start=False, stop=False, skip_group_check=True)
                            if br == 0:
                                last = mm_(D[3][r, 0:NCMP], q, KCB[s % 2][:, NCMP * g:NCMP * g + NCMP], start=False, stop=False, skip_group_check=True)
                        last.then_inc(dsc, 1)
                looped(pe, o, 2, keys, 2)
            for b in range(4):
                last = mm_(D[b][:, :], ZERO[:, :], Y[:, 0, 0:512], start=False, stop=True, skip_group_check=True)
            last.then_inc(sd_pe, 1)
            pe.wait_ge(sd_ev, 1)
            tr(S[0][0:NKV * NCMP, 0:P], PX[:, :], ident).then_inc(sd_pe, 1)
            pe.wait_ge(sd_ev, 2)
            mm_(S[1][:, 0:9], PTC[:, :], CON[0:NKV * NCMP, C_OVL:C_OVL + 9], start=True, stop=True).then_inc(sd_pe, 1)
            pe.wait_ge(sd_ev, 3)
            tr(S[0][0:NKV * NCMP, P:2 * P], PX[:, :], ident).then_inc(sd_pe, 1)
            pe.wait_ge(sd_ev, 4)
            mm_(S[2][:, 0:9], CON[:, C_RSUM:C_RSUM + P], IMP[:, :], start=True, stop=True).then_inc(sd_pe, 1)
            for br in range(2):
                pe.wait_ge(sd_ev, 6 + br)
                for t in range(NPG):
                    tr(S[br][:, P * t:P * t + P], SD[br][:, P * t:P * t + P], ident)
                tr(S[2][0:TS, P * br:P * br + P], PNEW[br][:, :], ident).then_inc(sd_pe, 1)
            for b in range(TS):
                last = mm_(O[:, NH * b:NH * b + NH], VCS[:, b, :], PTG[:, :].rearrange("p (g n) -> p g n", g=NKV)[:, :, 4 * b:4 * b + 4],
                           start=True, stop=True)
            last.then_inc(sd_pe, 1)
            pe.wait_ge(sd_ev, 9)
            for br in range(2):
                mm_(D[br][:, 0:P], ZERO[:, :], ident, start=True, stop=False, skip_group_check=True)
                pe.wait_ge(s_vn[br], 16)
                for g in range(NKV):
                    r = slice(32 * g, 32 * g + 32)
                    mm_(D[br][r, 0:P], PTN[:, br, r], VN[br][:, P * g:P * g + P], start=False, stop=False, skip_group_check=True)

                def vals(i, br=br):
                    for s in range(4):
                        b = 4 * i + s
                        m = 8 * br + b
                        base = 512 if s < 2 else 0
                        pe.wait_ge(s_pg[s], base + 160 + 64 * (i + 1) if br == 0 else base + 288 + 16 * (i + 1))
                        pe.wait_ge(pp_ready, m + 1)
                        for t in range(NPG):
                            for g in range(NKV):
                                r = slice(32 * g, 32 * g + 32)
                                last = mm_(D[br][r, 0:P], PPAD[s % 2][:, t, r], PG[s][:, t, P * g:P * g + P],
                                           start=False, stop=False, skip_group_check=True)
                        last.then_inc(pv, 1)
                looped(pe, o, 2, vals)
                mm_(D[br][:, 0:P], ZERO[:, :], ident, start=False, stop=True, skip_group_check=True).then_inc(sd_pe, 1)
            for br in range(2):
                pe.wait_ge(sd_ev, 11 + br)
                last = tr(S[0][:, P * br:P * br + P], ACC[br][:, :], ident)
            last.then_inc(sd_pe, 1)

            resid_pairs(2, Q_OB, D_OB, (ys, KT))
            pe.wait_ge(rms_ready, 3)
            for k4 in range(4):
                pe.wait_ge(hf_ready, 3 * KT + 4 * (k4 + 1))
                for t in range(5):
                    rows = P if t < NT else TS
                    n = 5 * k4 + t
                    wait(pe, yn_ready[n % 2], n // 2)
                    for k in range(4):
                        last = tr(S[n % 2][0:rows, P * k:P * k + P], X[:, 4 * k4 + k, t * P:t * P + rows], ident)
                    last.then_inc(yn_tr, 1)


_OUTS = [(1, 512, 2048), (8, 1, 2048), (1, 1, 15, 2048)] + [(1, 512, 4, 128)] * 6 + \
    [(1, 8, 15, 2048)] + [(8, 1, 4, 128)] * 4 + [(8, 512, 4, 128)] * 2


def kernel(**inputs):
    import concourse.bacc as bacc
    from concourse.bass_utils import run_bass_kernel_spmd

    nc = bacc.Bacc("TRN2", target_bir_lowering=False, num_devices=1)
    arrays = {n: np.ascontiguousarray(a) for n, a in inputs.items()}
    arrays["consts"] = shape_constants()
    arrays["onehots"] = bucket_onehots()
    ins = {n: nc.dram_tensor(f"in_{n}", a.shape, mybir.dt.from_np(a.dtype), kind="ExternalInput").ap() for n, a in arrays.items()}
    outs = [nc.dram_tensor(f"out_{i}", s, F32, kind="ExternalOutput").ap() for i, s in enumerate(_OUTS)]
    build(nc, ins, outs)
    r = run_bass_kernel_spmd(nc, [{f"in_{n}": a for n, a in arrays.items()}], core_ids=[0])
    return tuple(r.results[0][f"out_{i}"] for i in range(len(_OUTS)))
```
